# Optimizing a Trainium2 kernel written in Bass

```python
import jax, jax.numpy as jnp
from jax import lax
import numpy as np

D_MODEL = 1024
BATCH = 1
SEQ = 1024
DEPTH = 1
DEC_BATCH = 1
DEC_SEQ = 512
PAST_LEN = 128

MIX_WIDTH = D_MODEL
HEAD_DIM = 64
D_FOURIER = MIX_WIDTH // 2
D_LRU = MIX_WIDTH - D_FOURIER
N_FOURIER_HEADS = D_FOURIER // HEAD_DIM
N_LRU_HEADS = D_LRU // HEAD_DIM
D_IN = D_FOURIER + 2 * D_LRU
CONV_WIDTH = 4
CONV_PAD_LEFT = 2
CONV_PAD_RIGHT = CONV_WIDTH - 1 - CONV_PAD_LEFT
LRU_C = 8.0
D_FF = 4 * D_MODEL
N_MOD = 6
EPS = 1e-6

kernel_name = "hybrid_fnet_rglru_adaln_encoder"

def rms_norm(x, g):
    xf = x.astype(jnp.float32)
    y = xf * lax.rsqrt(jnp.mean(xf * xf, axis=-1, keepdims=True) + EPS)
    return (y * g.astype(jnp.float32)).astype(x.dtype)

def fourier_mixer(u, w_f):
    b, s, _ = u.shape
    uh = u.reshape(b, s, N_FOURIER_HEADS, HEAD_DIM).astype(jnp.float32)
    f = jnp.fft.fft2(uh, axes=(1, 3), norm="ortho").real.astype(u.dtype)
    y = jnp.einsum("bshd,hde->bshe", f, w_f)
    return y.reshape(b, s, D_FOURIER)

def centred_depthwise_conv(u, w, bias):
    s = u.shape[1]
    up = jnp.pad(u, ((0, 0), (CONV_PAD_LEFT, CONV_PAD_RIGHT), (0, 0)))
    out = bias
    for k in range(CONV_WIDTH):
        out = out + up[:, k:k + s, :] * w[k]
    return out

def _lru_combine(e1, e2):
    a1, b1 = e1
    a2, b2 = e2
    return a1 * a2, a2 * b1 + b2

def rglru_direction(x, w_r, b_r, w_i, b_i, lam, reverse):
    b, s, _ = x.shape
    xh = x.reshape(b, s, N_LRU_HEADS, HEAD_DIM)
    r = jax.nn.sigmoid(jnp.einsum("bshd,hde->bshe", xh, w_r) + b_r).reshape(b, s, D_LRU)
    i = jax.nn.sigmoid(jnp.einsum("bshd,hde->bshe", xh, w_i) + b_i).reshape(b, s, D_LRU)
    log_a = -LRU_C * r * jax.nn.softplus(-lam)
    a = jnp.exp(log_a)
    mult = jnp.sqrt(jnp.maximum(-jnp.expm1(2.0 * log_a), 0.0))
    bx = mult * (i * x)
    _, h = lax.associative_scan(_lru_combine, (a, bx), axis=1, reverse=reverse)
    return h

def bidirectional_rglru(u, w_rg, b_rg, w_ig, b_ig, lam):
    uf = u.astype(jnp.float32)
    w_rg = w_rg.astype(jnp.float32); b_rg = b_rg.astype(jnp.float32)
    w_ig = w_ig.astype(jnp.float32); b_ig = b_ig.astype(jnp.float32)
    lam = lam.astype(jnp.float32)
    h_fwd = rglru_direction(uf, w_rg[0], b_rg[0], w_ig[0], b_ig[0], lam[0], reverse=False)
    h_bwd = rglru_direction(uf, w_rg[1], b_rg[1], w_ig[1], b_ig[1], lam[1], reverse=True)
    return (h_fwd + h_bwd).astype(u.dtype)

def encoder_layer(x, c, g_mix, g_mlp, w_mod, b_mod, w_in, w_fourier, conv_w, conv_b,
                  w_rgate, b_rgate, w_igate, b_igate, lru_lambda, w_out, w_ff1, w_ff2):
    mod = jax.nn.silu(c.astype(jnp.float32)) @ w_mod.astype(jnp.float32) + b_mod.astype(jnp.float32)
    mod = mod.astype(x.dtype)[:, None, :]
    shift1, scale1, gate1, shift2, scale2, gate2 = jnp.split(mod, N_MOD, axis=-1)

    h = rms_norm(x, g_mix) * (1.0 + scale1) + shift1
    z = h @ w_in
    u_f = z[..., :D_FOURIER]
    u_r = z[..., D_FOURIER:D_FOURIER + D_LRU]
    u_g = z[..., D_FOURIER + D_LRU:]
    y_f = fourier_mixer(u_f, w_fourier)
    u_c = centred_depthwise_conv(u_r, conv_w, conv_b)
    y_r = bidirectional_rglru(u_c, w_rgate, b_rgate, w_igate, b_igate, lru_lambda) * jax.nn.gelu(u_g)
    mix = jnp.concatenate([y_f, y_r], axis=-1) @ w_out
    x = x + gate1 * mix

    h = rms_norm(x, g_mlp) * (1.0 + scale2) + shift2
    ff = jnp.square(jax.nn.relu(h @ w_ff1)) @ w_ff2
    return x + gate2 * ff

def trunk(x, c, g_mix, g_mlp, w_mod, b_mod, w_in, w_fourier, conv_w, conv_b,
          w_rgate, b_rgate, w_igate, b_igate, lru_lambda, w_out, w_ff1, w_ff2, g_final):
    for l in range(DEPTH):
        x = encoder_layer(x, c, g_mix[l], g_mlp[l], w_mod[l], b_mod[l], w_in[l], w_fourier[l],
                          conv_w[l], conv_b[l], w_rgate[l], b_rgate[l], w_igate[l], b_igate[l],
                          lru_lambda[l], w_out[l], w_ff1[l], w_ff2[l])
    return rms_norm(x, g_final)

def setup_inputs(seed: int = 0) -> dict:
    key = jax.random.key(seed)
    ks = jax.random.split(key, 24)
    f32 = jnp.float32
    nrm = lambda k, shape, scale: (jax.random.normal(k, shape, f32) * scale).astype(f32)
    a0 = jax.random.uniform(ks[18], (DEPTH, 2, D_LRU), f32, 0.9, 0.999)
    return {
        "x_prompt": nrm(ks[0], (BATCH, SEQ, D_MODEL), 1.0),
        "x_sample": nrm(ks[1], (DEC_BATCH, DEC_SEQ, D_MODEL), 1.0),
        "c_prompt": nrm(ks[2], (BATCH, D_MODEL), 1.0),
        "c_sample": nrm(ks[3], (DEC_BATCH, D_MODEL), 1.0),
        "g_mix": 1.0 + nrm(ks[4], (DEPTH, D_MODEL), 0.02),
        "g_mlp": 1.0 + nrm(ks[5], (DEPTH, D_MODEL), 0.02),
        "w_mod": nrm(ks[6], (DEPTH, D_MODEL, N_MOD * D_MODEL), 0.5 * D_MODEL ** -0.5),
        "b_mod": nrm(ks[7], (DEPTH, N_MOD * D_MODEL), 0.02),
        "w_in": nrm(ks[8], (DEPTH, D_MODEL, D_IN), D_MODEL ** -0.5),
        "w_fourier": nrm(ks[9], (DEPTH, N_FOURIER_HEADS, HEAD_DIM, HEAD_DIM), HEAD_DIM ** -0.5),
        "conv_w": nrm(ks[10], (DEPTH, CONV_WIDTH, D_LRU), 0.5),
        "conv_b": nrm(ks[11], (DEPTH, D_LRU), 0.02),
        "w_rgate": nrm(ks[12], (DEPTH, 2, N_LRU_HEADS, HEAD_DIM, HEAD_DIM), HEAD_DIM ** -0.5),
        "b_rgate": nrm(ks[13], (DEPTH, 2, N_LRU_HEADS, HEAD_DIM), 0.02),
        "w_igate": nrm(ks[14], (DEPTH, 2, N_LRU_HEADS, HEAD_DIM, HEAD_DIM), HEAD_DIM ** -0.5),
        "b_igate": nrm(ks[15], (DEPTH, 2, N_LRU_HEADS, HEAD_DIM), 0.02),
        "lru_lambda": jnp.log(a0) - jnp.log1p(-a0),
        "w_out": nrm(ks[16], (DEPTH, MIX_WIDTH, D_MODEL), MIX_WIDTH ** -0.5),
        "w_ff1": nrm(ks[17], (DEPTH, D_MODEL, D_FF), D_MODEL ** -0.5),
        "w_ff2": nrm(ks[19], (DEPTH, D_FF, D_MODEL), D_FF ** -0.5),
        "g_final": 1.0 + nrm(ks[20], (D_MODEL,), 0.02),
    }

def reference(x_prompt, x_sample, c_prompt, c_sample, g_mix, g_mlp, w_mod, b_mod, w_in,
              w_fourier, conv_w, conv_b, w_rgate, b_rgate, w_igate, b_igate, lru_lambda,
              w_out, w_ff1, w_ff2, g_final):
    y_prompt = trunk(x_prompt, c_prompt, g_mix, g_mlp, w_mod, b_mod, w_in, w_fourier, conv_w,
                     conv_b, w_rgate, b_rgate, w_igate, b_igate, lru_lambda, w_out, w_ff1,
                     w_ff2, g_final)
    y_sample = trunk(x_sample, c_sample, g_mix, g_mlp, w_mod, b_mod, w_in, w_fourier, conv_w,
                     conv_b, w_rgate, b_rgate, w_igate, b_igate, lru_lambda, w_out, w_ff1,
                     w_ff2, g_final)
    return (y_prompt, y_sample)


_drawn_inputs = setup_inputs


def setup_inputs(seed=0):
    import zlib

    import numpy as np

    out = dict(_drawn_inputs(seed))
    spreads = {}
    factors = {'g_mix': 8.0,
     'g_mlp': 18.057,
     'conv_b': 3.863,
     'b_rgate': 23.038,
     'b_igate': 8.0,
     'g_final': 8.049}
    for name, (base, spread) in spreads.items():
        noise = np.random.default_rng([zlib.crc32(name.encode()), seed]).standard_normal(out[name].shape)
        drawn = base * np.exp(spread * noise) if base else spread * noise
        out[name] = __import__('jax').numpy.asarray(drawn.astype(out[name].dtype))
    for name, factor in factors.items():
        out[name] = (out[name] * factor).astype(out[name].dtype)
    return out
```

```python
from contextlib import ExitStack

import numpy as np

import concourse.bass as bass
from concourse import mybir

F32 = mybir.dt.float32
F32R = mybir.dt.float32r
ALU = mybir.AluOpType
ACT = mybir.ActivationFunctionType
AX = mybir.AxisListType

P = 128
CH = 512
SEQS = (1024, 512)
OFFS = (0, 1024)
T = sum(SEQS)
NCH = T // CH
SEQ_OF = (0, 0, 1)
D = 1024
KD = D // P
DF = 512
FT = DF // P
HEAD = 64
DFF = 4096
FB = 256
NB = DFF // FB
JB = FB // P
EPS = 1e-6
LRU_C = 8.0
NMOD = 6
NTILE = 3 * FT
TILES = [FT + j // 2 if j % 2 == 0 else 2 * FT + j // 2 for j in range(2 * FT)] + list(range(FT))
PADL, PADR = 2, 1
UPAD = (0, PADL + SEQS[0] + PADR)
UPADW = UPAD[1] + PADL + SEQS[1] + PADR

V_C = 0
V_BMOD = V_C + 2 * KD
V_GMIX = V_BMOD + NMOD * KD
V_GMLP = V_GMIX + KD
V_GFIN = V_GMLP + KD
V_CONVW = V_GFIN + KD
V_CONVB = V_CONVW + 4 * FT
V_BR = V_CONVB + FT
V_BI = V_BR + 2 * FT
V_LAM = V_BI + 2 * FT
NV = V_LAM + 2 * FT
SHIFT1, SCALE1, GATE1, SHIFT2, SCALE2, GATE2 = range(NMOD)


def build_encoder(nc, vec_d, xT_d, w_mod_d, w_in_d, w_gate_d, w_four_d, w_out_d, w_ff1_d, w_ff2_d,
                  dft_head_d, dft_seq_d, yT_d):
    ctx = ExitStack()

    def sem(name):
        return ctx.enter_context(nc.semaphore(name))

    base = (nc.sbuf_base + 31) // 32 * 32
    at = {}

    def place(name, shape, dtype, offset):
        at[name] = offset
        return nc.alloc_sbuf_tensor_at(name, shape, dtype, offset=offset)

    cur = [base]

    def fixed(name, shape, dtype=F32):
        t = place(name, shape, dtype, cur[0])
        cur[0] += (4 * int(np.prod(shape[1:])) + 31) // 32 * 32
        return t

    vec = fixed("vec", [P, NV])
    ones = fixed("ones", [P, P])
    ident = fixed("ident", [P, P])
    dft_head = fixed("dft_head", [P, 2, P])
    c_sig = fixed("c_sig", [P, 2 * KD])
    c_silu = fixed("c_silu", [P, KD, 32])
    mod = fixed("mod", [P, NMOD, KD, 2])
    amp1 = fixed("amp1", [P, KD, 2])
    amp2 = fixed("amp2", [P, KD, 2])
    eps = fixed("eps", [P, 1])
    decay = fixed("decay", [P, 2, 2 * FT])
    sp = fixed("sp", [P, 6, 2 * FT])
    edge = fixed("edge", [P, 4])
    alt = fixed("alt", [P, 2, 2])
    bias_e = fixed("bias_e", [P, 2, 2])
    A0 = cur[0]
    QT = 4 * T
    HALF = FT * QT
    hi_f = place("hi_f", [P, NCH, FT, CH], F32R, A0)
    lo_f = place("lo_f", [P, NCH, FT, CH], F32R, A0 + HALF)
    hi_r = place("hi_r", [P, NCH, FT, CH], F32R, A0 + 2 * HALF)
    lo_r = place("lo_r", [P, NCH, FT, CH], F32R, A0 + 3 * HALF)
    X0 = A0 + 4 * HALF
    W0 = X0 + 2 * HALF
    x = place("x", [P, NCH, KD, CH], F32, X0)

    def hi(c, k):
        return (hi_f, hi_r)[k // FT][:, c, k % FT, :]

    def lo(c, k):
        return (lo_f, lo_r)[k // FT][:, c, k % FT, :]

    rr = place("rr", [P, T], F32, X0)
    ii = place("ii", [P, T], F32, X0 + QT)
    aa = place("aa", [P, T], F32, X0 + 2 * QT)
    qq = place("qq", [P, T], F32, X0 + 3 * QT)
    uc = place("uc", [P, T], F32, X0 + 4 * QT)
    hf = place("hf", [P, T], F32, X0 + 5 * QT)
    uc_hi = place("uc_hi", [P, T], F32R, X0 + 6 * QT)
    uc_lo = place("uc_lo", [P, T], F32R, X0 + 7 * QT)
    yr = place("yr", [P, FT, T], F32, W0)
    u_pad = place("u_pad", [P, UPADW], F32, W0 + HALF)
    s0 = W0 + HALF + (4 * UPADW + 31) // 32 * 32
    mod_raw = place("mod_raw", [P, 2, 2048], F32, s0)
    ab_hi = place("ab_hi", [P, 2, FT, P], F32R, s0)
    ab_lo = place("ab_lo", [P, 2, FT, P], F32R, s0 + 4096)
    a_f32 = place("a_f32", [P, FT, P], F32, s0 + 8192)
    mod_row = place("mod_row", [P, CH], F32, s0 + 16384)
    s1 = s0 + 16384 + 2048
    win_hi = [place(f"win_hi{i}", [P, KD, P], F32R, s1 + 8192 * i) for i in range(2)]
    win_lo = [place(f"win_lo{i}", [P, KD, P], F32R, s1 + 8192 * i + 4096) for i in range(2)]
    s2 = s1 + 16384
    win_raw = place("win_raw", [P, KD * P], F32, s2)
    s3 = s2 + 4096
    wg_hi = place("wg_hi", [P, 4, P], F32R, s3)
    wg_lo = place("wg_lo", [P, 4, P], F32R, s3 + 2048)
    wg_raw = place("wg_raw", [P, 4 * P], F32, s3 + 4096)
    assert s3 + 6144 <= nc.sbuf_usable_end
    n1_sq = [place(f"n1_sq{i}", [P, CH], F32, W0 + 2048 * i) for i in range(2)]
    n1_acc = place("n1_acc", [P, CH], F32, W0 + 4096)
    n1_rstd = place("n1_rstd", [P, CH], F32, W0 + 6144)
    wf_raw = place("wf_raw", [P, FT * P], F32, s3 + 4096)
    u_f = [place("u_f0", [P, T], F32, s0 + 10240), place("u_f1", [P, T], F32, X0 + 6 * QT),
           place("u_f2", [P, T], F32, X0 + 7 * QT), place("u_f3", [P, T], F32, W0 + HALF)]
    HT = T // 2
    HOFF = (0, SEQS[0] // 2)
    fold = place("fold", [P, 2, HT], F32, s3)
    fold_hi = place("fold_hi", [P, 2, HT], F32R, X0 + 4 * QT)
    fold_lo = place("fold_lo", [P, 2, HT], F32R, X0 + 5 * QT)
    tab_hi = place("tab_hi", [P, 2, 4, CH], F32R, A0)
    tab_lo = place("tab_lo", [P, 2, 4, CH], F32R, A0 + 16384)
    tab_raw = place("tab_raw", [P, 8, CH], F32, A0 + 32768)
    pq_at = (s1, W0 + 12288)
    pq_hi = [place(f"pq_hi{i}", [P, 3, CH], F32R, o) for i, o in enumerate(pq_at)]
    pq_lo = [place(f"pq_lo{i}", [P, 3, CH], F32R, o + 6144) for i, o in enumerate(pq_at)]
    e_sb = [place(f"e_sb{i}", [P, CH], F32, s2 + 2048 * i) for i in range(2)]
    yf = place("yf", [P, FT, T], F32, X0)
    wo_hi = [place(f"wo_hi{q}", [P, FT, P], F32R, W0 + 4096 * q) for q in range(16)]
    wo_lo = [place(f"wo_lo{q}", [P, FT, P], F32R, W0 + 4096 * q + 2048) for q in range(16)]
    wo_raw = [place(f"wo_raw{i}", [P, FT * P], F32, s2 + 2048 * i) for i in range(2)]
    tmp = [place(f"tmp{i}", [P, CH], F32, s3 + 2048 * i) for i in range(3)]
    assert s2 >= W0 + 65536
    n_sq = [place("n_sq", [P, CH], F32, s2), tmp[2]]
    n_acc = place("n_acc", [P, CH], F32, s2 + 2048)
    w1_hi = place("w1_hi", [P, KD, FB], F32R, W0)
    w1_lo = place("w1_lo", [P, KD, FB], F32R, W0 + 8192)
    w2_hi = place("w2_hi", [P, JB, D], F32R, W0 + 16384)
    w2_lo = place("w2_lo", [P, JB, D], F32R, W0 + 24576)
    w12_raw = place("w12_raw", [P, KD * FB], F32, W0 + 32768)
    hid_hi = place("hid_hi", [P, NCH, JB, CH], F32R, W0 + 40960)
    hid_lo = place("hid_lo", [P, NCH, JB, CH], F32R, W0 + 40960 + 12288)

    bank = [ctx.enter_context(nc.psum_tensor(f"bank{i}", [P, CH], F32)) for i in range(8)]
    GB, MB, NBK = (4, 5), 6, 7

    ld_vec, ld_dft, ld_win, ld_wg, ld_wf, ld_tab, ld_w12 = map(
        sem, ("ld_vec", "ld_dft", "ld_win", "ld_wg", "ld_wf", "ld_tab", "ld_w12"))
    ld_x = [sem(f"ld_x{c}") for c in range(NCH)]
    ld_mod = [sem(f"ld_mod{i}") for i in range(2)]
    ld_wo = [sem(f"ld_wo{i}") for i in range(2)]
    st_y = [sem(f"st_y{i}") for i in range(2)]
    const_set = sem("const_set")
    sig_c = sem("sig_c")
    silu_c = sem("silu_c")
    lam_exp = sem("lam_exp")
    lam_abs = sem("lam_abs")
    decay_set = sem("decay_set")
    dve_own = sem("dve_own")
    act_own = sem("act_own")
    pool_own = sem("pool_own")
    sq_done = sem("sq_done")
    sq_read = sem("sq_read")
    amp_set = sem("amp_set")
    lru_ix = sem("lru_ix")
    acc_done = sem("acc_done")
    norm_mm = sem("norm_mm")
    sd_done = sem("sd_done")
    rstd_done = sem("rstd_done")
    xn_done = sem("xn_done")
    h_done = sem("h_done")
    hhi_done = sem("hhi_done")
    hlo_done = sem("hlo_done")
    mod_mm = sem("mod_mm")
    mod_rows = sem("mod_rows")
    mod_tr = sem("mod_tr")
    mod_cols = sem("mod_cols")
    win_hi_done, win_lo_done = sem("win_hi_done"), sem("win_lo_done")
    wg_hi_done, wg_lo_done = sem("wg_hi_done"), sem("wg_lo_done")
    in_mm = sem("in_mm")
    in_evac = sem("in_evac")
    conv_done = sem("conv_done")
    gate_mm = sem("gate_mm")
    gate_sig = sem("gate_sig")
    lru_a, lru_t, lru_q = sem("lru_a"), sem("lru_t"), sem("lru_q")
    lru_m2 = sem("lru_m2")
    lru_m = sem("lru_m")
    lru_done = sem("lru_done")
    ab_mm, ab_act, ab_set = sem("ab_mm"), sem("ab_act"), sem("ab_set")
    fold_done = sem("fold_done")
    fold_hi_done, fold_lo_done = sem("fold_hi_done"), sem("fold_lo_done")
    edge_done = sem("edge_done")
    pq_mm = sem("pq_mm")
    pq_hi_done, pq_lo_done = sem("pq_hi_done"), sem("pq_lo_done")
    bias_done = sem("bias_done")
    yf_edge = sem("yf_edge")
    eo_mm = sem("eo_mm")
    e_done = sem("e_done")
    eo_done = sem("eo_done")
    tab_hi_done, tab_lo_done = sem("tab_hi_done"), sem("tab_lo_done")
    mixr_hi, mixr_lo = sem("mixr_hi"), sem("mixr_lo")
    mixf_hi, mixf_lo = sem("mixf_hi"), sem("mixf_lo")
    wo_hi_done, wo_lo_done = sem("wo_hi_done"), sem("wo_lo_done")
    out_mm = sem("out_mm")
    out_evac = sem("out_evac")
    w1_hi_done, w1_lo_done = sem("w1_hi_done"), sem("w1_lo_done")
    w2_hi_done, w2_lo_done = sem("w2_hi_done"), sem("w2_lo_done")
    ff1_mm, ff1_relu = sem("ff1_mm"), sem("ff1_relu")
    ff1_sq = sem("ff1_sq")
    hid_hi_done, hid_lo_done = sem("hid_hi_done"), sem("hid_lo_done")
    ff2_mm, ff2_evac = sem("ff2_mm"), sem("ff2_evac")
    y_done = sem("y_done")

    def after(eng, s, value):
        if not isinstance(value, int) or value > 0:
            eng.wait_ge(s, value)

    NLOAD = NCH * KD

    def gate_group_after(j):
        return j - 1 if 1 <= j <= 2 * FT else None

    def mod_steps_after(j):
        return range(KD + 2 * j, KD + 2 * j + 2) if j < KD else ()

    LRU_ALL = 2 * FT
    block = ctx.enter_context(nc.Block())

    @block.sync
    def _(sp):
        sp.dma_start(vec[:], vec_d).then_inc(ld_vec, 16)
        for c in range(NCH):
            sp.dma_start(x[:, c, :, :], xT_d[:, c * CH:(c + 1) * CH].rearrange("(k p) n -> p k n", p=P)
                         ).then_inc(ld_x[c], 16)
        sp.dma_start(win_raw[:], w_in_d[TILES[0]]).then_inc(ld_win, 16)
        sp.dma_start(dft_head[:], dft_head_d).then_inc(ld_dft, 16)

        def load_mod(s):
            r, k = divmod(s, KD)
            after(sp, mod_mm, s - 1)
            sp.dma_start(mod_raw[:, s % 2, :], w_mod_d[k * P:(k + 1) * P, r * 2048:(r + 1) * 2048]
                         ).then_inc(ld_mod[s % 2], 16)

        for s in range(KD):
            load_mod(s)
        sp.dma_start(wg_raw[:], w_gate_d[0]).then_inc(ld_wg, 16)
        for j in range(NTILE):
            if j + 1 < NTILE:
                sp.wait_ge(win_lo_done, j + 1)
                sp.dma_start(win_raw[:], w_in_d[TILES[j + 1]]).then_inc(ld_win, 16)
            for s in mod_steps_after(j):
                load_mod(s)
            if j % 2 == 1 and j // 2 + 1 < FT:
                f = j // 2 + 1
                sp.wait_ge(wg_lo_done, f)
                sp.dma_start(wg_raw[:], w_gate_d[f]).then_inc(ld_wg, 16)
            if j == 2 * FT - 1:
                sp.wait_ge(wg_lo_done, FT)
                sp.dma_start(wf_raw[:], w_four_d).then_inc(ld_wf, 16)
        sp.wait_ge(in_mm, NCH * NTILE)
        sp.dma_start(tab_raw[:], dft_seq_d).then_inc(ld_tab, 16)

        def load_wo(q):
            if q < 2:
                sp.wait_ge(eo_done, 3 * FT)
            else:
                sp.wait_ge(wo_lo_done, q - 1)
            half, d = divmod(q, KD)
            k0 = FT * (1 - half)
            sp.dma_start(wo_raw[q % 2][:], w_out_d[d, :, k0 * P:(k0 + FT) * P]).then_inc(ld_wo[q % 2], 16)

        for q in range(10):
            load_wo(q)
        sp.wait_ge(mixf_hi, FT * NCH)
        sp.wait_ge(mixf_lo, FT * NCH)
        for c in range(NCH):
            sp.dma_start(x[:, c, :, :], xT_d[:, c * CH:(c + 1) * CH].rearrange("(k p) n -> p k n", p=P)
                         ).then_inc(ld_x[c], 16)
        for q in range(10, 16):
            load_wo(q)
        w1_src = w_ff1_d
        w2_src = w_ff2_d
        sp.wait_ge(out_mm, (NCH - 1) * KD + 2)
        sp.dma_start(w12_raw[:], w1_src[0]).then_inc(ld_w12, 16)
        sp.wait_ge(w1_lo_done, 1)
        sp.dma_start(w12_raw[:], w2_src[0]).then_inc(ld_w12, 16)
        with sp.Fori(1, NB) as b:
            sp.wait_ge(w2_lo_done, b)
            sp.dma_start(w12_raw[:], w1_src[bass.ds(b, 1), :, :].rearrange("o p n -> (o p) n")
                         ).then_inc(ld_w12, 16)
            sp.wait_ge(w1_lo_done, b + 1)
            sp.dma_start(w12_raw[:], w2_src[bass.ds(b, 1), :, :].rearrange("o p n -> (o p) n")
                         ).then_inc(ld_w12, 16)
        n_st = [0, 0]
        for c in range(NCH):
            for half in range(2):
                sp.wait_ge(y_done, c * KD + 4 * half + 4)
                rows = yT_d[half * 4 * P:(half + 1) * 4 * P, c * CH:(c + 1) * CH]
                sp.dma_start(rows.rearrange("(k p) n -> p k n", p=P), x[:, c, 4 * half:4 * half + 4, :]
                             ).then_inc(st_y[half], 16)
                n_st[half] += 16
                if c < NCH - 1:
                    sp.wait_ge(st_y[half], n_st[half])
        for half in range(2):
            sp.wait_ge(st_y[half], n_st[half])

    @block.tensor
    def _(pe):
        def three(out, w_hi, w_lo, v_hi, v_lo, first, last):
            pe.matmul(out, w_lo, v_hi, start=first, stop=False)
            pe.matmul(out, w_hi, v_lo, start=False, stop=False)
            return pe.matmul(out, w_hi, v_hi, start=False, stop=last)

        def norm_sum(n, b):
            pe.wait_ge(acc_done, 1 + n)
            if n > 0:
                pe.wait_ge(sd_done, n)
            pe.matmul(bank[b][:], ones[:], (n1_acc if n < NCH else n_acc)[:], start=True, stop=True
                      ).then_inc(norm_mm, 1)

        def mod_step(s):
            r, k = divmod(s, KD)
            if k == 0 and r > 0:
                pe.wait_ge(mod_rows, r)
            pe.wait_ge(ld_mod[s % 2], 16 * (s // 2 + 1))
            for q in range(4):
                m = pe.matmul(bank[MB][32 * q:32 * q + 32, :], c_silu[:, k, :],
                              mod_raw[:, s % 2, q * CH:(q + 1) * CH], start=(k == 0), stop=(k == KD - 1),
                              skip_group_check=True)
            m.then_inc(mod_mm, 1)

        def mod_transpose(r):
            pe.wait_ge(mod_rows, r + 1)
            pe.wait_ge(sd_done, NCH)
            if r > 0:
                pe.wait_ge(mod_cols, r)
            for b in range(4):
                m = pe.transpose(bank[NBK][:, b * P:(b + 1) * P], mod_row[:, b * P:(b + 1) * P], ident[:])
            m.then_inc(mod_tr, 1)

        def in_tile(j, c):
            n = NCH * j + c
            if n >= 4:
                pe.wait_ge(in_evac, n - 3)
            pe.wait_ge(win_lo_done, j + 1)
            for k in range(KD):
                if j == 0:
                    pe.wait_ge(hlo_done, c * KD + k + 1)
                m = three(bank[n % 4][:], win_hi[j % 2][:, k, :], win_lo[j % 2][:, k, :], hi(c, k), lo(c, k),
                          k == 0, k == KD - 1)
            m.then_inc(in_mm, 1)

        def gate_group(g):
            f, d = divmod(g, 2)
            pe.wait_ge(wg_lo_done, f + 1)
            pe.wait_ge(conv_done, f + 1)
            for gate in range(2):
                for c in range(NCH):
                    n = (2 * g + gate) * NCH + c
                    if n >= 2:
                        pe.wait_ge(gate_sig, n - 1)
                    cols = slice(c * CH, (c + 1) * CH)
                    three(bank[GB[n % 2]][:], wg_hi[:, 2 * d + gate, :], wg_lo[:, 2 * d + gate, :],
                          uc_hi[:, cols], uc_lo[:, cols], True, True).then_inc(gate_mm, 1)

        pe.wait_ge(const_set, 4)
        for c in range(NCH):
            norm_sum(c, NBK)
        pe.wait_ge(silu_c, 1)
        for s in range(KD):
            mod_step(s)
        mod_transpose(0)
        for j in range(NTILE):
            for c in range(NCH):
                in_tile(j, c)
            g = gate_group_after(j)
            if g is not None:
                gate_group(g)
            for s in mod_steps_after(j):
                mod_step(s)
                if s % KD == KD - 1:
                    mod_transpose(s // KD)
            if j == 2 * FT:
                pe.wait_ge(ld_dft, 16)
                pe.wait_ge(ld_wf, 16)
                pe.wait_ge(mod_cols, 3)
                pe.wait_ge(gate_sig, 2 * NCH * (gate_group_after(j) + 1))
                for t in range(2):
                    m = pe.matmul(bank[GB[t]][:], dft_head[:, t, :], wf_raw[:], start=True, stop=True)
                m.then_inc(ab_mm, 1)

        BP, BQ, BS, BE, BO, BT = 0, 1, 2, 3, 4, 5

        def pq(f):
            if f == 0:
                pe.wait_ge(in_evac, NCH * NTILE)
                pe.wait_ge(ab_set, 1)
                pe.wait_ge(mod_cols, 3)
            else:
                pe.wait_ge(pq_lo_done, 3 * f)
                pe.wait_ge(yf_edge, f)
            pe.wait_ge(fold_lo_done, f + 1)
            for t in range(2):
                for s in range(2):
                    for n in range(SEQS[s] // 2 // P):
                        cols = slice(HOFF[s] + n * P, HOFF[s] + (n + 1) * P)
                        out = (bank[t] if s == 0 else bank[BS])[:, (n + 2 * s * t) * P:(n + 2 * s * t + 1) * P]
                        m = three(out, fold_hi[:, t, cols], fold_lo[:, t, cols],
                                  ab_hi[:, t, f, :], ab_lo[:, t, f, :], True, True)
                m.then_inc(pq_mm, 1)
            pe.wait_ge(edge_done, f + 1)
            pe.matmul(bank[NBK][:, 0:4], a_f32[:, f, :], edge[:], start=True, stop=True).then_inc(pq_mm, 1)

        def eo(f):
            b = f % 2
            pe.wait_ge(pq_lo_done, 3 * f + 3)
            pe.wait_ge(tab_lo_done, 8)
            if f == 0:
                pe.wait_ge(ab_set, 1)
            for t in range(2):
                if f > 0:
                    pe.wait_ge(eo_done, 3 * (f - 1) + 1)
                for n in range(4):
                    m = three(bank[BE + t][:], pq_hi[b][:, t, n * P:(n + 1) * P], pq_lo[b][:, t, n * P:(n + 1) * P],
                              tab_hi[:, t, n, :], tab_lo[:, t, n, :], n == 0, n == 3)
            m.then_inc(eo_mm, 1)
            if f > 0:
                pe.wait_ge(eo_done, 3 * f)
            for t in range(2):
                for n in range(2):
                    w = slice((2 * t + n) * P, (2 * t + n + 1) * P)
                    m = three(bank[BT][:, t * 256:(t + 1) * 256], pq_hi[b][:, 2, w], pq_lo[b][:, 2, w],
                              tab_hi[:, t, n, ::2], tab_lo[:, t, n, ::2], n == 0, n == 1)
            m.then_inc(eo_mm, 1)

        pq(0)
        for f in range(FT):
            if f + 1 < FT:
                pq(f + 1)
            eo(f)

        def out_half(c, d, half, b, first, last):
            for kk in range(FT):
                k = FT * (1 - half) + kk
                q = half * KD + d
                m = three(bank[b][:], wo_hi[q][:, kk, :], wo_lo[q][:, kk, :], hi(c, k), lo(c, k),
                          first and kk == 0, last and kk == FT - 1)
            return m

        pe.wait_ge(eo_done, 3 * FT)
        pe.wait_ge(mixr_lo, FT * NCH)
        for d in range(KD):
            pe.wait_ge(wo_lo_done, d + 1)
            out_half(0, d, 0, d, True, False)
        for d in range(KD):
            pe.wait_ge(wo_lo_done, KD + d + 1)
            pe.wait_ge(mixf_lo, FT)
            out_half(0, d, 1, d, False, True).then_inc(out_mm, 1)
        pe.wait_ge(mixf_lo, FT * NCH)
        for c in range(1, NCH):
            for d in range(KD):
                n = (c - 1) * KD + d
                pe.wait_ge(out_evac, n % 6 + 1 if n < 6 else KD + n - 5)
                out_half(c, d, 0, n % 6, True, False)
                out_half(c, d, 1, n % 6, False, True).then_inc(out_mm, 1)
                if d == 3:
                    if c == 1:
                        pe.wait_ge(out_evac, KD)
                    norm_sum(NCH + c - 1, NBK)
        pe.wait_ge(out_evac, NCH * KD)

        def mlp_block(b, middle=None):
            pe.wait_ge(w1_lo_done, b + 1)
            for c in range(NCH):
                if isinstance(b, int) and b == 0:
                    pe.wait_ge(hlo_done, NLOAD + (c + 1) * KD)
                for j in range(JB):
                    n = JB * c + j
                    after(pe, ff1_relu, JB * NCH * b + n - 2)
                    for k in range(KD):
                        w = slice(j * P, (j + 1) * P)
                        m = three(bank[n % 3][:], w1_hi[:, k, w], w1_lo[:, k, w], hi(c, k), lo(c, k),
                                  k == 0, k == KD - 1)
                    m.then_inc(ff1_mm, 1)
                if middle == "norm2" and c == 0:
                    norm_sum(2 * NCH - 1, NBK)
            pe.wait_ge(w2_lo_done, b + 1)
            for c in range(NCH):
                pe.wait_ge(hid_lo_done, JB * NCH * b + JB * (c + 1))
                for d in range(KD):
                    n = KD * c + d
                    after(pe, ff2_evac, NCH * KD * b + n - 3)
                    w = slice(d * P, (d + 1) * P)
                    for j in range(JB):
                        m = three(bank[3 + n % 4][:], w2_hi[:, j, w], w2_lo[:, j, w],
                                  hid_hi[:, c, j, :], hid_lo[:, c, j, :], j == 0, j == JB - 1)
                    m.then_inc(ff2_mm, 1)
                if middle == "norm3" and c > 0:
                    norm_sum(2 * NCH + c - 1, NBK)

        mlp_block(0, "norm2")
        with pe.Fori(1, NB - 1) as b:
            mlp_block(b)
        mlp_block(NB - 1, "norm3")
        norm_sum(3 * NCH - 1, NBK)

    @block.scalar
    def _(act):
        own = [0]

        def chain(ins):
            own[0] += 1
            ins.then_inc(act_own, 1)
            act.wait_ge(act_own, own[0])

        def squares(n, c):
            first = n < NCH
            for k in range(KD):
                m = n * KD + k
                if first:
                    if k == 0:
                        act.wait_ge(ld_x[c], 16)
                        after(act, norm_mm, n)
                    dst = n1_acc if k == 0 else n1_sq[k % 2]
                else:
                    if n < 2 * NCH:
                        act.wait_ge(out_evac, c * KD + k + 1)
                    else:
                        act.wait_ge(ff2_evac, (NB - 1) * NCH * KD + c * KD + k + 1)
                    if k == 0:
                        act.wait_ge(norm_mm, n)
                        if n == NCH:
                            act.wait_ge(wo_lo_done, 16)
                        else:
                            if n <= 2 * NCH:
                                act.wait_ge(hlo_done, (n - NCH + NCH) * KD)
                            else:
                                act.wait_ge(y_done, (n - 2 * NCH) * KD)
                    dst = n_acc if k == 0 else n_sq[k % 2]
                if first and k == 2:
                    after(act, rstd_done, n)
                if k > 2:
                    act.wait_ge(sq_read, n * (KD - 1) + k - 2)
                act.activation(dst[:], x[:, c, k, :], ACT.Square).then_inc(sq_done, 1)

        def root(n):
            act.wait_ge(norm_mm, n + 1)
            act.wait_ge(sq_read, (n + 1) * (KD - 1))
            dst = n1_sq[0] if n < NCH else n_sq[0]
            act.activation(dst[:], bank[NBK][:], ACT.Sqrt, bias=eps[:], scale=1.0 / D).then_inc(sd_done, 1)

        def split_win_hi(j):
            act.wait_ge(ld_win, 16 * (j + 1))
            if j >= 2:
                act.wait_ge(in_mm, NCH * (j - 1))
            act.activation(win_hi[j % 2][:].rearrange("p k m -> p (k m)"), win_raw[:], ACT.Copy
                           ).then_inc(win_hi_done, 1)

        def split_wg_hi(f):
            act.wait_ge(ld_wg, 16 * (f + 1))
            after(act, gate_mm, 4 * NCH * f)
            act.activation(wg_hi[:].rearrange("p g m -> p (g m)"), wg_raw[:], ACT.Copy).then_inc(wg_hi_done, 1)

        act.wait_ge(ld_vec, 16)
        act.activation(c_sig[:], vec[:, V_C:V_C + 2 * KD], ACT.Sigmoid).then_inc(sig_c, 1)
        act.wait_ge(lam_abs, 1)
        act.activation(sp[:, 1, :], sp[:, 0, :], ACT.Exp, scale=-1.0).then_inc(lam_exp, 1)
        act.wait_ge(const_set, 4)
        for c in range(NCH):
            squares(c, c)
            root(c)
        split_win_hi(0)

        def mod_copy(r):
            act.wait_ge(mod_mm, KD * (r + 1))
            if r > 0:
                act.wait_ge(mod_tr, r)
            act.activation(mod_row[:], bank[MB][:], ACT.Copy).then_inc(mod_rows, 1)

        mod_copy(0)
        act.wait_ge(mod_cols, 1)
        act.wait_ge(amp_set, 1)
        for c in range(NCH):
            s = SEQ_OF[c]
            for k in range(KD):
                n = c * KD + k
                act.wait_ge(xn_done, n + 1)
                act.activation(x[:, c, k, :], x[:, c, k, :], ACT.Identity, bias=mod[:, SHIFT1, k, s:s + 1],
                               scale=amp1[:, k, s:s + 1]).then_inc(h_done, 1)
                act.wait_ge(h_done, n + 1)
                act.activation(hi(c, k), x[:, c, k, :], ACT.Copy).then_inc(hhi_done, 1)
        split_win_hi(1)
        act.wait_ge(hlo_done, NLOAD)
        split_wg_hi(0)

        def evac_in(j):
            for c in range(NCH):
                n = NCH * j + c
                act.wait_ge(in_mm, n + 1)
                src = bank[n % 4][:]
                cols = slice(c * CH, (c + 1) * CH)
                if j < 2 * FT and j % 2 == 0:
                    s = SEQ_OF[c]
                    after(act, conv_done, j // 2)
                    o = UPAD[s] + PADL + c * CH - OFFS[s]
                    act.activation(u_pad[:, o:o + CH], src, ACT.Copy).then_inc(in_evac, 1)
                elif j < 2 * FT:
                    act.activation(yr[:, j // 2, cols], src, ACT.Gelu_apprx_tanh).then_inc(in_evac, 1)
                else:
                    f = j - 2 * FT
                    if f == 0:
                        act.wait_ge(mod_mm, 3 * KD)
                    if f in (1, 2):
                        act.wait_ge(gate_mm, 2 * NCH * LRU_ALL)
                    if f == 3:
                        act.wait_ge(conv_done, FT)
                    act.activation(u_f[f][:, cols], src, ACT.Copy).then_inc(in_evac, 1)

        def lru_group(g):
            f, d = divmod(g, 2)
            after(act, lru_done, g)
            for gate, (dst, col) in enumerate(((rr, V_BR), (ii, V_BI))):
                for c in range(NCH):
                    n = (2 * g + gate) * NCH + c
                    act.wait_ge(gate_mm, n + 1)
                    b = vec[:, col + d * FT + f:col + d * FT + f + 1]
                    act.activation(dst[:, c * CH:(c + 1) * CH], bank[GB[n % 2]][:], ACT.Sigmoid, bias=b
                                   ).then_inc(gate_sig, 1)
            act.wait_ge(gate_sig, (2 * g + 1) * NCH)
            act.wait_ge(decay_set, 1)
            w = d * FT + f
            act.activation(aa[:], rr[:], ACT.Exp, scale=decay[:, 0, w:w + 1]).then_inc(lru_a, 1)
            act.wait_ge(lru_a, g + 1)
            act.activation(rr[:], rr[:], ACT.Tanh, scale=decay[:, 1, w:w + 1]).then_inc(lru_t, 1)
            act.activation(qq[:], aa[:], ACT.Square).then_inc(lru_q, 1)
            act.wait_ge(lru_m2, g + 1)
            act.activation(qq[:], qq[:], ACT.Sqrt).then_inc(lru_m, 1)

        for j in range(NTILE):
            if j + 1 < NTILE and j > 0:
                split_win_hi(j + 1)
            if j % 2 == 1 and 0 < (j + 1) // 2 < FT:
                pass
            evac_in(j)
            g = gate_group_after(j)
            if g is not None:
                lru_group(g)
                if g % 2 == 1 and g // 2 + 1 < FT:
                    split_wg_hi(g // 2 + 1)
            if j == 3:
                mod_copy(1)
            if j == 7:
                mod_copy(2)
            if j == 2 * FT:
                act.wait_ge(ab_mm, 1)
                act.activation(a_f32[:].rearrange("p f m -> p (f m)"), bank[GB[0]][:], ACT.Copy)
                act.activation(ab_hi[:, 0].rearrange("p f m -> p (f m)"), bank[GB[0]][:], ACT.Copy)
                act.activation(ab_hi[:, 1].rearrange("p f m -> p (f m)"), bank[GB[1]][:], ACT.Copy
                               ).then_inc(ab_act, 1)

        def fold_split_hi(f):
            act.wait_ge(fold_done, f + 1)
            if f > 0:
                act.wait_ge(pq_mm, 3 * (f - 1) + 2)
            else:
                act.wait_ge(lru_done, LRU_ALL)
            act.activation(fold_hi[:].rearrange("p t n -> p (t n)"), fold[:].rearrange("p t n -> p (t n)"),
                           ACT.Copy).then_inc(fold_hi_done, 1)

        def pq_split_hi(f):
            b = f % 2
            if f == 0:
                act.wait_ge(in_mm, NCH * NTILE)
            elif f == 1:
                act.wait_ge(mixr_hi, FT * NCH)
                act.wait_ge(mixr_lo, FT * NCH)
            else:
                act.wait_ge(eo_mm, 2 * (f - 1))
            act.wait_ge(pq_mm, 3 * f + 2)
            for i in range(3):
                act.activation(pq_hi[b][:, i, :], bank[i][:], ACT.Copy,
                               scale=SEQS[0 if i < 2 else 1] ** -0.5).then_inc(pq_hi_done, 1)

        def edge_out(f):
            act.wait_ge(pq_mm, 3 * f + 3)
            if f > 0:
                act.wait_ge(e_done, 4 * f)
            for s in range(2):
                norm = SEQS[s] ** -0.5
                for sign in range(2):
                    act.activation(bias_e[:, s, sign:sign + 1], bank[NBK][:, 2 * s:2 * s + 1], ACT.Copy,
                                   scale=norm * (1 - 2 * sign)).then_inc(bias_done, 1)
            for s in range(2):
                k = OFFS[s] + SEQS[s] // 2
                m = act.activation(yf[:, f, k:k + 1], bank[NBK][:, 2 * s + 1:2 * s + 2], ACT.Copy,
                                   scale=SEQS[s] ** -0.5)
            m.then_inc(yf_edge, 1)

        def copy_e(f):
            act.wait_ge(bias_done, 4 * (f + 1))
            for s in range(2):
                act.wait_ge(eo_mm, 2 * f + s + 1)
                after(act, eo_done, 3 * (f - 1) + 1 + 2 * s)
                src = bank[3][:] if s == 0 else bank[5][:, 0:256]
                h = SEQS[s] // 2
                for sign in range(2):
                    act.activation(e_sb[s][:, sign:h:2], src[:, sign::2], ACT.Identity,
                                   bias=bias_e[:, s, sign:sign + 1]).then_inc(e_done, 1)

        fold_split_hi(0)
        act.wait_ge(in_mm, NCH * NTILE)
        for f in range(FT):
            for c in range(NCH):
                act.activation(hi_r[:, c, f, :], yr[:, f, c * CH:(c + 1) * CH], ACT.Copy).then_inc(mixr_hi, 1)
        pq_split_hi(0)
        edge_out(0)
        act.wait_ge(ld_tab, 16)
        for i in range(8):
            act.activation(tab_hi[:, i // 4, i % 4, :], tab_raw[:, i, :], ACT.Copy).then_inc(tab_hi_done, 1)
        for f in range(FT):
            if f + 1 < FT:
                fold_split_hi(f + 1)
                pq_split_hi(f + 1)
            copy_e(f)
            if f + 1 < FT:
                edge_out(f + 1)

        def split_wo_hi(q):
            act.wait_ge(ld_wo[q % 2], 16 * (q // 2 + 1))
            act.activation(wo_hi[q][:].rearrange("p k m -> p (k m)"), wo_raw[q % 2][:], ACT.Copy
                           ).then_inc(wo_hi_done, 1)

        act.wait_ge(eo_done, 3 * FT)
        split_wo_hi(0)
        split_wo_hi(1)
        for c in range(NCH):
            for f in range(FT):
                act.activation(hi_f[:, c, f, :], yf[:, f, c * CH:(c + 1) * CH], ACT.Copy).then_inc(mixf_hi, 1)
            for q in range(4 * c + 2, 4 * c + 6):
                split_wo_hi(q)
        for q in range(14, 16):
            split_wo_hi(q)

        def modulate(n, c):
            s = SEQ_OF[c]
            for k in range(KD):
                m = n * KD + k
                act.wait_ge(xn_done, m + 1)
                act.activation(n_sq[k % 2][:], n_sq[k % 2][:], ACT.Identity, bias=mod[:, SHIFT2, k, s:s + 1],
                               scale=amp2[:, k, s:s + 1]).then_inc(h_done, 1)
                act.wait_ge(h_done, m + 1)
                act.activation(hi(c, k), n_sq[k % 2][:], ACT.Copy).then_inc(hhi_done, 1)

        def split_w(b, which):
            dst, done, used = ((w1_hi, w1_hi_done, None), (w2_hi, w2_hi_done, None))[which]
            act.wait_ge(ld_w12, 16 * (2 * b + which + 1))
            if isinstance(b, int) and b == 0:
                act.wait_ge(out_mm, (NCH - 1) * KD + 4 if which == 0 else NCH * KD)
            elif which == 0:
                act.wait_ge(ff1_mm, JB * NCH * b)
            else:
                act.wait_ge(ff2_mm, NCH * KD * b)
            flat = dst[:].rearrange("p a m -> p (a m)")
            for i in range(4):
                act.activation(flat[:, i * CH:(i + 1) * CH], w12_raw[:, i * CH:(i + 1) * CH], ACT.Copy
                               ).then_inc(done, 1)

        for c in range(NCH - 1):
            squares(NCH + c, c)
            root(NCH + c)
            modulate(NCH + c, c)
        split_w(0, 0)
        squares(2 * NCH - 1, NCH - 1)

        def hidden(b, c):
            for j in range(JB):
                i = JB * c + j
                n = JB * NCH * b + i
                act.wait_ge(ff1_mm, n + 1)
                after(act, hid_lo_done, n - 1)
                act.activation(tmp[j][:], bank[i % 3][:], ACT.Relu).then_inc(ff1_relu, 1)
                act.wait_ge(ff1_relu, n + 1)
                act.activation(tmp[j][:], tmp[j][:], ACT.Square).then_inc(ff1_sq, 1)
                act.wait_ge(ff1_sq, n + 1)
                act.activation(hid_hi[:, c, j, :], tmp[j][:], ACT.Copy).then_inc(hid_hi_done, 1)

        def mlp_block(b, first=False, last=False):
            hidden(b, 0)
            if first:
                root(2 * NCH - 1)
                modulate(2 * NCH - 1, NCH - 1)
            split_w(b, 1)
            hidden(b, 1)
            hidden(b, 2)
            if not last:
                split_w(b + 1, 0)

        mlp_block(0, first=True)
        with act.Fori(1, NB - 1) as b:
            mlp_block(b)
        mlp_block(NB - 1, last=True)
        for c in range(NCH):
            squares(2 * NCH + c, c)
            root(2 * NCH + c)

    @block.vector
    def _(dve):
        own = [0]

        def chain(ins):
            own[0] += 1
            ins.then_inc(dve_own, 1)
            dve.wait_ge(dve_own, own[0])

        def sum_squares(n):
            acc, sq = (n1_acc, n1_sq) if n < NCH else (n_acc, n_sq)
            for k in range(1, KD):
                dve.wait_ge(sq_done, n * KD + k + 1)
                m = dve.tensor_tensor(acc[:], acc[:], sq[k % 2][:], ALU.add).then_inc(sq_read, 1)
                dve.wait_ge(sq_read, n * (KD - 1) + k)
            dve.sem_inc(acc_done, 1)

        def rstd(n):
            dve.wait_ge(sd_done, n + 1)
            if n < NCH:
                dve.reciprocal(n1_rstd[:], n1_sq[0][:]).then_inc(rstd_done, 1)
            else:
                dve.reciprocal(n_acc[:], n_sq[0][:]).then_inc(rstd_done, 1)
            dve.wait_ge(rstd_done, n + 1)

        def amplitude(dst, g, scale):
            for s in range(2):
                m = dve.scalar_tensor_tensor(dst[:, :, s], mod[:, scale, :, s], 1.0, vec[:, g:g + KD], ALU.add,
                                             ALU.mult)
            m.then_inc(amp_set, 1)

        def mod_columns(r):
            dve.wait_ge(mod_tr, r + 1)
            src = bank[NBK][:].rearrange("p (b i h s) -> p i h b s", b=4, i=2, h=2)
            bm = vec[:, V_BMOD + 2 * r * KD:V_BMOD + 2 * (r + 1) * KD].rearrange("p (i h b) -> p i h b", i=2, h=2)
            dst = mod[:, 2 * r:2 * r + 2, :, :].rearrange("p i (h b) s -> p i h b s", h=2)
            for s in range(2):
                for i in range(2):
                    m = dve.tensor_tensor(dst[:, i, :, :, s], src[:, i, :, :, s], bm[:, i], ALU.add)
            m.then_inc(mod_cols, 1)
            dve.wait_ge(mod_cols, r + 1)

        dve.wait_ge(ld_vec, 16)
        dve.wait_ge(const_set, 4)
        lam = vec[:, V_LAM:V_LAM + 2 * FT]
        chain(dve.tensor_scalar(sp[:, 2, :], lam, -1.0, None, ALU.mult))
        chain(dve.tensor_tensor(sp[:, 0, :], lam, sp[:, 2, :], ALU.max))
        dve.sem_inc(lam_abs, 1)
        dve.wait_ge(sig_c, 1)
        for s in range(2):
            m = dve.tensor_tensor(c_silu[:, :, s], vec[:, V_C + s * KD:V_C + (s + 1) * KD],
                                  c_sig[:, s * KD:(s + 1) * KD], ALU.mult)
        m.then_inc(silu_c, 1)
        dve.wait_ge(lam_exp, 1)
        chain(dve.tensor_scalar(sp[:, 3, :], sp[:, 1, :], 2.0, None, ALU.add))
        chain(dve.reciprocal(sp[:, 4, :], sp[:, 3, :]))
        chain(dve.tensor_tensor(sp[:, 3, :], sp[:, 1, :], sp[:, 4, :], ALU.mult))
        chain(dve.tensor_tensor(sp[:, 4, :], sp[:, 3, :], sp[:, 3, :], ALU.mult))
        chain(dve.tensor_scalar(sp[:, 5, :], sp[:, 4, :], 1.0 / 19, None, ALU.mult))
        for odd in range(17, 2, -2):
            chain(dve.scalar_tensor_tensor(sp[:, 5, :], sp[:, 5, :], 1.0 / odd, sp[:, 4, :], ALU.add, ALU.mult))
        chain(dve.scalar_tensor_tensor(sp[:, 5, :], sp[:, 5, :], 1.0, sp[:, 3, :], ALU.add, ALU.mult))
        chain(dve.tensor_scalar(sp[:, 2, :], sp[:, 2, :], 0.0, None, ALU.max))
        chain(dve.scalar_tensor_tensor(sp[:, 5, :], sp[:, 5, :], 2.0, sp[:, 2, :], ALU.mult, ALU.add))
        dve.tensor_scalar(decay[:, 0, :], sp[:, 5, :], -LRU_C, None, ALU.mult)
        dve.tensor_scalar(decay[:, 1, :], sp[:, 5, :], LRU_C, None, ALU.mult).then_inc(decay_set, 1)
        for c in range(NCH):
            sum_squares(c)
            rstd(c)
            for k in range(KD):
                dve.tensor_tensor(x[:, c, k, :], x[:, c, k, :], n1_rstd[:], ALU.mult).then_inc(xn_done, 1)
            dve.wait_ge(xn_done, (c + 1) * KD)
        mod_columns(0)
        amplitude(amp1, V_GMIX, SCALE1)
        for c in range(NCH):
            for k in range(KD):
                dve.wait_ge(hhi_done, c * KD + k + 1)
                dve.tensor_tensor(lo(c, k), x[:, c, k, :], hi(c, k), ALU.subtract).then_inc(hlo_done, 1)

        def conv(f):
            dve.wait_ge(in_evac, NCH * (2 * f + 1))
            after(dve, lru_done, 2 * f)
            after(dve, gate_mm, 4 * NCH * f)
            w = [vec[:, V_CONVW + t * FT + f:V_CONVW + t * FT + f + 1] for t in range(4)]
            b = vec[:, V_CONVB + f:V_CONVB + f + 1]
            for t in range(4):
                for s in range(2):
                    src = u_pad[:, UPAD[s] + t:UPAD[s] + t + SEQS[s]]
                    dst = uc[:, OFFS[s]:OFFS[s] + SEQS[s]]
                    if t == 0:
                        m = dve.tensor_scalar(dst, src, w[0], b, ALU.mult, ALU.add)
                    else:
                        m = dve.scalar_tensor_tensor(dst, src, w[t], dst, ALU.mult, ALU.add)
                chain(m)
            chain(dve.tensor_copy(uc_hi[:], uc[:]))
            dve.tensor_tensor(uc_lo[:], uc[:], uc_hi[:], ALU.subtract).then_inc(conv_done, 1)

        def lru_group(g):
            f, d = divmod(g, 2)
            dve.wait_ge(gate_sig, 2 * NCH * (g + 1))
            dve.tensor_tensor(ii[:], ii[:], uc[:], ALU.mult).then_inc(lru_ix, 1)
            dve.wait_ge(lru_q, g + 1)
            chain(dve.scalar_tensor_tensor(qq[:], qq[:], 1.0, rr[:], ALU.add, ALU.mult))
            dve.tensor_scalar(qq[:], qq[:], 0.0, None, ALU.max).then_inc(lru_m2, 1)
            dve.wait_ge(lru_m, g + 1)
            dve.wait_ge(lru_ix, g + 1)
            chain(dve.tensor_tensor(ii[:], ii[:], qq[:], ALU.mult))
            dst = (hf, rr)[d]
            for s in range(2):
                o, e = OFFS[s], OFFS[s] + SEQS[s]
                cols = slice(o, e) if d == 0 else slice(e - 1, o - 1 if o else None, -1)
                m = dve.tensor_tensor_scan(dst[:, cols], aa[:, cols], ii[:, cols], 0.0, ALU.mult, ALU.add)
            if d == 0:
                m.then_inc(lru_done, 1)
            else:
                chain(m)
                chain(dve.tensor_tensor(hf[:], hf[:], rr[:], ALU.add))
                dve.wait_ge(in_evac, NCH * (2 * f + 2))
                dve.tensor_tensor(yr[:, f, :], yr[:, f, :], hf[:], ALU.mult).then_inc(lru_done, 1)
                dve.wait_ge(lru_done, g + 1)

        for j in range(NTILE):
            g = gate_group_after(j)
            if g is not None:
                lru_group(g)
            if j % 2 == 0 and j < 2 * FT:
                conv(j // 2)
            if j == 3:
                mod_columns(1)
            if j == 7:
                mod_columns(2)
                amplitude(amp2, V_GMLP, SCALE2)
            if j == 2 * FT:
                dve.wait_ge(ab_act, 1)
                for t in range(2):
                    m = dve.tensor_tensor(ab_lo[:, t].rearrange("p f m -> p (f m)"), bank[GB[t]][:],
                                          ab_hi[:, t].rearrange("p f m -> p (f m)"), ALU.subtract)
                m.then_inc(ab_set, 1)

        def edges(f):
            dve.wait_ge(in_evac, NCH * (2 * FT + f + 1))
            if f > 0:
                dve.wait_ge(pq_mm, 3 * f)
            for s in range(2):
                u = u_f[f][:, OFFS[s]:OFFS[s] + SEQS[s]]
                dve.tensor_copy(edge[:, 2 * s:2 * s + 1], u[:, SEQS[s] // 2:SEQS[s] // 2 + 1])
                m = dve.tensor_reduce(alt[:, s, :], u.rearrange("p (n t) -> p t n", t=2), AX.X, ALU.add)
            chain(m)
            for s in range(2):
                m = dve.tensor_tensor(edge[:, 2 * s + 1:2 * s + 2], alt[:, s, 0:1], alt[:, s, 1:2], ALU.subtract)
            m.then_inc(edge_done, 1)

        def pq_split_lo(f):
            b = f % 2
            for i in range(3):
                dve.wait_ge(pq_hi_done, 3 * f + i + 1)
                dve.scalar_tensor_tensor(pq_lo[b][:, i, :], bank[i][:], SEQS[0 if i < 2 else 1] ** -0.5,
                                         pq_hi[b][:, i, :], ALU.mult, ALU.subtract).then_inc(pq_lo_done, 1)

        def unfold(f):
            for s in range(2):
                h = SEQS[s] // 2
                o = OFFS[s]
                dve.wait_ge(e_done, 4 * f + 2 * s + 2)
                dve.wait_ge(eo_mm, 2 * f + s + 1)
                odd = bank[4][:] if s == 0 else bank[5][:, 256:512]
                m = dve.tensor_tensor(yf[:, f, o:o + h], e_sb[s][:, 0:h], odd[:, 0:h], ALU.subtract)
                if s == 0:
                    m = dve.tensor_tensor(yf[:, f, o + 2 * h - 1:o + h:-1], e_sb[s][:, 1:h], odd[:, 1:h], ALU.add)
                    m.then_inc(eo_done, 1)
                else:
                    m.then_inc(eo_done, 1)
                    dve.tensor_tensor(yf[:, f, o + 2 * h - 1:o + h:-1], e_sb[s][:, 1:h], odd[:, 1:h], ALU.add
                                      ).then_inc(eo_done, 1)

        edges(0)
        pq_split_lo(0)
        for i in range(8):
            dve.wait_ge(tab_hi_done, i + 1)
            dve.tensor_tensor(tab_lo[:, i // 4, i % 4, :], tab_raw[:, i, :], tab_hi[:, i // 4, i % 4, :],
                              ALU.subtract).then_inc(tab_lo_done, 1)
        for f in range(FT):
            if f + 1 < FT:
                edges(f + 1)
                pq_split_lo(f + 1)
            unfold(f)
        for c in range(NCH):
            for f in range(FT):
                dve.wait_ge(mixf_hi, c * FT + f + 1)
                dve.tensor_tensor(lo_f[:, c, f, :], yf[:, f, c * CH:(c + 1) * CH], hi_f[:, c, f, :],
                                  ALU.subtract).then_inc(mixf_lo, 1)

        def norm_apply(n, c):
            rstd(n)
            for k in range(KD + 1):
                if k < KD:
                    if k >= 2:
                        dve.wait_ge(hlo_done, n * KD + k - 1)
                    dve.tensor_tensor(n_sq[k % 2][:], x[:, c, k, :], n_acc[:], ALU.mult).then_inc(xn_done, 1)
                if k > 0:
                    dve.wait_ge(hhi_done, n * KD + k)
                    dve.tensor_tensor(lo(c, k - 1), n_sq[(k - 1) % 2][:], hi(c, k - 1), ALU.subtract
                                      ).then_inc(hlo_done, 1)

        for c in range(NCH):
            s = SEQ_OF[c]
            dve.wait_ge(ld_x[c], 32)
            for d in range(KD):
                n = c * KD + d
                dve.wait_ge(out_mm, n + 1)
                b = d if c == 0 else (n - KD) % 6
                dve.scalar_tensor_tensor(x[:, c, d, :], bank[b][:], mod[:, GATE1, d, s:s + 1], x[:, c, d, :],
                                         ALU.mult, ALU.add).then_inc(out_evac, 1)
                if c > 0 and d == 4:
                    norm_apply(NCH + c - 1, c - 1)
            sum_squares(NCH + c)

        def hidden_lo(b, c):
            for j in range(JB):
                n = JB * NCH * b + JB * c + j
                dve.wait_ge(hid_hi_done, n + 1)
                dve.tensor_tensor(hid_lo[:, c, j, :], tmp[j][:], hid_hi[:, c, j, :], ALU.subtract
                                  ).then_inc(hid_lo_done, 1)

        def mlp_block(b, first=False, last=False):
            hidden_lo(b, 0)
            if first:
                norm_apply(2 * NCH - 1, NCH - 1)
            hidden_lo(b, 1)
            hidden_lo(b, 2)
            for c in range(NCH):
                s = SEQ_OF[c]
                for d in range(KD):
                    n = KD * c + d
                    dve.wait_ge(ff2_mm, NCH * KD * b + n + 1)
                    dve.scalar_tensor_tensor(x[:, c, d, :], bank[3 + n % 4][:], mod[:, GATE2, d, s:s + 1],
                                             x[:, c, d, :], ALU.mult, ALU.add).then_inc(ff2_evac, 1)
                    if last and c > 0 and d == 4:
                        final(c - 1)
                if last:
                    sum_squares(2 * NCH + c)

        def final(c):
            n = 2 * NCH + c
            rstd(n)
            for k in range(KD):
                dve.scalar_tensor_tensor(x[:, c, k, :], x[:, c, k, :], vec[:, V_GFIN + k:V_GFIN + k + 1], n_acc[:],
                                         ALU.mult, ALU.mult).then_inc(y_done, 1)

        mlp_block(0, first=True)
        with dve.Fori(1, NB - 1) as b:
            mlp_block(b)
        mlp_block(NB - 1, last=True)
        final(NCH - 1)

    @block.gpsimd
    def _(pool):
        pool.memset(c_silu[:], 0.0).then_inc(const_set, 1)
        pool.memset(ones[:], 1.0).then_inc(const_set, 1)
        pool.memset(eps[:], EPS).then_inc(const_set, 1)
        pool.memset(ident[:], 0.0).then_inc(pool_own, 1)
        pool.wait_ge(pool_own, 1)
        pool.affine_select(out=ident[:], in_=ident[:], compare_op=ALU.not_equal, fill=1.0, base=0,
                           pattern=[[-1, P]], channel_multiplier=1).then_inc(const_set, 1)
        for s in range(2):
            pool.memset(u_pad[:, UPAD[s]:UPAD[s] + PADL], 0.0)
            m = pool.memset(u_pad[:, UPAD[s] + PADL + SEQS[s]:UPAD[s] + PADL + SEQS[s] + PADR], 0.0)
        m.then_inc(const_set, 1)

        def split_win_lo(j):
            pool.wait_ge(win_hi_done, j + 1)
            pool.tensor_tensor(win_lo[j % 2][:].rearrange("p k m -> p (k m)"), win_raw[:],
                               win_hi[j % 2][:].rearrange("p k m -> p (k m)"), ALU.subtract
                               ).then_inc(win_lo_done, 1)

        split_win_lo(0)
        split_win_lo(1)

        def split_wg_lo(f):
            pool.wait_ge(wg_hi_done, f + 1)
            pool.tensor_tensor(wg_lo[:].rearrange("p g m -> p (g m)"), wg_raw[:],
                               wg_hi[:].rearrange("p g m -> p (g m)"), ALU.subtract).then_inc(wg_lo_done, 1)

        split_wg_lo(0)
        for j in range(NTILE):
            if j + 1 < NTILE and j > 0:
                split_win_lo(j + 1)
            g = gate_group_after(j)
            if g is not None and g % 2 == 1 and g // 2 + 1 < FT:
                split_wg_lo(g // 2 + 1)

        def make_fold(f):
            pool.wait_ge(in_evac, NCH * (2 * FT + f + 1))
            if f == 0:
                pool.wait_ge(gate_mm, 2 * NCH * LRU_ALL)
                pool.wait_ge(ab_mm, 1)
            else:
                pool.wait_ge(fold_lo_done, f)
            for s in range(2):
                h, o, fo = SEQS[s] // 2, OFFS[s], HOFF[s]
                u = u_f[f]
                mirror = u[:, o + 2 * h - 1:o + h:-1]
                pool.tensor_tensor(fold[:, 0, fo + 1:fo + h], u[:, o + 1:o + h], mirror, ALU.add)
                pool.tensor_tensor(fold[:, 1, fo + 1:fo + h], u[:, o + 1:o + h], mirror, ALU.subtract)
                pool.tensor_copy(fold[:, 0, fo:fo + 1], u[:, o:o + 1])
                m = pool.memset(fold[:, 1, fo:fo + 1], 0.0)
            m.then_inc(fold_done, 1)

        def fold_split_lo(f):
            pool.wait_ge(fold_hi_done, f + 1)
            pool.tensor_tensor(fold_lo[:].rearrange("p t n -> p (t n)"), fold[:].rearrange("p t n -> p (t n)"),
                               fold_hi[:].rearrange("p t n -> p (t n)"), ALU.subtract).then_inc(fold_lo_done, 1)

        make_fold(0)
        fold_split_lo(0)
        for f in range(FT):
            for c in range(NCH):
                pool.wait_ge(mixr_hi, f * NCH + c + 1)
                pool.tensor_tensor(lo_r[:, c, f, :], yr[:, f, c * CH:(c + 1) * CH], hi_r[:, c, f, :],
                                   ALU.subtract).then_inc(mixr_lo, 1)
            if f == 0:
                make_fold(1)
        for f in range(1, FT):
            fold_split_lo(f)
            if f + 1 < FT:
                make_fold(f + 1)
        for q in range(16):
            pool.wait_ge(wo_hi_done, q + 1)
            pool.tensor_tensor(wo_lo[q][:].rearrange("p k m -> p (k m)"), wo_raw[q % 2][:],
                               wo_hi[q][:].rearrange("p k m -> p (k m)"), ALU.subtract).then_inc(wo_lo_done, 1)

        def split_w(b, which):
            dst, src, hi_done, done = ((w1_lo, w1_hi, w1_hi_done, w1_lo_done),
                                       (w2_lo, w2_hi, w2_hi_done, w2_lo_done))[which]
            dst = dst[:].rearrange("p a m -> p (a m)")
            src = src[:].rearrange("p a m -> p (a m)")
            for i in range(4):
                cols = slice(i * CH, (i + 1) * CH)
                pool.wait_ge(hi_done, 4 * b + i + 1)
                m = pool.tensor_tensor(dst[:, cols], w12_raw[:, cols], src[:, cols], ALU.subtract)
            m.then_inc(done, 1)

        split_w(0, 0)
        split_w(0, 1)
        with pool.Fori(1, NB) as b:
            split_w(b, 0)
            split_w(b, 1)

    ctx.close()


def kernel(**inputs):
    import concourse.bacc as bacc
    from concourse.bass_utils import run_bass_kernel_spmd as run

    a = {k: np.asarray(v) for k, v in inputs.items()}

    def columns(v):
        return np.ascontiguousarray(np.asarray(v).reshape(-1, P).T)

    vec = np.concatenate([columns(v) for v in (
        a["c_prompt"], a["c_sample"], a["b_mod"], a["g_mix"], a["g_mlp"], a["g_final"], a["conv_w"],
        a["conv_b"], a["b_rgate"], a["b_igate"], a["lru_lambda"])], axis=1)

    def block_diagonal(w):
        lead = w.shape[:-3]
        out = np.zeros(lead + (w.shape[-3] // 2, P, P), w.dtype)
        out[..., :HEAD, :HEAD] = w[..., 0::2, :, :]
        out[..., HEAD:, HEAD:] = w[..., 1::2, :, :]
        return out

    xT = np.concatenate([a["x_prompt"][0].T, a["x_sample"][0].T], axis=1)
    w_in = a["w_in"][0].reshape(KD, P, NTILE, P).transpose(2, 1, 0, 3).reshape(NTILE, P, KD * P)
    gates = np.stack([block_diagonal(a["w_rgate"][0]), block_diagonal(a["w_igate"][0])], axis=1)
    w_gate = gates.transpose(2, 3, 0, 1, 4).reshape(FT, P, 4 * P)
    w_four = block_diagonal(a["w_fourier"][0]).transpose(1, 0, 2).reshape(P, FT * P)
    w_out = a["w_out"][0].reshape(KD, P, KD, P).transpose(2, 1, 0, 3).reshape(KD, P, KD * P)
    w_ff1 = a["w_ff1"][0].reshape(KD, P, NB, FB).transpose(2, 1, 0, 3).reshape(NB, P, KD * FB)
    w_ff2 = a["w_ff2"][0].reshape(NB, JB, P, D).transpose(0, 2, 1, 3).reshape(NB, P, JB * D)
    th = 2 * np.pi * (np.outer(np.arange(HEAD), np.arange(HEAD)) % HEAD) / HEAD
    dft_head = np.zeros((P, 2, P))
    for t, m in enumerate((np.cos(th), np.sin(th))):
        for h in range(2):
            dft_head[h * HEAD:(h + 1) * HEAD, t, h * HEAD:(h + 1) * HEAD] = m * HEAD ** -0.5
    ts = 2 * np.pi * (np.outer(np.arange(512), np.arange(CH)) % 1024) / 1024
    dft_seq = np.stack([np.cos(ts), np.sin(ts)]).reshape(2 * 4, P, CH).transpose(1, 0, 2)

    arrays, args = {}, {}
    nc = bacc.Bacc("TRN2", target_bir_lowering=False, num_devices=1, dynamic_dma_scratch_size=1024)
    for name, v in (("vec", vec), ("xT", xT), ("w_mod", a["w_mod"][0]), ("w_in", w_in), ("w_gate", w_gate),
                    ("w_four", w_four), ("w_out", w_out), ("w_ff1", w_ff1), ("w_ff2", w_ff2),
                    ("dft_head", dft_head.astype(np.float32)), ("dft_seq", dft_seq.astype(np.float32))):
        v = np.ascontiguousarray(v)
        arrays[f"in_{name}"] = v
        args[f"{name}_d"] = nc.dram_tensor(f"in_{name}", v.shape, mybir.dt.from_np(v.dtype),
                                           kind="ExternalInput").ap()
    args["yT_d"] = nc.dram_tensor("out_yT", (D, T), F32, kind="ExternalOutput").ap()
    build_encoder(nc, **args)
    r = run(nc, [arrays], core_ids=[0])
    yT = r.results[0]["out_yT"]
    return (np.ascontiguousarray(yT[:, :SEQS[0]].T)[None], np.ascontiguousarray(yT[:, SEQS[0]:].T)[None])
```

```python
from contextlib import ExitStack

import numpy as np

import concourse.bass as bass
from concourse import mybir

F32 = mybir.dt.float32
F32R = mybir.dt.float32r
ALU = mybir.AluOpType
ACT = mybir.ActivationFunctionType
AX = mybir.AxisListType

P = 128
CH = 512
SEQS = (1024, 512)
OFFS = (0, 1024)
T = sum(SEQS)
NCH = T // CH
SEQ_OF = (0, 0, 1)
D = 1024
KD = D // P
DF = 512
FT = DF // P
HEAD = 64
DFF = 4096
FB = 256
NB = DFF // FB
JB = FB // P
EPS = 1e-6
LRU_C = 8.0
NMOD = 6
NTILE = 3 * FT
TILES = [FT + j // 2 if j % 2 == 0 else 2 * FT + j // 2 for j in range(2 * FT)] + list(range(FT))
PADL, PADR = 2, 1
UPAD = (0, PADL + SEQS[0] + PADR)
UPADW = UPAD[1] + PADL + SEQS[1] + PADR

V_C = 0
V_BMOD = V_C + 2 * KD
V_GMIX = V_BMOD + NMOD * KD
V_GMLP = V_GMIX + KD
V_GFIN = V_GMLP + KD
V_CONVW = V_GFIN + KD
V_CONVB = V_CONVW + 4 * FT
V_BR = V_CONVB + FT
V_BI = V_BR + 2 * FT
V_LAM = V_BI + 2 * FT
NV = V_LAM + 2 * FT
SHIFT1, SCALE1, GATE1, SHIFT2, SCALE2, GATE2 = range(NMOD)


def build_encoder(nc, vec_d, xT_d, w_mod_d, w_in_d, w_gate_d, w_four_d, w_out_d, w_ff1_d, w_ff2_d,
                  dft_head_d, dft_seq_d, yT_d):
    ctx = ExitStack()

    def sem(name):
        return ctx.enter_context(nc.semaphore(name))

    base = (nc.sbuf_base + 31) // 32 * 32
    at = {}

    def place(name, shape, dtype, offset):
        at[name] = offset
        return nc.alloc_sbuf_tensor_at(name, shape, dtype, offset=offset)

    cur = [base]

    def fixed(name, shape, dtype=F32):
        t = place(name, shape, dtype, cur[0])
        cur[0] += (4 * int(np.prod(shape[1:])) + 31) // 32 * 32
        return t

    vec = fixed("vec", [P, NV])
    ones = fixed("ones", [P, P])
    ident = fixed("ident", [P, P])
    dft_head = fixed("dft_head", [P, 2, P])
    c_sig = fixed("c_sig", [P, 2 * KD])
    c_silu = fixed("c_silu", [P, KD, 32])
    mod = fixed("mod", [P, NMOD, KD, 2])
    amp1 = fixed("amp1", [P, KD, 2])
    amp2 = fixed("amp2", [P, KD, 2])
    eps = fixed("eps", [P, 1])
    decay = fixed("decay", [P, 2, 2 * FT])
    sp = fixed("sp", [P, 6, 2 * FT])
    edge = fixed("edge", [P, FT, 4])
    alt = fixed("alt", [P, 2, 2])
    bias_e = fixed("bias_e", [P, FT, 2, 2])
    A0 = cur[0]
    QT = 4 * T
    HALF = FT * QT
    hi_f = place("hi_f", [P, NCH, FT, CH], F32R, A0)
    lo_f = place("lo_f", [P, NCH, FT, CH], F32R, A0 + HALF)
    hi_r = place("hi_r", [P, NCH, FT, CH], F32R, A0 + 2 * HALF)
    lo_r = place("lo_r", [P, NCH, FT, CH], F32R, A0 + 3 * HALF)
    X0 = A0 + 4 * HALF
    W0 = X0 + 2 * HALF
    x = place("x", [P, NCH, KD, CH], F32, X0)

    def hi(c, k):
        return (hi_f, hi_r)[k // FT][:, c, k % FT, :]

    def lo(c, k):
        return (lo_f, lo_r)[k // FT][:, c, k % FT, :]

    rr = place("rr", [P, T], F32, X0)
    ii = place("ii", [P, T], F32, X0 + QT)
    aa = place("aa", [P, T], F32, X0 + 2 * QT)
    qq = place("qq", [P, T], F32, X0 + 3 * QT)
    uc = place("uc", [P, T], F32, X0 + 4 * QT)
    hf = place("hf", [P, T], F32, X0 + 5 * QT)
    uc_hi = place("uc_hi", [P, T], F32R, X0 + 6 * QT)
    uc_lo = place("uc_lo", [P, T], F32R, X0 + 7 * QT)
    yr = place("yr", [P, FT, T], F32, W0)
    u_pad = place("u_pad", [P, UPADW], F32, W0 + HALF)
    s0 = W0 + HALF + (4 * UPADW + 31) // 32 * 32
    mod_raw = place("mod_raw", [P, 2, 2048], F32, s0)
    ab_hi = place("ab_hi", [P, 2, FT, P], F32R, s0)
    ab_lo = place("ab_lo", [P, 2, FT, P], F32R, s0 + 4096)
    a_f32 = place("a_f32", [P, FT, P], F32, s0 + 8192)
    mod_row = place("mod_row", [P, CH], F32, s0 + 16384)
    s1 = s0 + 16384 + 2048
    win_hi = [place(f"win_hi{i}", [P, KD, P], F32R, s1 + 8192 * i) for i in range(2)]
    win_lo = [place(f"win_lo{i}", [P, KD, P], F32R, s1 + 8192 * i + 4096) for i in range(2)]
    s2 = s1 + 16384
    win_raw = place("win_raw", [P, KD * P], F32, s2)
    s3 = s2 + 4096
    wg_hi = place("wg_hi", [P, 4, P], F32R, s3)
    wg_lo = place("wg_lo", [P, 4, P], F32R, s3 + 2048)
    wg_raw = place("wg_raw", [P, 4 * P], F32, s3 + 4096)
    assert s3 + 6144 <= nc.sbuf_usable_end
    n1_sq = [place(f"n1_sq{i}", [P, CH], F32, W0 + 2048 * i) for i in range(2)]
    n1_acc = place("n1_acc", [P, CH], F32, W0 + 4096)
    n1_rstd = place("n1_rstd", [P, CH], F32, W0 + 6144)
    wf_raw = place("wf_raw", [P, FT * P], F32, s3 + 4096)
    u_f = [place("u_f0", [P, T], F32, s0 + 10240), place("u_f1", [P, T], F32, W0 + HALF),
           place("u_f2", [P, T], F32, X0 + 6 * QT), place("u_f3", [P, T], F32, X0 + 7 * QT)]
    HT = T // 2
    HOFF = (0, SEQS[0] // 2)
    fold = [place(f"fold{f}", [P, 2, HT], F32, o) for f, o in enumerate((s3, X0 + 3 * QT, s3, s0 + 10240))]
    fold_at = (X0 + 4 * QT, A0 + 32768)
    fold_hi = [place(f"fold_hi{i}", [P, 2, HT], F32R, o) for i, o in enumerate(fold_at)]
    fold_lo = [place(f"fold_lo{i}", [P, 2, HT], F32R, o + QT) for i, o in enumerate(fold_at)]
    tab_hi = place("tab_hi", [P, 2, 4, CH], F32R, A0)
    tab_lo = place("tab_lo", [P, 2, 4, CH], F32R, A0 + 16384)
    tab_raw = place("tab_raw", [P, 8, CH], F32, X0)
    pq_at = (s1, W0 + 12288)
    pq_hi = [place(f"pq_hi{i}", [P, 3, CH], F32R, o) for i, o in enumerate(pq_at)]
    pq_lo = [place(f"pq_lo{i}", [P, 3, CH], F32R, o + 6144) for i, o in enumerate(pq_at)]
    e_sb = [place(f"e_sb{i}", [P, CH], F32, s2 + 2048 * i) for i in range(2)]
    yf = place("yf", [P, FT, T], F32, X0)
    WO_ORDER = (0, 1, 2, 4, 5, 3, 11, 6, 7, 12, 13, 14, 15, 8, 9, 10)
    wo_slot = dict(zip(WO_ORDER, (0, 1, 2, 6, 7, 8, 9, 10, 11, 12, 13, 14, 15, 3, 4, 5)))
    wo_at = [W0 + 4096 * wo_slot[q] for q in range(16)]
    wo_hi = [place(f"wo_hi{q}", [P, FT, P], F32R, o) for q, o in enumerate(wo_at)]
    wo_lo = [place(f"wo_lo{q}", [P, FT, P], F32R, o + 2048) for q, o in enumerate(wo_at)]
    wo_raw = [place(f"wo_raw{i}", [P, FT * P], F32, s3 + 2048 * i) for i in range(3)]
    tmp = [place(f"tmp{i}", [P, CH], F32, s3 + 2048 * i) for i in range(3)]
    assert s2 >= W0 + 65536
    n_sq = [place("n_sq", [P, CH], F32, s2), tmp[2]]
    n_acc = place("n_acc", [P, CH], F32, s2 + 2048)
    w1_hi = place("w1_hi", [P, KD, FB], F32R, W0)
    w1_lo = place("w1_lo", [P, KD, FB], F32R, W0 + 8192)
    w2_hi = place("w2_hi", [P, JB, D], F32R, W0 + 16384)
    w2_lo = place("w2_lo", [P, JB, D], F32R, W0 + 24576)
    w12_raw = place("w12_raw", [P, KD * FB], F32, W0 + 32768)
    hid_hi = place("hid_hi", [P, NCH, JB, CH], F32R, W0 + 40960)
    hid_lo = place("hid_lo", [P, NCH, JB, CH], F32R, W0 + 40960 + 12288)

    bank = [ctx.enter_context(nc.psum_tensor(f"bank{i}", [P, CH], F32)) for i in range(8)]
    GB, MB, NBK = (4, 5, 7), 6, 7

    ld_vec, ld_dft, ld_win, ld_wg, ld_wf, ld_tab, ld_w12 = map(
        sem, ("ld_vec", "ld_dft", "ld_win", "ld_wg", "ld_wf", "ld_tab", "ld_w12"))
    ld_x = [sem(f"ld_x{c}") for c in range(NCH)]
    ld_mod = [sem(f"ld_mod{i}") for i in range(2)]
    ld_wo = [sem(f"ld_wo{i}") for i in range(3)]
    st_y = [sem(f"st_y{i}") for i in range(2)]
    const_set = sem("const_set")
    sig_c = sem("sig_c")
    silu_c = sem("silu_c")
    lam_exp = sem("lam_exp")
    lam_abs = sem("lam_abs")
    decay_set = sem("decay_set")
    dve_own = sem("dve_own")
    pool_own = sem("pool_own")
    sq_done = sem("sq_done")
    sq_read = sem("sq_read")
    amp_set = sem("amp_set")
    lru_ix = sem("lru_ix")
    acc_done = sem("acc_done")
    norm_mm = sem("norm_mm")
    sd_done = sem("sd_done")
    rstd_done = sem("rstd_done")
    xn_done = sem("xn_done")
    h_done = sem("h_done")
    hhi_done = sem("hhi_done")
    hlo_done = sem("hlo_done")
    mod_mm = sem("mod_mm")
    mod_rows = sem("mod_rows")
    mod_tr = sem("mod_tr")
    mod_cols = sem("mod_cols")
    win_hi_done, win_lo_done = sem("win_hi_done"), sem("win_lo_done")
    wg_hi_done, wg_lo_done = sem("wg_hi_done"), sem("wg_lo_done")
    in_mm = sem("in_mm")
    in_evac = sem("in_evac")
    conv_done = sem("conv_done")
    gate_mm = sem("gate_mm")
    gate_sig = sem("gate_sig")
    lru_a, lru_t, lru_q = sem("lru_a"), sem("lru_t"), sem("lru_q")
    lru_m2 = sem("lru_m2")
    lru_m = sem("lru_m")
    lru_scan = sem("lru_scan")
    lru_done = sem("lru_done")
    ab_mm, ab_act, ab_set = sem("ab_mm"), sem("ab_act"), sem("ab_set")
    fold_done = sem("fold_done")
    fold_hi_done, fold_lo_done = sem("fold_hi_done"), sem("fold_lo_done")
    edge_done = sem("edge_done")
    pq_mm = sem("pq_mm")
    edge_mm = sem("edge_mm")
    pq_hi_done, pq_lo_done = sem("pq_hi_done"), sem("pq_lo_done")
    bias_done = sem("bias_done")
    yf_edge = sem("yf_edge")
    eo_mm = sem("eo_mm")
    e_done = sem("e_done")
    eo_done = sem("eo_done")
    tab_hi_done, tab_lo_done = sem("tab_hi_done"), sem("tab_lo_done")
    mixr_hi, mixr_lo = sem("mixr_hi"), sem("mixr_lo")
    mixf_hi, mixf_lo = sem("mixf_hi"), sem("mixf_lo")
    wo_hi_done, wo_lo_done = sem("wo_hi_done"), sem("wo_lo_done")
    out_mm = sem("out_mm")
    out_evac = sem("out_evac")
    w1_hi_done, w1_lo_done = sem("w1_hi_done"), sem("w1_lo_done")
    w2_hi_done, w2_lo_done = sem("w2_hi_done"), sem("w2_lo_done")
    ff1_mm, ff1_relu = sem("ff1_mm"), sem("ff1_relu")
    ff1_sq = sem("ff1_sq")
    hid_hi_done, hid_lo_done = sem("hid_hi_done"), sem("hid_lo_done")
    ff2_mm, ff2_evac = sem("ff2_mm"), sem("ff2_evac")
    y_done = sem("y_done")

    def after(eng, s, value):
        if not isinstance(value, int) or value > 0:
            eng.wait_ge(s, value)

    NLOAD = NCH * KD

    def gates_after(j, c):
        f, r = divmod(NCH * j + c - (2 * NCH - 1), 2 * NCH)
        return (2 * f + r // 2, r % 2) if 0 <= f < FT and r < 4 else None

    def mod_steps_after(j):
        return range(KD + 2 * j, KD + 2 * j + 2) if j < KD else ()

    LRU_ALL = 2 * FT
    MIX_ORDER = (2, 3, 0, 1)
    MOD_AFTER = {(5, 0): 1, (9, 1): 2}
    AB_AFTER = 2 * FT + 1
    block = ctx.enter_context(nc.Block())

    @block.sync
    def _(sp):
        sp.dma_start(vec[:], vec_d).then_inc(ld_vec, 16)
        for c in range(NCH):
            sp.dma_start(x[:, c, :, :], xT_d[:, c * CH:(c + 1) * CH].rearrange("(k p) n -> p k n", p=P)
                         ).then_inc(ld_x[c], 16)
        sp.dma_start(win_raw[:], w_in_d[TILES[0]]).then_inc(ld_win, 16)
        sp.dma_start(dft_head[:], dft_head_d).then_inc(ld_dft, 16)

        def load_mod(s):
            r, k = divmod(s, KD)
            after(sp, mod_mm, s - 1)
            sp.dma_start(mod_raw[:, s % 2, :], w_mod_d[k * P:(k + 1) * P, r * 2048:(r + 1) * 2048]
                         ).then_inc(ld_mod[s % 2], 16)

        for s in range(KD):
            load_mod(s)
        sp.dma_start(wg_raw[:], w_gate_d[0]).then_inc(ld_wg, 16)
        for j in range(NTILE):
            if j + 1 < NTILE:
                sp.wait_ge(win_lo_done, j + 1)
                sp.dma_start(win_raw[:], w_in_d[TILES[j + 1]]).then_inc(ld_win, 16)
            for s in mod_steps_after(j):
                load_mod(s)
            if j % 2 == 1 and j // 2 + 1 < FT:
                f = j // 2 + 1
                sp.wait_ge(wg_lo_done, f)
                sp.dma_start(wg_raw[:], w_gate_d[f]).then_inc(ld_wg, 16)
            if j == 2 * FT - 1:
                sp.wait_ge(wg_lo_done, FT)
                sp.dma_start(wf_raw[:], w_four_d).then_inc(ld_wf, 16)
        sp.wait_ge(lru_done, FT)
        sp.dma_start(tab_raw[:], dft_seq_d).then_inc(ld_tab, 16)

        def load_wo(i):
            if i < 3:
                sp.wait_ge(fold_lo_done, 3)
            else:
                sp.wait_ge(wo_lo_done, i - 2)
            half, d = divmod(WO_ORDER[i], KD)
            k0 = FT * (1 - half)
            sp.dma_start(wo_raw[i % 3][:], w_out_d[d, :, k0 * P:(k0 + FT) * P]).then_inc(ld_wo[i % 3], 16)

        for i in range(16):
            load_wo(i)
        sp.wait_ge(mixf_hi, FT * NCH)
        sp.wait_ge(mixf_lo, FT * NCH)
        for c in range(NCH):
            sp.dma_start(x[:, c, :, :], xT_d[:, c * CH:(c + 1) * CH].rearrange("(k p) n -> p k n", p=P)
                         ).then_inc(ld_x[c], 16)
        w1_src = w_ff1_d
        w2_src = w_ff2_d
        sp.wait_ge(out_mm, (NCH - 1) * KD + 4)
        sp.dma_start(w12_raw[:], w1_src[0]).then_inc(ld_w12, 16)
        sp.wait_ge(w1_lo_done, 1)
        sp.dma_start(w12_raw[:], w2_src[0]).then_inc(ld_w12, 16)
        with sp.Fori(1, NB) as b:
            sp.wait_ge(w2_lo_done, b)
            sp.dma_start(w12_raw[:], w1_src[bass.ds(b, 1), :, :].rearrange("o p n -> (o p) n")
                         ).then_inc(ld_w12, 16)
            sp.wait_ge(w1_lo_done, b + 1)
            sp.dma_start(w12_raw[:], w2_src[bass.ds(b, 1), :, :].rearrange("o p n -> (o p) n")
                         ).then_inc(ld_w12, 16)
        n_st = [0, 0]
        for c in range(NCH):
            for half in range(2):
                sp.wait_ge(y_done, c * KD + 4 * half + 4)
                rows = yT_d[half * 4 * P:(half + 1) * 4 * P, c * CH:(c + 1) * CH]
                sp.dma_start(rows.rearrange("(k p) n -> p k n", p=P), x[:, c, 4 * half:4 * half + 4, :]
                             ).then_inc(st_y[half], 16)
                n_st[half] += 16
                if c < NCH - 1:
                    sp.wait_ge(st_y[half], n_st[half])
        for half in range(2):
            sp.wait_ge(st_y[half], n_st[half])

    @block.tensor
    def _(pe):
        def three(out, w_hi, w_lo, v_hi, v_lo, first, last):
            pe.matmul(out, w_lo, v_hi, start=first, stop=False)
            pe.matmul(out, w_hi, v_lo, start=False, stop=False)
            return pe.matmul(out, w_hi, v_hi, start=False, stop=last)

        def norm_sum(n, b):
            pe.wait_ge(acc_done, 1 + n)
            if n > 0:
                pe.wait_ge(sd_done, n)
            pe.matmul(bank[b][:], ones[:], (n1_acc if n < NCH else n_acc)[:], start=True, stop=True
                      ).then_inc(norm_mm, 1)

        def mod_step(s):
            r, k = divmod(s, KD)
            if k == 0 and r > 0:
                pe.wait_ge(mod_rows, r)
            pe.wait_ge(ld_mod[s % 2], 16 * (s // 2 + 1))
            for q in range(4):
                m = pe.matmul(bank[MB][32 * q:32 * q + 32, :], c_silu[:, k, :],
                              mod_raw[:, s % 2, q * CH:(q + 1) * CH], start=(k == 0), stop=(k == KD - 1),
                              skip_group_check=True)
            m.then_inc(mod_mm, 1)

        def mod_transpose(r):
            pe.wait_ge(mod_rows, r + 1)
            pe.wait_ge(sd_done, NCH)
            after(pe, gate_sig, (0, LRU_ALL // 2, LRU_ALL)[r] * 2 * NCH)
            for b in range(4):
                m = pe.transpose(bank[NBK][:, b * P:(b + 1) * P], mod_row[:, b * P:(b + 1) * P], ident[:])
            m.then_inc(mod_tr, 1)

        def in_tile(j, c):
            n = NCH * j + c
            if n >= 4:
                pe.wait_ge(in_evac, n - 3)
            pe.wait_ge(win_lo_done, j + 1)
            for k in range(KD):
                if j == 0:
                    pe.wait_ge(hlo_done, c * KD + k + 1)
                m = three(bank[n % 4][:], win_hi[j % 2][:, k, :], win_lo[j % 2][:, k, :], hi(c, k), lo(c, k),
                          k == 0, k == KD - 1)
            m.then_inc(in_mm, 1)

        def gates(g, gate):
            f, d = divmod(g, 2)
            pe.wait_ge(wg_lo_done, f + 1)
            pe.wait_ge(conv_done, f + 1)
            pe.wait_ge(mod_cols, 1 if g < LRU_ALL // 2 else 2)
            for c in range(NCH):
                after(pe, gate_sig, (2 * g + gate - 1) * NCH + c + 1)
                cols = slice(c * CH, (c + 1) * CH)
                three(bank[GB[c]][:], wg_hi[:, 2 * d + gate, :], wg_lo[:, 2 * d + gate, :],
                      uc_hi[:, cols], uc_lo[:, cols], True, True).then_inc(gate_mm, 1)

        pe.wait_ge(const_set, 4)
        for c in range(NCH):
            norm_sum(c, NBK)
        pe.wait_ge(silu_c, 1)
        for s in range(KD):
            mod_step(s)
        mod_transpose(0)
        for j in range(NTILE):
            for c in range(NCH):
                in_tile(j, c)
                if gates_after(j, c):
                    gates(*gates_after(j, c))
                if (j, c) in MOD_AFTER:
                    mod_transpose(MOD_AFTER[j, c])
            for s in mod_steps_after(j):
                mod_step(s)
            if j == AB_AFTER:
                pe.wait_ge(ld_dft, 16)
                pe.wait_ge(ld_wf, 16)
                pe.wait_ge(gate_sig, 2 * NCH * LRU_ALL)
                for t in range(2):
                    m = pe.matmul(bank[GB[t]][:], dft_head[:, t, :], wf_raw[:], start=True, stop=True)
                m.then_inc(ab_mm, 1)

        BP, BQ, BS, BE, BO, BT = 0, 1, 2, 3, 4, 5

        def pq(f):
            if f == 0:
                pe.wait_ge(in_evac, NCH * NTILE)
                pe.wait_ge(ab_set, 1)
                pe.wait_ge(mod_cols, 3)
            else:
                pe.wait_ge(pq_lo_done, 3 * f)
            pe.wait_ge(fold_lo_done, f + 1)
            for t in range(2):
                for s in range(2):
                    for n in range(SEQS[s] // 2 // P):
                        cols = slice(HOFF[s] + n * P, HOFF[s] + (n + 1) * P)
                        out = (bank[t] if s == 0 else bank[BS])[:, (n + 2 * s * t) * P:(n + 2 * s * t + 1) * P]
                        m = three(out, fold_hi[f % 2][:, t, cols], fold_lo[f % 2][:, t, cols],
                                  ab_hi[:, t, f, :], ab_lo[:, t, f, :], True, True)
                m.then_inc(pq_mm, 1)

        def edge_products():
            pe.wait_ge(edge_done, FT)
            for f in range(FT):
                m = pe.matmul(bank[NBK][:, 4 * f:4 * f + 4], a_f32[:, f, :], edge[:, f, :], start=True, stop=True)
            m.then_inc(edge_mm, 1)

        def eo(f):
            b = f % 2
            pe.wait_ge(pq_lo_done, 3 * f + 3)
            pe.wait_ge(tab_lo_done, 8)
            if f == 0:
                pe.wait_ge(ab_set, 1)
            for t in range(2):
                if f > 0:
                    pe.wait_ge(eo_done, 3 * (f - 1) + 1)
                for n in range(4):
                    m = three(bank[BE + t][:], pq_hi[b][:, t, n * P:(n + 1) * P], pq_lo[b][:, t, n * P:(n + 1) * P],
                              tab_hi[:, t, n, :], tab_lo[:, t, n, :], n == 0, n == 3)
            m.then_inc(eo_mm, 1)
            if f > 0:
                pe.wait_ge(eo_done, 3 * f)
            for t in range(2):
                for n in range(2):
                    w = slice((2 * t + n) * P, (2 * t + n + 1) * P)
                    m = three(bank[BT][:, t * 256:(t + 1) * 256], pq_hi[b][:, 2, w], pq_lo[b][:, 2, w],
                              tab_hi[:, t, n, ::2], tab_lo[:, t, n, ::2], n == 0, n == 1)
            m.then_inc(eo_mm, 1)

        pq(0)
        for f in range(FT):
            if f + 1 < FT:
                pq(f + 1)
            if f == 0:
                edge_products()
            eo(f)

        def out_half(c, d, half, b, first, last):
            for kk in range(FT):
                k = FT * (1 - half) + kk
                q = half * KD + d
                m = three(bank[b][:], wo_hi[q][:, kk, :], wo_lo[q][:, kk, :], hi(c, k), lo(c, k),
                          first and kk == 0, last and kk == FT - 1)
            return m

        pe.wait_ge(mixr_lo, FT * NCH)
        for d in range(KD):
            if d == BE:
                pe.wait_ge(eo_done, 3 * FT)
            if d == NBK:
                pe.wait_ge(yf_edge, 1)
            pe.wait_ge(wo_lo_done, WO_ORDER.index(d) + 1)
            out_half(0, d, 0, d, True, False)
        for d in range(KD):
            pe.wait_ge(wo_lo_done, WO_ORDER.index(KD + d) + 1)
            pe.wait_ge(mixf_lo, FT)
            out_half(0, d, 1, d, False, True).then_inc(out_mm, 1)
        pe.wait_ge(mixf_lo, FT * NCH)
        for c in range(1, NCH):
            for d in range(KD):
                n = (c - 1) * KD + d
                pe.wait_ge(out_evac, n % 6 + 1 if n < 6 else KD + n - 5)
                out_half(c, d, 0, n % 6, True, False)
                out_half(c, d, 1, n % 6, False, True).then_inc(out_mm, 1)
                if d == 3:
                    if c == 1:
                        pe.wait_ge(out_evac, KD)
                    norm_sum(NCH + c - 1, NBK)
        pe.wait_ge(out_evac, NCH * KD)

        def mlp_block(b, middle=None):
            pe.wait_ge(w1_lo_done, b + 1)
            for c in range(NCH):
                if isinstance(b, int) and b == 0:
                    pe.wait_ge(hlo_done, NLOAD + (c + 1) * KD)
                for j in range(JB):
                    n = JB * c + j
                    after(pe, ff1_relu, JB * NCH * b + n - 2)
                    for k in range(KD):
                        w = slice(j * P, (j + 1) * P)
                        m = three(bank[n % 3][:], w1_hi[:, k, w], w1_lo[:, k, w], hi(c, k), lo(c, k),
                                  k == 0, k == KD - 1)
                    m.then_inc(ff1_mm, 1)
                if middle == "norm2" and c == 0:
                    norm_sum(2 * NCH - 1, NBK)
            pe.wait_ge(w2_lo_done, b + 1)
            for c in range(NCH):
                pe.wait_ge(hid_lo_done, JB * NCH * b + JB * (c + 1))
                for d in range(KD):
                    n = KD * c + d
                    after(pe, ff2_evac, NCH * KD * b + n - 3)
                    w = slice(d * P, (d + 1) * P)
                    for j in range(JB):
                        m = three(bank[3 + n % 4][:], w2_hi[:, j, w], w2_lo[:, j, w],
                                  hid_hi[:, c, j, :], hid_lo[:, c, j, :], j == 0, j == JB - 1)
                    m.then_inc(ff2_mm, 1)
                if middle == "norm3" and c > 0:
                    norm_sum(2 * NCH + c - 1, NBK)

        mlp_block(0, "norm2")
        with pe.Fori(1, NB - 1) as b:
            mlp_block(b)
        mlp_block(NB - 1, "norm3")
        norm_sum(3 * NCH - 1, NBK)

    @block.scalar
    def _(act):
        def squares(n, c):
            first = n < NCH
            for k in range(KD):
                m = n * KD + k
                if first:
                    if k == 0:
                        act.wait_ge(ld_x[c], 16)
                        after(act, norm_mm, n)
                    dst = n1_acc if k == 0 else n1_sq[k % 2]
                else:
                    if n < 2 * NCH:
                        act.wait_ge(out_evac, c * KD + k + 1)
                    else:
                        act.wait_ge(ff2_evac, (NB - 1) * NCH * KD + c * KD + k + 1)
                    if k == 0:
                        act.wait_ge(norm_mm, n)
                        if n == NCH:
                            act.wait_ge(wo_lo_done, 16)
                        else:
                            if n <= 2 * NCH:
                                act.wait_ge(hlo_done, (n - NCH + NCH) * KD)
                            else:
                                act.wait_ge(y_done, (n - 2 * NCH) * KD)
                    dst = n_acc if k == 0 else n_sq[k % 2]
                if first and k == 2:
                    after(act, rstd_done, n)
                if k > 2:
                    act.wait_ge(sq_read, n * (KD - 1) + k - 2)
                act.activation(dst[:], x[:, c, k, :], ACT.Square).then_inc(sq_done, 1)

        def root(n):
            act.wait_ge(norm_mm, n + 1)
            act.wait_ge(sq_read, (n + 1) * (KD - 1))
            dst = n1_sq[0] if n < NCH else n_sq[0]
            act.activation(dst[:], bank[NBK][:], ACT.Sqrt, bias=eps[:], scale=1.0 / D).then_inc(sd_done, 1)

        def split_win_hi(j):
            act.wait_ge(ld_win, 16 * (j + 1))
            if j >= 2:
                act.wait_ge(in_mm, NCH * (j - 1))
            act.activation(win_hi[j % 2][:].rearrange("p k m -> p (k m)"), win_raw[:], ACT.Copy
                           ).then_inc(win_hi_done, 1)

        def split_wg_hi(f):
            act.wait_ge(ld_wg, 16 * (f + 1))
            after(act, gate_mm, 4 * NCH * f)
            act.activation(wg_hi[:].rearrange("p g m -> p (g m)"), wg_raw[:], ACT.Copy).then_inc(wg_hi_done, 1)

        act.wait_ge(ld_vec, 16)
        act.activation(c_sig[:], vec[:, V_C:V_C + 2 * KD], ACT.Sigmoid).then_inc(sig_c, 1)
        act.wait_ge(lam_abs, 1)
        act.activation(sp[:, 1, :], sp[:, 0, :], ACT.Exp, scale=-1.0).then_inc(lam_exp, 1)
        act.wait_ge(const_set, 4)
        for c in range(NCH):
            squares(c, c)
            root(c)
        split_win_hi(0)

        def mod_copy(r):
            act.wait_ge(mod_mm, KD * (r + 1))
            if r > 0:
                act.wait_ge(mod_tr, r)
            act.activation(mod_row[:], bank[MB][:], ACT.Copy).then_inc(mod_rows, 1)

        mod_copy(0)
        act.wait_ge(mod_cols, 1)
        act.wait_ge(amp_set, 1)
        for c in range(NCH):
            s = SEQ_OF[c]
            for k in range(KD):
                n = c * KD + k
                act.wait_ge(xn_done, n + 1)
                act.activation(x[:, c, k, :], x[:, c, k, :], ACT.Identity, bias=mod[:, SHIFT1, k, s:s + 1],
                               scale=amp1[:, k, s:s + 1]).then_inc(h_done, 1)
                act.wait_ge(h_done, n + 1)
                act.activation(hi(c, k), x[:, c, k, :], ACT.Copy).then_inc(hhi_done, 1)
        split_win_hi(1)
        act.wait_ge(hlo_done, NLOAD)
        split_wg_hi(0)

        def evac_in(j):
            for c in range(NCH):
                n = NCH * j + c
                act.wait_ge(in_mm, n + 1)
                src = bank[n % 4][:]
                cols = slice(c * CH, (c + 1) * CH)
                if j < 2 * FT and j % 2 == 0:
                    s = SEQ_OF[c]
                    after(act, conv_done, j // 2)
                    o = UPAD[s] + PADL + c * CH - OFFS[s]
                    act.activation(u_pad[:, o:o + CH], src, ACT.Copy).then_inc(in_evac, 1)
                elif j < 2 * FT:
                    act.activation(yr[:, j // 2, cols], src, ACT.Gelu_apprx_tanh).then_inc(in_evac, 1)
                else:
                    f = j - 2 * FT
                    if f == 0:
                        act.wait_ge(mod_mm, 3 * KD)
                    if f == 1:
                        act.wait_ge(conv_done, FT)
                    if f > 1:
                        act.wait_ge(gate_mm, 2 * NCH * LRU_ALL)
                    act.activation(u_f[f][:, cols], src, ACT.Copy).then_inc(in_evac, 1)
                if c == 1 and 0 < j < NTILE - 1:
                    split_win_hi(j + 1)
                if gates_after(j, c):
                    g, gate = gates_after(j, c)
                    gate_sigmoids(g, gate)
                    if gate == 1:
                        lru_coefficients(g)
                        if g % 2 == 0:
                            lru_sqrt(g)
                        elif g // 2 + 1 < FT:
                            split_wg_hi(g // 2 + 1)
                elif n >= 2 * NCH and gates_after(*divmod(n - 1, NCH)):
                    lru_sqrt(gates_after(*divmod(n - 1, NCH))[0])
                if (j, c) in ((4, 0), (8, 0)):
                    mod_copy(j // 4)

        def gate_sigmoids(g, gate):
            f, d = divmod(g, 2)
            dst, col = ((rr, V_BR), (ii, V_BI))[gate]
            after(act, (lru_m2, lru_scan)[gate], g)
            for c in range(NCH):
                act.wait_ge(gate_mm, (2 * g + gate) * NCH + c + 1)
                b = vec[:, col + d * FT + f:col + d * FT + f + 1]
                act.activation(dst[:, c * CH:(c + 1) * CH], bank[GB[c]][:], ACT.Sigmoid, bias=b
                               ).then_inc(gate_sig, 1)

        def lru_coefficients(g):
            f, d = divmod(g, 2)
            act.wait_ge(gate_sig, (2 * g + 1) * NCH)
            act.wait_ge(decay_set, 1)
            w = d * FT + f
            act.activation(aa[:], rr[:], ACT.Exp, scale=decay[:, 0, w:w + 1]).then_inc(lru_a, 1)
            act.wait_ge(lru_a, g + 1)
            act.activation(rr[:], rr[:], ACT.Tanh, scale=decay[:, 1, w:w + 1]).then_inc(lru_t, 1)
            after(act, lru_done, f)
            act.activation(qq[:], aa[:], ACT.Square).then_inc(lru_q, 1)

        def lru_sqrt(g):
            act.wait_ge(lru_m2, g + 1)
            act.activation(qq[:], qq[:], ACT.Sqrt).then_inc(lru_m, 1)

        def fold_split_hi(f):
            act.wait_ge(fold_done, f + 1)
            if f > 1:
                act.wait_ge(pq_mm, 2 * (f - 1))
            elif f == 1:
                act.wait_ge(in_mm, NCH * NTILE)
            else:
                act.wait_ge(lru_done, FT)
            act.activation(fold_hi[f % 2][:].rearrange("p t n -> p (t n)"),
                           fold[f][:].rearrange("p t n -> p (t n)"), ACT.Copy).then_inc(fold_hi_done, 1)

        for j in range(NTILE):
            evac_in(j)
            if j == NTILE - 2:
                fold_split_hi(0)
            if j == AB_AFTER:
                act.wait_ge(ab_mm, 1)
                act.activation(a_f32[:].rearrange("p f m -> p (f m)"), bank[GB[0]][:], ACT.Copy)
                act.activation(ab_hi[:, 0].rearrange("p f m -> p (f m)"), bank[GB[0]][:], ACT.Copy)
                act.activation(ab_hi[:, 1].rearrange("p f m -> p (f m)"), bank[GB[1]][:], ACT.Copy
                               ).then_inc(ab_act, 1)

        def split_wo_hi(i):
            act.wait_ge(ld_wo[i % 3], 16 * (i // 3 + 1))
            if i == 0:
                act.wait_ge(mixr_lo, FT * NCH)
                act.wait_ge(fold_done, 2)
            elif i == 4:
                act.wait_ge(pq_mm, 2 * FT)
                act.wait_ge(fold_lo_done, FT)
            elif i == 9:
                act.wait_ge(eo_mm, 2 * (FT - 1))
            elif i == 13:
                act.wait_ge(eo_mm, 2 * FT)
            act.activation(wo_hi[WO_ORDER[i]][:].rearrange("p k m -> p (k m)"), wo_raw[i % 3][:], ACT.Copy
                           ).then_inc(wo_hi_done, 1)

        def pq_split_hi(f):
            b = f % 2
            if f == 0:
                act.wait_ge(in_mm, NCH * NTILE)
            elif f == 1:
                act.wait_ge(mixr_lo, FT * NCH // 2)
            else:
                act.wait_ge(eo_mm, 2 * (f - 1))
            act.wait_ge(pq_mm, 2 * f + 2)
            for i in range(3):
                act.activation(pq_hi[b][:, i, :], bank[i][:], ACT.Copy,
                               scale=SEQS[0 if i < 2 else 1] ** -0.5).then_inc(pq_hi_done, 1)

        def edge_out():
            act.wait_ge(edge_mm, 1)
            src = bank[NBK][:, 0:4 * FT].rearrange("p (f e) -> p f e", e=4)
            for s in range(2):
                for sign in range(2):
                    m = act.activation(bias_e[:, :, s, sign], src[:, :, 2 * s], ACT.Copy,
                                       scale=SEQS[s] ** -0.5 * (1 - 2 * sign))
            m.then_inc(bias_done, 1)
            act.wait_ge(tab_lo_done, 8)
            for s in range(2):
                m = act.activation(yf[:, :, OFFS[s] + SEQS[s] // 2], src[:, :, 2 * s + 1], ACT.Copy,
                                   scale=SEQS[s] ** -0.5)
            m.then_inc(yf_edge, 1)

        def copy_e(f):
            act.wait_ge(bias_done, 1)
            for s in range(2):
                act.wait_ge(eo_mm, 2 * f + s + 1)
                after(act, eo_done, 3 * (f - 1) + 1 + 2 * s)
                src = bank[3][:] if s == 0 else bank[5][:, 0:256]
                h = SEQS[s] // 2
                for sign in range(2):
                    act.activation(e_sb[s][:, sign:h:2], src[:, sign::2], ACT.Identity,
                                   bias=bias_e[:, f, s, sign:sign + 1]).then_inc(e_done, 1)

        fold_split_hi(1)
        act.wait_ge(ld_tab, 16)
        act.wait_ge(in_mm, NCH * NTILE)
        for i in range(8):
            act.activation(tab_hi[:, i // 4, i % 4, :], tab_raw[:, i, :], ACT.Copy).then_inc(tab_hi_done, 1)
        pq_split_hi(0)
        for f in range(FT):
            if f + 2 < FT:
                fold_split_hi(f + 2)
            if f + 1 < FT:
                pq_split_hi(f + 1)
            if f == 0:
                edge_out()
            if f == FT - 1:
                for i in range(9, 13):
                    split_wo_hi(i)
            copy_e(f)
            if f in (1, 2):
                for i in range(4 * (f - 1), 4 + 5 * (f - 1)):
                    split_wo_hi(i)

        act.wait_ge(eo_done, 3 * FT)
        for c in range(NCH):
            for f in range(FT):
                act.activation(hi_f[:, c, f, :], yf[:, f, c * CH:(c + 1) * CH], ACT.Copy).then_inc(mixf_hi, 1)
        for i in range(13, 16):
            split_wo_hi(i)

        def modulate(n, c):
            s = SEQ_OF[c]
            for k in range(KD):
                m = n * KD + k
                act.wait_ge(xn_done, m + 1)
                act.activation(n_sq[k % 2][:], n_sq[k % 2][:], ACT.Identity, bias=mod[:, SHIFT2, k, s:s + 1],
                               scale=amp2[:, k, s:s + 1]).then_inc(h_done, 1)
                act.wait_ge(h_done, m + 1)
                act.activation(hi(c, k), n_sq[k % 2][:], ACT.Copy).then_inc(hhi_done, 1)

        def split_w(b, which):
            dst, done, used = ((w1_hi, w1_hi_done, None), (w2_hi, w2_hi_done, None))[which]
            act.wait_ge(ld_w12, 16 * (2 * b + which + 1))
            if isinstance(b, int) and b == 0:
                act.wait_ge(out_mm, (NCH - 1) * KD + 4 if which == 0 else NCH * KD)
            elif which == 0:
                act.wait_ge(ff1_mm, JB * NCH * b)
            else:
                act.wait_ge(ff2_mm, NCH * KD * b)
            flat = dst[:].rearrange("p a m -> p (a m)")
            for i in range(4):
                act.activation(flat[:, i * CH:(i + 1) * CH], w12_raw[:, i * CH:(i + 1) * CH], ACT.Copy
                               ).then_inc(done, 1)

        for c in range(NCH - 1):
            squares(NCH + c, c)
            root(NCH + c)
            modulate(NCH + c, c)
        split_w(0, 0)
        squares(2 * NCH - 1, NCH - 1)

        def hidden(b, c):
            for j in range(JB):
                i = JB * c + j
                n = JB * NCH * b + i
                act.wait_ge(ff1_mm, n + 1)
                after(act, hid_lo_done, n - 1)
                act.activation(tmp[j][:], bank[i % 3][:], ACT.Relu).then_inc(ff1_relu, 1)
                act.wait_ge(ff1_relu, n + 1)
                act.activation(tmp[j][:], tmp[j][:], ACT.Square).then_inc(ff1_sq, 1)
                act.wait_ge(ff1_sq, n + 1)
                act.activation(hid_hi[:, c, j, :], tmp[j][:], ACT.Copy).then_inc(hid_hi_done, 1)

        def mlp_block(b, first=False, last=False):
            hidden(b, 0)
            if first:
                root(2 * NCH - 1)
                modulate(2 * NCH - 1, NCH - 1)
            split_w(b, 1)
            hidden(b, 1)
            hidden(b, 2)
            if not last:
                split_w(b + 1, 0)

        mlp_block(0, first=True)
        with act.Fori(1, NB - 1) as b:
            mlp_block(b)
        mlp_block(NB - 1, last=True)
        for c in range(NCH):
            squares(2 * NCH + c, c)
            root(2 * NCH + c)

    @block.vector
    def _(dve):
        own = [0]

        def chain(ins):
            own[0] += 1
            ins.then_inc(dve_own, 1)
            dve.wait_ge(dve_own, own[0])

        def sum_squares(n):
            acc, sq = (n1_acc, n1_sq) if n < NCH else (n_acc, n_sq)
            for k in range(1, KD):
                dve.wait_ge(sq_done, n * KD + k + 1)
                m = dve.tensor_tensor(acc[:], acc[:], sq[k % 2][:], ALU.add).then_inc(sq_read, 1)
                dve.wait_ge(sq_read, n * (KD - 1) + k)
            dve.sem_inc(acc_done, 1)

        def rstd(n):
            dve.wait_ge(sd_done, n + 1)
            if n < NCH:
                dve.reciprocal(n1_rstd[:], n1_sq[0][:]).then_inc(rstd_done, 1)
            else:
                dve.reciprocal(n_acc[:], n_sq[0][:]).then_inc(rstd_done, 1)
            dve.wait_ge(rstd_done, n + 1)

        def amplitude(dst, g, scale):
            for s in range(2):
                m = dve.scalar_tensor_tensor(dst[:, :, s], mod[:, scale, :, s], 1.0, vec[:, g:g + KD], ALU.add,
                                             ALU.mult)
            m.then_inc(amp_set, 1)

        def mod_columns(r):
            dve.wait_ge(mod_tr, r + 1)
            src = bank[NBK][:].rearrange("p (b i h s) -> p i h b s", b=4, i=2, h=2)
            bm = vec[:, V_BMOD + 2 * r * KD:V_BMOD + 2 * (r + 1) * KD].rearrange("p (i h b) -> p i h b", i=2, h=2)
            dst = mod[:, 2 * r:2 * r + 2, :, :].rearrange("p i (h b) s -> p i h b s", h=2)
            for s in range(2):
                for i in range(2):
                    m = dve.tensor_tensor(dst[:, i, :, :, s], src[:, i, :, :, s], bm[:, i], ALU.add)
            m.then_inc(mod_cols, 1)
            dve.wait_ge(mod_cols, r + 1)

        dve.wait_ge(ld_vec, 16)
        dve.wait_ge(const_set, 4)
        lam = vec[:, V_LAM:V_LAM + 2 * FT]
        chain(dve.tensor_scalar(sp[:, 2, :], lam, -1.0, None, ALU.mult))
        chain(dve.tensor_tensor(sp[:, 0, :], lam, sp[:, 2, :], ALU.max))
        dve.sem_inc(lam_abs, 1)
        dve.wait_ge(sig_c, 1)
        for s in range(2):
            m = dve.tensor_tensor(c_silu[:, :, s], vec[:, V_C + s * KD:V_C + (s + 1) * KD],
                                  c_sig[:, s * KD:(s + 1) * KD], ALU.mult)
        m.then_inc(silu_c, 1)
        dve.wait_ge(lam_exp, 1)
        chain(dve.tensor_scalar(sp[:, 3, :], sp[:, 1, :], 2.0, None, ALU.add))
        chain(dve.reciprocal(sp[:, 4, :], sp[:, 3, :]))
        chain(dve.tensor_tensor(sp[:, 3, :], sp[:, 1, :], sp[:, 4, :], ALU.mult))
        chain(dve.tensor_tensor(sp[:, 4, :], sp[:, 3, :], sp[:, 3, :], ALU.mult))
        chain(dve.tensor_scalar(sp[:, 5, :], sp[:, 4, :], 1.0 / 19, None, ALU.mult))
        for odd in range(17, 2, -2):
            chain(dve.scalar_tensor_tensor(sp[:, 5, :], sp[:, 5, :], 1.0 / odd, sp[:, 4, :], ALU.add, ALU.mult))
        chain(dve.scalar_tensor_tensor(sp[:, 5, :], sp[:, 5, :], 1.0, sp[:, 3, :], ALU.add, ALU.mult))
        chain(dve.tensor_scalar(sp[:, 2, :], sp[:, 2, :], 0.0, None, ALU.max))
        chain(dve.scalar_tensor_tensor(sp[:, 5, :], sp[:, 5, :], 2.0, sp[:, 2, :], ALU.mult, ALU.add))
        dve.tensor_scalar(decay[:, 0, :], sp[:, 5, :], -LRU_C, None, ALU.mult)
        dve.tensor_scalar(decay[:, 1, :], sp[:, 5, :], LRU_C, None, ALU.mult).then_inc(decay_set, 1)
        for c in range(NCH):
            sum_squares(c)
            rstd(c)
            for k in range(KD):
                dve.tensor_tensor(x[:, c, k, :], x[:, c, k, :], n1_rstd[:], ALU.mult).then_inc(xn_done, 1)
            dve.wait_ge(xn_done, (c + 1) * KD)
        mod_columns(0)
        amplitude(amp1, V_GMIX, SCALE1)
        for c in range(NCH):
            for k in range(KD):
                dve.wait_ge(hhi_done, c * KD + k + 1)
                dve.tensor_tensor(lo(c, k), x[:, c, k, :], hi(c, k), ALU.subtract).then_inc(hlo_done, 1)

        def conv(f):
            dve.wait_ge(in_evac, NCH * (2 * f + 1))
            after(dve, lru_ix, 2 * f)
            after(dve, gate_mm, 4 * NCH * f)
            w = [vec[:, V_CONVW + t * FT + f:V_CONVW + t * FT + f + 1] for t in range(4)]
            b = vec[:, V_CONVB + f:V_CONVB + f + 1]
            for t in range(4):
                for s in range(2):
                    src = u_pad[:, UPAD[s] + t:UPAD[s] + t + SEQS[s]]
                    dst = uc[:, OFFS[s]:OFFS[s] + SEQS[s]]
                    if t == 0:
                        m = dve.tensor_scalar(dst, src, w[0], b, ALU.mult, ALU.add)
                    else:
                        m = dve.scalar_tensor_tensor(dst, src, w[t], dst, ALU.mult, ALU.add)
                chain(m)

        def conv_split():
            chain(dve.tensor_copy(uc_hi[:], uc[:]))
            dve.tensor_tensor(uc_lo[:], uc[:], uc_hi[:], ALU.subtract).then_inc(conv_done, 1)

        def lru_input(g):
            dve.wait_ge(gate_sig, 2 * NCH * (g + 1))
            dve.tensor_tensor(ii[:], ii[:], uc[:], ALU.mult).then_inc(lru_ix, 1)

        def lru_root(g):
            dve.wait_ge(lru_q, g + 1)
            chain(dve.scalar_tensor_tensor(qq[:], qq[:], 1.0, rr[:], ALU.add, ALU.mult))
            dve.tensor_scalar(qq[:], qq[:], 0.0, None, ALU.max).then_inc(lru_m2, 1)

        def lru_group(g):
            f, d = divmod(g, 2)
            dve.wait_ge(lru_m, g + 1)
            dve.wait_ge(lru_ix, g + 1)
            chain(dve.tensor_tensor(ii[:], ii[:], qq[:], ALU.mult))
            dst = (hf, qq)[d]
            for s in range(2):
                o, e = OFFS[s], OFFS[s] + SEQS[s]
                cols = slice(o, e) if d == 0 else slice(e - 1, o - 1 if o else None, -1)
                m = dve.tensor_tensor_scan(dst[:, cols], aa[:, cols], ii[:, cols], 0.0, ALU.mult, ALU.add)
            m.then_inc(lru_scan, 1)
            if d == 1:
                dve.wait_ge(lru_scan, g + 1)
                chain(dve.tensor_tensor(hf[:], hf[:], qq[:], ALU.add))
                dve.wait_ge(in_evac, NCH * (2 * f + 2))
                dve.tensor_tensor(yr[:, f, :], yr[:, f, :], hf[:], ALU.mult).then_inc(lru_done, 1)
                dve.wait_ge(lru_done, f + 1)

        conv(0)
        conv_split()
        for g in range(LRU_ALL):
            lru_input(g)
            following = g % 2 == 1 and g // 2 + 1 < FT
            if following:
                conv(g // 2 + 1)
            lru_root(g)
            if following:
                conv_split()
            if g == 3:
                mod_columns(1)
            lru_group(g)
        mod_columns(2)
        amplitude(amp2, V_GMLP, SCALE2)
        dve.wait_ge(ab_act, 1)
        for t in range(2):
            m = dve.tensor_tensor(ab_lo[:, t].rearrange("p f m -> p (f m)"), bank[GB[t]][:],
                                  ab_hi[:, t].rearrange("p f m -> p (f m)"), ALU.subtract)
        m.then_inc(ab_set, 1)

        def edges(f):
            dve.wait_ge(in_evac, NCH * (2 * FT + f + 1))
            for s in range(2):
                u = u_f[f][:, OFFS[s]:OFFS[s] + SEQS[s]]
                dve.tensor_copy(edge[:, f, 2 * s:2 * s + 1], u[:, SEQS[s] // 2:SEQS[s] // 2 + 1])
                m = dve.tensor_reduce(alt[:, s, :], u.rearrange("p (n t) -> p t n", t=2), AX.X, ALU.add)
            chain(m)
            for s in range(2):
                m = dve.tensor_tensor(edge[:, f, 2 * s + 1:2 * s + 2], alt[:, s, 0:1], alt[:, s, 1:2], ALU.subtract)
            m.then_inc(edge_done, 1)
            dve.wait_ge(edge_done, f + 1)

        def make_fold(f):
            if f == 0:
                dve.wait_ge(gate_mm, 2 * NCH * LRU_ALL)
                dve.wait_ge(ab_mm, 1)
            elif f == 2:
                dve.wait_ge(fold_lo_done, 1)
            elif f == 3:
                dve.wait_ge(fold_done, 1)
            for s in range(2):
                h, o, fo = SEQS[s] // 2, OFFS[s], HOFF[s]
                u = u_f[f]
                mirror = u[:, o + 2 * h - 1:o + h:-1]
                dve.tensor_tensor(fold[f][:, 0, fo + 1:fo + h], u[:, o + 1:o + h], mirror, ALU.add)
                dve.tensor_tensor(fold[f][:, 1, fo + 1:fo + h], u[:, o + 1:o + h], mirror, ALU.subtract)
                dve.tensor_copy(fold[f][:, 0, fo:fo + 1], u[:, o:o + 1])
                m = dve.memset(fold[f][:, 1, fo:fo + 1], 0.0)
            m.then_inc(fold_done, 1)

        def fold_split_lo(f):
            dve.wait_ge(fold_hi_done, f + 1)
            dve.tensor_tensor(fold_lo[f % 2][:].rearrange("p t n -> p (t n)"),
                              fold[f][:].rearrange("p t n -> p (t n)"),
                              fold_hi[f % 2][:].rearrange("p t n -> p (t n)"), ALU.subtract).then_inc(fold_lo_done, 1)

        def mix_split_hi(tiles):
            for f in tiles:
                for c in range(NCH):
                    dve.tensor_copy(hi_r[:, c, f, :], yr[:, f, c * CH:(c + 1) * CH]).then_inc(mixr_hi, 1)

        def pq_split_lo(f):
            b = f % 2
            for i in range(3):
                dve.wait_ge(pq_hi_done, 3 * f + i + 1)
                dve.scalar_tensor_tensor(pq_lo[b][:, i, :], bank[i][:], SEQS[0 if i < 2 else 1] ** -0.5,
                                         pq_hi[b][:, i, :], ALU.mult, ALU.subtract).then_inc(pq_lo_done, 1)

        def unfold(f):
            for s in range(2):
                h = SEQS[s] // 2
                o = OFFS[s]
                dve.wait_ge(e_done, 4 * f + 2 * s + 2)
                dve.wait_ge(eo_mm, 2 * f + s + 1)
                odd = bank[4][:] if s == 0 else bank[5][:, 256:512]
                m = dve.tensor_tensor(yf[:, f, o:o + h], e_sb[s][:, 0:h], odd[:, 0:h], ALU.subtract)
                if s == 0:
                    m = dve.tensor_tensor(yf[:, f, o + 2 * h - 1:o + h:-1], e_sb[s][:, 1:h], odd[:, 1:h], ALU.add)
                    m.then_inc(eo_done, 1)
                else:
                    m.then_inc(eo_done, 1)
                    dve.tensor_tensor(yf[:, f, o + 2 * h - 1:o + h:-1], e_sb[s][:, 1:h], odd[:, 1:h], ALU.add
                                      ).then_inc(eo_done, 1)

        edges(0)
        make_fold(0)
        edges(1)
        make_fold(1)
        fold_split_lo(0)
        edges(2)
        make_fold(2)
        dve.wait_ge(in_mm, NCH * NTILE)
        mix_split_hi(MIX_ORDER[:2])
        fold_split_lo(1)
        for i in range(8):
            dve.wait_ge(tab_hi_done, i + 1)
            dve.tensor_tensor(tab_lo[:, i // 4, i % 4, :], tab_raw[:, i, :], tab_hi[:, i // 4, i % 4, :],
                              ALU.subtract).then_inc(tab_lo_done, 1)
        pq_split_lo(0)
        mix_split_hi(MIX_ORDER[2:])
        edges(3)
        make_fold(3)
        for f in range(FT):
            if f + 2 < FT:
                fold_split_lo(f + 2)
            if f + 1 < FT:
                pq_split_lo(f + 1)
            unfold(f)
        for c in range(NCH):
            for f in range(FT):
                dve.wait_ge(mixf_hi, c * FT + f + 1)
                dve.tensor_tensor(lo_f[:, c, f, :], yf[:, f, c * CH:(c + 1) * CH], hi_f[:, c, f, :],
                                  ALU.subtract).then_inc(mixf_lo, 1)

        def norm_apply(n, c):
            rstd(n)
            for k in range(KD + 1):
                if k < KD:
                    if k >= 2:
                        dve.wait_ge(hlo_done, n * KD + k - 1)
                    dve.tensor_tensor(n_sq[k % 2][:], x[:, c, k, :], n_acc[:], ALU.mult).then_inc(xn_done, 1)
                if k > 0:
                    dve.wait_ge(hhi_done, n * KD + k)
                    dve.tensor_tensor(lo(c, k - 1), n_sq[(k - 1) % 2][:], hi(c, k - 1), ALU.subtract
                                      ).then_inc(hlo_done, 1)

        for c in range(NCH):
            s = SEQ_OF[c]
            dve.wait_ge(ld_x[c], 32)
            for d in range(KD):
                n = c * KD + d
                dve.wait_ge(out_mm, n + 1)
                b = d if c == 0 else (n - KD) % 6
                dve.scalar_tensor_tensor(x[:, c, d, :], bank[b][:], mod[:, GATE1, d, s:s + 1], x[:, c, d, :],
                                         ALU.mult, ALU.add).then_inc(out_evac, 1)
                if c > 0 and d == 4:
                    norm_apply(NCH + c - 1, c - 1)
            sum_squares(NCH + c)

        def hidden_lo(b, c):
            for j in range(JB):
                n = JB * NCH * b + JB * c + j
                dve.wait_ge(hid_hi_done, n + 1)
                dve.tensor_tensor(hid_lo[:, c, j, :], tmp[j][:], hid_hi[:, c, j, :], ALU.subtract
                                  ).then_inc(hid_lo_done, 1)

        def mlp_block(b, first=False, last=False):
            hidden_lo(b, 0)
            if first:
                norm_apply(2 * NCH - 1, NCH - 1)
            hidden_lo(b, 1)
            hidden_lo(b, 2)
            for c in range(NCH):
                s = SEQ_OF[c]
                for d in range(KD):
                    n = KD * c + d
                    dve.wait_ge(ff2_mm, NCH * KD * b + n + 1)
                    dve.scalar_tensor_tensor(x[:, c, d, :], bank[3 + n % 4][:], mod[:, GATE2, d, s:s + 1],
                                             x[:, c, d, :], ALU.mult, ALU.add).then_inc(ff2_evac, 1)
                    if last and c > 0 and d == 4:
                        final(c - 1)
                if last:
                    sum_squares(2 * NCH + c)

        def final(c):
            n = 2 * NCH + c
            rstd(n)
            for k in range(KD):
                dve.scalar_tensor_tensor(x[:, c, k, :], x[:, c, k, :], vec[:, V_GFIN + k:V_GFIN + k + 1], n_acc[:],
                                         ALU.mult, ALU.mult).then_inc(y_done, 1)

        mlp_block(0, first=True)
        with dve.Fori(1, NB - 1) as b:
            mlp_block(b)
        mlp_block(NB - 1, last=True)
        final(NCH - 1)

    @block.gpsimd
    def _(pool):
        pool.memset(c_silu[:], 0.0).then_inc(const_set, 1)
        pool.memset(ones[:], 1.0).then_inc(const_set, 1)
        pool.memset(eps[:], EPS).then_inc(const_set, 1)
        pool.memset(ident[:], 0.0).then_inc(pool_own, 1)
        pool.wait_ge(pool_own, 1)
        pool.affine_select(out=ident[:], in_=ident[:], compare_op=ALU.not_equal, fill=1.0, base=0,
                           pattern=[[-1, P]], channel_multiplier=1).then_inc(const_set, 1)
        for s in range(2):
            pool.memset(u_pad[:, UPAD[s]:UPAD[s] + PADL], 0.0)
            m = pool.memset(u_pad[:, UPAD[s] + PADL + SEQS[s]:UPAD[s] + PADL + SEQS[s] + PADR], 0.0)
        m.then_inc(const_set, 1)

        def split_win_lo(j):
            pool.wait_ge(win_hi_done, j + 1)
            pool.tensor_tensor(win_lo[j % 2][:].rearrange("p k m -> p (k m)"), win_raw[:],
                               win_hi[j % 2][:].rearrange("p k m -> p (k m)"), ALU.subtract
                               ).then_inc(win_lo_done, 1)

        split_win_lo(0)
        split_win_lo(1)

        def split_wg_lo(f):
            pool.wait_ge(wg_hi_done, f + 1)
            pool.tensor_tensor(wg_lo[:].rearrange("p g m -> p (g m)"), wg_raw[:],
                               wg_hi[:].rearrange("p g m -> p (g m)"), ALU.subtract).then_inc(wg_lo_done, 1)

        split_wg_lo(0)
        for j in range(NTILE):
            if j + 1 < NTILE and j > 0:
                split_win_lo(j + 1)
            if j % 2 == 0 and 0 < j < 2 * FT:
                split_wg_lo(j // 2)

        for i, (f, c) in enumerate((f, c) for f in MIX_ORDER for c in range(NCH)):
            pool.wait_ge(mixr_hi, i + 1)
            pool.tensor_tensor(lo_r[:, c, f, :], yr[:, f, c * CH:(c + 1) * CH], hi_r[:, c, f, :],
                               ALU.subtract).then_inc(mixr_lo, 1)
        for i in range(16):
            pool.wait_ge(wo_hi_done, i + 1)
            pool.tensor_tensor(wo_lo[WO_ORDER[i]][:].rearrange("p k m -> p (k m)"), wo_raw[i % 3][:],
                               wo_hi[WO_ORDER[i]][:].rearrange("p k m -> p (k m)"), ALU.subtract).then_inc(wo_lo_done, 1)

        def split_w(b, which):
            dst, src, hi_done, done = ((w1_lo, w1_hi, w1_hi_done, w1_lo_done),
                                       (w2_lo, w2_hi, w2_hi_done, w2_lo_done))[which]
            dst = dst[:].rearrange("p a m -> p (a m)")
            src = src[:].rearrange("p a m -> p (a m)")
            for i in range(4):
                cols = slice(i * CH, (i + 1) * CH)
                pool.wait_ge(hi_done, 4 * b + i + 1)
                m = pool.tensor_tensor(dst[:, cols], w12_raw[:, cols], src[:, cols], ALU.subtract)
            m.then_inc(done, 1)

        split_w(0, 0)
        split_w(0, 1)
        with pool.Fori(1, NB) as b:
            split_w(b, 0)
            split_w(b, 1)

    ctx.close()


def kernel(**inputs):
    import concourse.bacc as bacc
    from concourse.bass_utils import run_bass_kernel_spmd as run

    a = {k: np.asarray(v) for k, v in inputs.items()}

    def columns(v):
        return np.ascontiguousarray(np.asarray(v).reshape(-1, P).T)

    vec = np.concatenate([columns(v) for v in (
        a["c_prompt"], a["c_sample"], a["b_mod"], a["g_mix"], a["g_mlp"], a["g_final"], a["conv_w"],
        a["conv_b"], a["b_rgate"], a["b_igate"], a["lru_lambda"])], axis=1)

    def block_diagonal(w):
        lead = w.shape[:-3]
        out = np.zeros(lead + (w.shape[-3] // 2, P, P), w.dtype)
        out[..., :HEAD, :HEAD] = w[..., 0::2, :, :]
        out[..., HEAD:, HEAD:] = w[..., 1::2, :, :]
        return out

    xT = np.concatenate([a["x_prompt"][0].T, a["x_sample"][0].T], axis=1)
    w_in = a["w_in"][0].reshape(KD, P, NTILE, P).transpose(2, 1, 0, 3).reshape(NTILE, P, KD * P)
    gates = np.stack([block_diagonal(a["w_rgate"][0]), block_diagonal(a["w_igate"][0])], axis=1)
    w_gate = gates.transpose(2, 3, 0, 1, 4).reshape(FT, P, 4 * P)
    w_four = block_diagonal(a["w_fourier"][0]).transpose(1, 0, 2).reshape(P, FT * P)
    w_out = a["w_out"][0].reshape(KD, P, KD, P).transpose(2, 1, 0, 3).reshape(KD, P, KD * P)
    w_ff1 = a["w_ff1"][0].reshape(KD, P, NB, FB).transpose(2, 1, 0, 3).reshape(NB, P, KD * FB)
    w_ff2 = a["w_ff2"][0].reshape(NB, JB, P, D).transpose(0, 2, 1, 3).reshape(NB, P, JB * D)
    th = 2 * np.pi * (np.outer(np.arange(HEAD), np.arange(HEAD)) % HEAD) / HEAD
    dft_head = np.zeros((P, 2, P))
    for t, m in enumerate((np.cos(th), np.sin(th))):
        for h in range(2):
            dft_head[h * HEAD:(h + 1) * HEAD, t, h * HEAD:(h + 1) * HEAD] = m * HEAD ** -0.5
    ts = 2 * np.pi * (np.outer(np.arange(512), np.arange(CH)) % 1024) / 1024
    dft_seq = np.stack([np.cos(ts), np.sin(ts)]).reshape(2 * 4, P, CH).transpose(1, 0, 2)

    arrays, args = {}, {}
    nc = bacc.Bacc("TRN2", target_bir_lowering=False, num_devices=1, dynamic_dma_scratch_size=1024)
    for name, v in (("vec", vec), ("xT", xT), ("w_mod", a["w_mod"][0]), ("w_in", w_in), ("w_gate", w_gate),
                    ("w_four", w_four), ("w_out", w_out), ("w_ff1", w_ff1), ("w_ff2", w_ff2),
                    ("dft_head", dft_head.astype(np.float32)), ("dft_seq", dft_seq.astype(np.float32))):
        v = np.ascontiguousarray(v)
        arrays[f"in_{name}"] = v
        args[f"{name}_d"] = nc.dram_tensor(f"in_{name}", v.shape, mybir.dt.from_np(v.dtype),
                                           kind="ExternalInput").ap()
    args["yT_d"] = nc.dram_tensor("out_yT", (D, T), F32, kind="ExternalOutput").ap()
    build_encoder(nc, **args)
    r = run(nc, [arrays], core_ids=[0])
    yT = r.results[0]["out_yT"]
    return (np.ascontiguousarray(yT[:, :SEQS[0]].T)[None], np.ascontiguousarray(yT[:, SEQS[0]:].T)[None])
```

```python
from contextlib import ExitStack

import numpy as np

import concourse.bass as bass
from concourse import mybir

F32 = mybir.dt.float32
F32R = mybir.dt.float32r
ALU = mybir.AluOpType
ACT = mybir.ActivationFunctionType
AX = mybir.AxisListType

P = 128
CH = 512
SEQS = (1024, 512)
OFFS = (0, 1024)
T = sum(SEQS)
NCH = T // CH
SEQ_OF = (0, 0, 1)
D = 1024
KD = D // P
DF = 512
FT = DF // P
HEAD = 64
DFF = 4096
FB = 256
NB = DFF // FB
JB = FB // P
EPS = 1e-6
LRU_C = 8.0
NMOD = 6
NTILE = 3 * FT
TILES = [FT + j // 2 if j % 2 == 0 else 2 * FT + j // 2 for j in range(2 * FT)] + list(range(FT))
PADL, PADR = 2, 1
UPAD = (0, PADL + SEQS[0] + PADR)
UPADW = UPAD[1] + PADL + SEQS[1] + PADR

V_C = 0
V_BMOD = V_C + 2 * KD
V_GMIX = V_BMOD + NMOD * KD
V_GMLP = V_GMIX + KD
V_GFIN = V_GMLP + KD
V_CONVW = V_GFIN + KD
V_CONVB = V_CONVW + 4 * FT
V_BR = V_CONVB + FT
V_BI = V_BR + 2 * FT
V_LAM = V_BI + 2 * FT
NV = V_LAM + 2 * FT
SHIFT1, SCALE1, GATE1, SHIFT2, SCALE2, GATE2 = range(NMOD)


def build_encoder(nc, vec_d, xT_d, w_mod_d, w_mod1_d, w_in_d, w_gate_d, w_four_d, w_out_d, w_ff1_d, w_ff2_d,
                  dft_head_d, dft_seq_d, yT_d):
    ctx = ExitStack()

    def sem(name):
        return ctx.enter_context(nc.semaphore(name))

    base = (nc.sbuf_base + 31) // 32 * 32
    at = {}

    def place(name, shape, dtype, offset):
        at[name] = offset
        return nc.alloc_sbuf_tensor_at(name, shape, dtype, offset=offset)

    cur = [base]

    def fixed(name, shape, dtype=F32):
        t = place(name, shape, dtype, cur[0])
        cur[0] += (4 * int(np.prod(shape[1:])) + 31) // 32 * 32
        return t

    vec = fixed("vec", [P, NV])
    ones = fixed("ones", [P, P])
    ident = fixed("ident", [P, P])
    dft_head = fixed("dft_head", [P, 2, P])
    c_sig = fixed("c_sig", [P, 2 * KD])
    pick = fixed("pick", [P, 2])
    c_silu = fixed("c_silu", [P, KD, 32])
    mod = fixed("mod", [P, NMOD, KD, 2])
    amp1 = fixed("amp1", [P, KD, 2])
    amp2 = fixed("amp2", [P, KD, 2])
    eps = fixed("eps", [P, 1])
    decay = fixed("decay", [P, 2, 2 * FT])
    sp = fixed("sp", [P, 6, 2 * FT])
    edge = fixed("edge", [P, FT, 4])
    alt = fixed("alt", [P, 2, 2])
    bias_e = fixed("bias_e", [P, FT, 2, 2])
    sd = fixed("sd", [P, 4])
    rc = fixed("rc", [P, 4])
    A0 = cur[0]
    QT = 4 * T
    HALF = FT * QT
    hi_f = place("hi_f", [P, NCH, FT, CH], F32R, A0)
    lo_f = place("lo_f", [P, NCH, FT, CH], F32R, A0 + HALF)
    hi_r = place("hi_r", [P, NCH, FT, CH], F32R, A0 + 2 * HALF)
    lo_r = place("lo_r", [P, NCH, FT, CH], F32R, A0 + 3 * HALF)
    X0 = A0 + 4 * HALF
    W0 = X0 + 2 * HALF
    x = place("x", [P, NCH, KD, CH], F32, X0)

    def hi(c, k):
        return (hi_f, hi_r)[k // FT][:, c, k % FT, :]

    def lo(c, k):
        return (lo_f, lo_r)[k // FT][:, c, k % FT, :]

    rr = place("rr", [P, T], F32, X0)
    ii = place("ii", [P, T], F32, X0 + QT)
    aa = place("aa", [P, T], F32, X0 + 2 * QT)
    qq = place("qq", [P, T], F32, X0 + 3 * QT)
    uc = place("uc", [P, T], F32, X0 + 4 * QT)
    hf = place("hf", [P, T], F32, X0 + 5 * QT)
    uc_hi = place("uc_hi", [P, T], F32R, X0 + 6 * QT)
    uc_lo = place("uc_lo", [P, T], F32R, X0 + 7 * QT)
    yr = place("yr", [P, FT, T], F32, W0)
    u_pad = place("u_pad", [P, UPADW], F32, W0 + HALF)
    s0 = W0 + HALF + (4 * UPADW + 31) // 32 * 32
    mod_raw = place("mod_raw", [P, 2, 2048], F32, s0)
    ab_hi = place("ab_hi", [P, 2, FT, P], F32R, s0)
    ab_lo = place("ab_lo", [P, 2, FT, P], F32R, s0 + 4096)
    a_f32 = place("a_f32", [P, FT, P], F32, s0 + 8192)
    mod_row = place("mod_row", [P, CH], F32, s0 + 16384)
    s1 = s0 + 16384 + 2048
    win_hi = [place(f"win_hi{i}", [P, KD, P], F32R, s1 + 8192 * i) for i in range(2)]
    win_lo = [place(f"win_lo{i}", [P, KD, P], F32R, s1 + 8192 * i + 4096) for i in range(2)]
    s2 = s1 + 16384
    win_raw = place("win_raw", [P, KD * P], F32, s2)
    s3 = s2 + 4096
    wg_hi = place("wg_hi", [P, 4, P], F32R, s3)
    wg_lo = place("wg_lo", [P, 4, P], F32R, s3 + 2048)
    wg_raw = place("wg_raw", [P, 4 * P], F32, s3 + 4096)
    assert s3 + 6144 <= nc.sbuf_usable_end
    sq8 = place("sq8", [P, KD, CH], F32, W0)
    sq8_other = place("sq8_other", [P, KD, CH], F32, A0 + 16384)
    diag_first = place("diag_first", [P, CH], F32, W0 + 16384)
    diag_last = place("diag_last", [P, CH], F32, W0 + 32768)
    rstd_sb = place("rstd_sb", [P, CH], F32, W0 + 18432)
    NQ = 4
    QF = D // NQ
    mod_first = [place(f"mod_first{q}", [P, 2, KD, QF], F32, o)
                 for q, o in enumerate((A0, A0 + 2 * HALF, A0 + 2 * HALF + 16384, s0))]
    wf_raw = place("wf_raw", [P, FT * P], F32, s3 + 4096)
    u_f = [place("u_f0", [P, T], F32, s0 + 10240), place("u_f1", [P, T], F32, W0 + HALF),
           place("u_f2", [P, T], F32, X0 + 6 * QT), place("u_f3", [P, T], F32, X0 + 7 * QT)]
    HT = T // 2
    HOFF = (0, SEQS[0] // 2)
    fold = [place(f"fold{f}", [P, 2, HT], F32, o) for f, o in enumerate((s3, X0 + 3 * QT, s3, s0 + 10240))]
    fold_at = (X0 + 4 * QT, A0 + 32768)
    fold_hi = [place(f"fold_hi{i}", [P, 2, HT], F32R, o) for i, o in enumerate(fold_at)]
    fold_lo = [place(f"fold_lo{i}", [P, 2, HT], F32R, o + QT) for i, o in enumerate(fold_at)]
    tab_hi = place("tab_hi", [P, 2, 4, CH], F32R, A0)
    tab_lo = place("tab_lo", [P, 2, 4, CH], F32R, A0 + 16384)
    tab_raw = place("tab_raw", [P, 8, CH], F32, X0)
    pq_at = (s1, W0 + 12288)
    pq_hi = [place(f"pq_hi{i}", [P, 3, CH], F32R, o) for i, o in enumerate(pq_at)]
    pq_lo = [place(f"pq_lo{i}", [P, 3, CH], F32R, o + 6144) for i, o in enumerate(pq_at)]
    e_sb = [place(f"e_sb{i}", [P, CH], F32, s2 + 2048 * i) for i in range(2)]
    yf = place("yf", [P, FT, T], F32, X0)
    WO_ORDER = (0, 1, 2, 4, 5, 3, 11, 6, 7, 12, 13, 14, 15, 8, 9, 10)
    wo_slot = dict(zip(WO_ORDER, (0, 1, 2, 6, 7, 8, 9, 10, 11, 12, 13, 14, 15, 3, 4, 5)))
    wo_at = [W0 + 4096 * wo_slot[q] for q in range(16)]
    wo_hi = [place(f"wo_hi{q}", [P, FT, P], F32R, o) for q, o in enumerate(wo_at)]
    wo_lo = [place(f"wo_lo{q}", [P, FT, P], F32R, o + 2048) for q, o in enumerate(wo_at)]
    wo_raw = [place(f"wo_raw{i}", [P, FT * P], F32, s3 + 2048 * i) for i in range(3)]
    tmp = [place(f"tmp{i}", [P, CH], F32, s3 + 2048 * i) for i in range(3)]
    assert s2 >= W0 + 65536
    n_acc = place("n_acc", [P, CH], F32, s2 + 2048)
    n_sq = tmp[:2]
    n_t = [place("n_t", [P, CH], F32, s2), tmp[2]]
    w1_hi = place("w1_hi", [P, KD, FB], F32R, W0)
    w1_lo = place("w1_lo", [P, KD, FB], F32R, W0 + 8192)
    w2_hi = place("w2_hi", [P, JB, D], F32R, W0 + 16384)
    w2_lo = place("w2_lo", [P, JB, D], F32R, W0 + 24576)
    w12_raw = place("w12_raw", [P, KD * FB], F32, W0 + 32768)
    hid_hi = place("hid_hi", [P, NCH, JB, CH], F32R, W0 + 40960)
    hid_lo = place("hid_lo", [P, NCH, JB, CH], F32R, W0 + 40960 + 12288)

    bank = [ctx.enter_context(nc.psum_tensor(f"bank{i}", [P, CH], F32)) for i in range(8)]
    GB, MB, NBK = (4, 5, 7), 6, 7

    ld_vec, ld_dft, ld_win, ld_wg, ld_wf, ld_tab, ld_w12 = map(
        sem, ("ld_vec", "ld_dft", "ld_win", "ld_wg", "ld_wf", "ld_tab", "ld_w12"))
    ld_x = [sem(f"ld_x{c}") for c in range(NCH)]
    ld_first = [sem(f"ld_first{q}") for q in range(NQ)]
    ld_mod = [sem(f"ld_mod{i}") for i in range(2)]
    ld_wo = [sem(f"ld_wo{i}") for i in range(3)]
    st_y = [sem(f"st_y{i}") for i in range(4)]
    const_set = sem("const_set")
    sig_c = sem("sig_c")
    silu_c = sem("silu_c")
    lam_exp = sem("lam_exp")
    lam_abs = sem("lam_abs")
    decay_set = sem("decay_set")
    dve_own = sem("dve_own")
    pool_own = sem("pool_own")
    sq_done = sem("sq_done")
    sq_added = sem("sq_added")
    sq_added_p = sem("sq_added_p")
    amp_set = sem("amp_set")
    lru_ix = sem("lru_ix")
    norm_mm = sem("norm_mm")
    sd_done = sem("sd_done")
    rstd_done = sem("rstd_done")
    norm_bc = sem("norm_bc")
    xn_done = sem("xn_done")
    rstd_copied = sem("rstd_copied")
    xn_done_p = sem("xn_done_p")
    h_done = sem("h_done")
    hhi_done = sem("hhi_done")
    hlo_done = sem("hlo_done")
    hlo_done_p = sem("hlo_done_p")
    mod_mm = sem("mod_mm")
    mod_rows = sem("mod_rows")
    mod_tr = sem("mod_tr")
    mod_cols = sem("mod_cols")
    win_hi_done, win_lo_done = sem("win_hi_done"), sem("win_lo_done")
    wg_hi_done, wg_lo_done = sem("wg_hi_done"), sem("wg_lo_done")
    in_mm = sem("in_mm")
    in_evac = sem("in_evac")
    conv_done = sem("conv_done")
    gate_mm = sem("gate_mm")
    gate_sig = sem("gate_sig")
    lru_a, lru_t, lru_q = sem("lru_a"), sem("lru_t"), sem("lru_q")
    lru_m2 = sem("lru_m2")
    lru_m = sem("lru_m")
    lru_scan = sem("lru_scan")
    lru_done = sem("lru_done")
    ab_mm, ab_act, ab_set = sem("ab_mm"), sem("ab_act"), sem("ab_set")
    fold_done = sem("fold_done")
    fold_hi_done, fold_lo_done = sem("fold_hi_done"), sem("fold_lo_done")
    edge_done = sem("edge_done")
    pq_mm = sem("pq_mm")
    edge_mm = sem("edge_mm")
    pq_hi_done, pq_lo_done = sem("pq_hi_done"), sem("pq_lo_done")
    bias_done = sem("bias_done")
    yf_edge = sem("yf_edge")
    eo_mm = sem("eo_mm")
    e_done = sem("e_done")
    eo_done = sem("eo_done")
    tab_hi_done, tab_lo_done = sem("tab_hi_done"), sem("tab_lo_done")
    mixr_hi, mixr_lo = sem("mixr_hi"), sem("mixr_lo")
    mixf_hi, mixf_lo = sem("mixf_hi"), sem("mixf_lo")
    wo_hi_done, wo_lo_done = sem("wo_hi_done"), sem("wo_lo_done")
    out_mm = sem("out_mm")
    out_evac = sem("out_evac")
    w1_hi_done, w1_lo_done = sem("w1_hi_done"), sem("w1_lo_done")
    w2_hi_done, w2_lo_done = sem("w2_hi_done"), sem("w2_lo_done")
    ff1_mm, ff1_relu = sem("ff1_mm"), sem("ff1_relu")
    ff1_sq = sem("ff1_sq")
    hid_hi_done, hid_lo_done = sem("hid_hi_done"), sem("hid_lo_done")
    ff2_mm, ff2_evac = sem("ff2_mm"), sem("ff2_evac")
    y_done = sem("y_done")

    def after(eng, s, value):
        if not isinstance(value, int) or value > 0:
            eng.wait_ge(s, value)

    NLOAD = NCH * KD
    NN = NCH

    def shared(n):
        return n < NN or n >= 2 * NN

    def pool_share(n):
        return 0 if not shared(n) else 4 if n < NN else 6

    def add_order(n):
        return tuple(range(pool_share(n) + 1, KD)) + ((0,) if shared(n) else ())

    def adds_v(n):
        return sum(len(add_order(m)) for m in range(n))

    def adds_p(n):
        return sum(pool_share(m) - 1 for m in range(n) if shared(m))

    def squares(n):
        return sq8_other if n == 1 else sq8

    def xn_count(n):
        return (n - 1) * KD

    def norm_bank(n):
        return bank[(4, 5, 3)[n] if n < NN else NBK if n < 2 * NN else n - 2 * NN]

    def norm_diag(n):
        return diag_first if n < NN else n_acc if n < 2 * NN else diag_last

    def gates_after(j, c):
        f, r = divmod(NCH * j + c - (2 * NCH - 1), 2 * NCH)
        return (2 * f + r // 2, r % 2) if 0 <= f < FT and r < 4 else None

    def mod_steps_after(j):
        return range(KD + 2 * j, KD + 2 * j + 2) if j < KD else ()

    LRU_ALL = 2 * FT
    MIX_ORDER = (2, 3, 0, 1)

    def mod_count(s):
        return NQ + s - KD + 1

    MOD_AFTER = {(5, 0): 1, (9, 1): 2}
    AB_AFTER = 2 * FT + 1
    block = ctx.enter_context(nc.Block())

    @block.sync
    def _(sp):
        sp.dma_start(vec[:], vec_d).then_inc(ld_vec, 16)
        for c in range(NCH):
            sp.dma_start(x[:, c, :, :], xT_d[:, c * CH:(c + 1) * CH].rearrange("(k p) n -> p k n", p=P)
                         ).then_inc(ld_x[c], 16)
        sp.dma_start(win_raw[:], w_in_d[TILES[0]]).then_inc(ld_win, 16)
        sp.dma_start(dft_head[:], dft_head_d).then_inc(ld_dft, 16)

        for q in range(NQ):
            sp.dma_start(mod_first[q][:].rearrange("p i k n -> p (i k n)"), w_mod1_d[q]).then_inc(ld_first[q], 16)

        def load_mod(s):
            r, k = divmod(s, KD)
            sp.wait_ge(mod_mm, mod_count(max(s - 2, KD - 1)))
            sp.dma_start(mod_raw[:, s % 2, :], w_mod_d[k * P:(k + 1) * P, (r - 1) * 2048:r * 2048]
                         ).then_inc(ld_mod[s % 2], 16)

        sp.dma_start(wg_raw[:], w_gate_d[0]).then_inc(ld_wg, 16)
        for j in range(NTILE):
            if j + 1 < NTILE:
                sp.wait_ge(win_lo_done, j + 1)
                sp.dma_start(win_raw[:], w_in_d[TILES[j + 1]]).then_inc(ld_win, 16)
            for s in mod_steps_after(j):
                load_mod(s)
            if j % 2 == 1 and j // 2 + 1 < FT:
                f = j // 2 + 1
                sp.wait_ge(wg_lo_done, f)
                sp.dma_start(wg_raw[:], w_gate_d[f]).then_inc(ld_wg, 16)
            if j == 2 * FT - 1:
                sp.wait_ge(wg_lo_done, FT)
                sp.dma_start(wf_raw[:], w_four_d).then_inc(ld_wf, 16)
        sp.wait_ge(lru_done, FT)
        sp.dma_start(tab_raw[:], dft_seq_d).then_inc(ld_tab, 16)

        def load_wo(i):
            if i < 3:
                sp.wait_ge(fold_lo_done, 3)
            else:
                sp.wait_ge(wo_lo_done, i - 2)
            half, d = divmod(WO_ORDER[i], KD)
            k0 = FT * (1 - half)
            sp.dma_start(wo_raw[i % 3][:], w_out_d[d, :, k0 * P:(k0 + FT) * P]).then_inc(ld_wo[i % 3], 16)

        for i in range(16):
            load_wo(i)
        sp.wait_ge(mixf_hi, FT * NCH)
        sp.wait_ge(mixf_lo, FT * NCH)
        for c in range(NCH):
            sp.dma_start(x[:, c, :, :], xT_d[:, c * CH:(c + 1) * CH].rearrange("(k p) n -> p k n", p=P)
                         ).then_inc(ld_x[c], 16)
        sp.wait_ge(out_mm, (NCH - 1) * KD + 4)
        sp.dma_start(w12_raw[:], w_ff1_d[0]).then_inc(ld_w12, 16)
        sp.wait_ge(w1_lo_done, 1)
        sp.dma_start(w12_raw[:], w_ff2_d[0]).then_inc(ld_w12, 16)
        with sp.Fori(1, NB) as b:
            sp.wait_ge(w2_lo_done, b)
            sp.dma_start(w12_raw[:], w_ff1_d[bass.ds(b, 1), :, :].rearrange("o p n -> (o p) n")
                         ).then_inc(ld_w12, 16)
            sp.wait_ge(w1_lo_done, b + 1)
            sp.dma_start(w12_raw[:], w_ff2_d[bass.ds(b, 1), :, :].rearrange("o p n -> (o p) n")
                         ).then_inc(ld_w12, 16)
        for c in range(NCH):
            for q in range(4):
                sp.wait_ge(y_done, c * KD + 2 * q + 2)
                if c > 0:
                    sp.wait_ge(st_y[q], 16 * c)
                rows = yT_d[2 * q * P:2 * (q + 1) * P, c * CH:(c + 1) * CH]
                sp.dma_start(rows.rearrange("(k p) n -> p k n", p=P), x[:, c, 2 * q:2 * q + 2, :]
                             ).then_inc(st_y[q], 16)
        for q in range(4):
            sp.wait_ge(st_y[q], 16 * NCH)

    @block.tensor
    def _(pe):
        def three(out, w_hi, w_lo, v_hi, v_lo, first, last):
            pe.matmul(out, w_lo, v_hi, start=first, stop=False)
            pe.matmul(out, w_hi, v_lo, start=False, stop=False)
            return pe.matmul(out, w_hi, v_hi, start=False, stop=last)

        def norm_sum(n):
            pe.wait_ge(sq_added, adds_v(n + 1))
            if NN < n < 2 * NN:
                pe.wait_ge(xn_done, xn_count(n))
            total = squares(n)[:, pool_share(n), :] if shared(n) else n_acc[:]
            for b in range(4):
                m = pe.matmul(norm_bank(n)[:, b:b + 1], total[:, b * P:(b + 1) * P], ones[:, 0:1],
                              start=True, stop=True)
            m.then_inc(norm_mm, 1)

        def norm_spread(n):
            pe.wait_ge(rstd_done, n + 1)
            pe.matmul(norm_bank(n)[:], ones[:], norm_diag(n)[:], start=True, stop=True).then_inc(norm_bc, 1)

        def mod_step(s):
            r, k = divmod(s, KD)
            if k == 0 and r > 0:
                pe.wait_ge(mod_rows, NQ + r - 1)
            pe.wait_ge(ld_mod[s % 2], 16 * ((s - KD) // 2 + 1))
            for q in range(4):
                m = pe.matmul(bank[MB][32 * q:32 * q + 32, :], c_silu[:, k, :],
                              mod_raw[:, s % 2, q * CH:(q + 1) * CH], start=(k == 0), stop=(k == KD - 1),
                              skip_group_check=True)
            m.then_inc(mod_mm, 1)

        def mod_quarter(q):
            after(pe, mod_rows, q)
            pe.wait_ge(ld_first[q], 16)
            for k in range(KD):
                g = 32 * (k % 4)
                m = pe.matmul(bank[MB][g:g + 32, :], c_silu[:, k, :], mod_first[q][:, :, k, :],
                              start=(k < 4), stop=(k >= 4), skip_group_check=True)
            m.then_inc(mod_mm, 1)

        def mod_quarter_sum(q):
            pe.wait_ge(mod_rows, q + 1)
            after(pe, mod_cols, q)
            for b in range(4):
                m = pe.matmul(bank[NBK][:, 2 * b:2 * b + 2], mod_row[:, b * P:(b + 1) * P], pick[:],
                              start=True, stop=True)
            m.then_inc(mod_tr, 1)

        def first_tile(q):
            pe.wait_ge(win_lo_done, 1)
            for c in range(NCH):
                for k in (2 * q, 2 * q + 1):
                    pe.wait_ge((hlo_done, hlo_done_p)[k % 2], q * NCH + c + 1)
                    m = three(bank[c][:], win_hi[0][:, k, :], win_lo[0][:, k, :], hi(c, k), lo(c, k),
                              k == 0, k == KD - 1)
                if q == NQ - 1:
                    m.then_inc(in_mm, 1)

        def mod_transpose(r):
            pe.wait_ge(mod_rows, NQ + r)
            after(pe, gate_sig, (0, LRU_ALL // 2, LRU_ALL)[r] * 2 * NCH)
            for b in range(4):
                m = pe.transpose(bank[NBK][:, b * P:(b + 1) * P], mod_row[:, b * P:(b + 1) * P], ident[:])
            m.then_inc(mod_tr, 1)

        def in_tile(j, c):
            n = NCH * j + c
            if n >= 4:
                pe.wait_ge(in_evac, n - 3)
            elif n == 3:
                pe.wait_ge(xn_done, xn_count(NN))
            pe.wait_ge(win_lo_done, j + 1)
            for k in range(KD):
                m = three(bank[n % 4][:], win_hi[j % 2][:, k, :], win_lo[j % 2][:, k, :], hi(c, k), lo(c, k),
                          k == 0, k == KD - 1)
            m.then_inc(in_mm, 1)

        def gates(g, gate):
            f, d = divmod(g, 2)
            pe.wait_ge(wg_lo_done, f + 1)
            pe.wait_ge(conv_done, f + 1)
            if g == 0:
                pe.wait_ge(xn_done, xn_count(NN))
                pe.wait_ge(rstd_copied, 1)
            pe.wait_ge(mod_cols, NQ if g < LRU_ALL // 2 else NQ + 1)
            for c in range(NCH):
                after(pe, gate_sig, (2 * g + gate - 1) * NCH + c + 1)
                cols = slice(c * CH, (c + 1) * CH)
                three(bank[GB[c]][:], wg_hi[:, 2 * d + gate, :], wg_lo[:, 2 * d + gate, :],
                      uc_hi[:, cols], uc_lo[:, cols], True, True).then_inc(gate_mm, 1)

        pe.wait_ge(const_set, 4)
        norm_sum(0)
        norm_spread(0)
        norm_sum(1)
        norm_spread(1)
        norm_sum(2)
        pe.wait_ge(silu_c, 1)
        mod_quarter(0)
        norm_spread(2)
        mod_quarter_sum(0)
        for q in range(1, NQ - 1):
            mod_quarter(q)
            mod_quarter_sum(q)
        mod_quarter(NQ - 1)
        first_tile(0)
        mod_quarter_sum(NQ - 1)
        for q in range(1, NQ):
            first_tile(q)
        for j in range(NTILE):
            for c in range(NCH):
                if j > 0:
                    in_tile(j, c)
                if gates_after(j, c):
                    gates(*gates_after(j, c))
                if (j, c) in MOD_AFTER:
                    mod_transpose(MOD_AFTER[j, c])
            for s in mod_steps_after(j):
                mod_step(s)
            if j == AB_AFTER:
                pe.wait_ge(ld_dft, 16)
                pe.wait_ge(ld_wf, 16)
                pe.wait_ge(gate_sig, 2 * NCH * LRU_ALL)
                for t in range(2):
                    m = pe.matmul(bank[GB[t]][:], dft_head[:, t, :], wf_raw[:], start=True, stop=True)
                m.then_inc(ab_mm, 1)

        BE, BT = 3, 5

        def pq(f):
            if f == 0:
                pe.wait_ge(in_evac, NCH * NTILE)
                pe.wait_ge(ab_set, 1)
            pe.wait_ge(fold_lo_done, f + 1)
            for i, parts in enumerate((((0, 0),), ((1, 0),), ((0, 1), (1, 1)))):
                after(pe, pq_lo_done, 3 * (f - 1) + i + 1)
                for t, s in parts:
                    for n in range(SEQS[s] // 2 // P):
                        cols = slice(HOFF[s] + n * P, HOFF[s] + (n + 1) * P)
                        o = (n + 2 * s * t) * P
                        m = three(bank[i][:, o:o + P], fold_hi[f % 2][:, t, cols], fold_lo[f % 2][:, t, cols],
                                  ab_hi[:, t, f, :], ab_lo[:, t, f, :], True, True)
                m.then_inc(pq_mm, 1)

        def edge_products():
            pe.wait_ge(mod_cols, NQ + 2)
            pe.wait_ge(edge_done, FT)
            for f in range(FT):
                m = pe.matmul(bank[NBK][:, 4 * f:4 * f + 4], a_f32[:, f, :], edge[:, f, :], start=True, stop=True)
            m.then_inc(edge_mm, 1)

        def eo(f):
            b = f % 2
            for t in range(2):
                pe.wait_ge(pq_lo_done, 3 * f + t + 1)
                pe.wait_ge(tab_lo_done, 4 * (t + 1))
                after(pe, eo_done, 3 * (f - 1) + 1)
                for n in range(4):
                    m = three(bank[BE + t][:], pq_hi[b][:, t, n * P:(n + 1) * P], pq_lo[b][:, t, n * P:(n + 1) * P],
                              tab_hi[:, t, n, :], tab_lo[:, t, n, :], n == 0, n == 3)
            m.then_inc(eo_mm, 1)
            pe.wait_ge(pq_lo_done, 3 * f + 3)
            after(pe, eo_done, 3 * f)
            for t in range(2):
                for n in range(2):
                    w = slice((2 * t + n) * P, (2 * t + n + 1) * P)
                    m = three(bank[BT][:, t * 256:(t + 1) * 256], pq_hi[b][:, 2, w], pq_lo[b][:, 2, w],
                              tab_hi[:, t, n, ::2], tab_lo[:, t, n, ::2], n == 0, n == 1)
            m.then_inc(eo_mm, 1)

        pq(0)
        for f in range(FT):
            if f + 1 < FT:
                pq(f + 1)
            if f == 0:
                edge_products()
            eo(f)

        def out_half(c, d, half, b, first, last):
            for kk in range(FT):
                k = FT * (1 - half) + kk
                q = half * KD + d
                m = three(bank[b][:], wo_hi[q][:, kk, :], wo_lo[q][:, kk, :], hi(c, k), lo(c, k),
                          first and kk == 0, last and kk == FT - 1)
            return m

        pe.wait_ge(mixr_lo, FT * NCH)
        for d in range(KD):
            if d == BE:
                pe.wait_ge(eo_done, 3 * FT)
            if d == NBK:
                pe.wait_ge(yf_edge, 1)
            pe.wait_ge(wo_lo_done, WO_ORDER.index(d) + 1)
            out_half(0, d, 0, d, True, False)
        for d in range(KD):
            pe.wait_ge(wo_lo_done, WO_ORDER.index(KD + d) + 1)
            pe.wait_ge(mixf_lo, FT)
            out_half(0, d, 1, d, False, True).then_inc(out_mm, 1)
        pe.wait_ge(mixf_lo, FT * NCH)
        for c in range(1, NCH):
            for d in range(KD):
                n = (c - 1) * KD + d
                pe.wait_ge(out_evac, n % 6 + 1 if n < 6 else KD + n - 5)
                out_half(c, d, 0, n % 6, True, False)
                out_half(c, d, 1, n % 6, False, True).then_inc(out_mm, 1)
                if d == 0:
                    if c == 1:
                        pe.wait_ge(out_evac, KD)
                    norm_sum(NN + c - 1)
                elif d == 1:
                    norm_spread(NN + c - 1)
        pe.wait_ge(out_evac, NCH * KD)

        def mlp_block(b, first=False, last=False):
            pe.wait_ge(w1_lo_done, b + 1)
            for c in range(NCH):
                for j in range(JB):
                    n = JB * c + j
                    after(pe, ff1_relu, JB * NCH * b + n - 2)
                    for k in range(KD):
                        if first and j == 0:
                            pe.wait_ge(hlo_done, NLOAD // 2 + c * KD + k + 1)
                        w = slice(j * P, (j + 1) * P)
                        m = three(bank[n % 3][:], w1_hi[:, k, w], w1_lo[:, k, w], hi(c, k), lo(c, k),
                                  k == 0, k == KD - 1)
                        if first and n == 0 and k == KD // 2:
                            norm_sum(2 * NN - 1)
                    m.then_inc(ff1_mm, 1)
                    if first and n == 0:
                        norm_spread(2 * NN - 1)
            pe.wait_ge(w2_lo_done, b + 1)
            for c in range(NCH):
                pe.wait_ge(hid_lo_done, JB * NCH * b + JB * (c + 1))
                for d in range(KD):
                    n = KD * c + d
                    after(pe, ff2_evac, NCH * KD * b + n - 3)
                    w = slice(d * P, (d + 1) * P)
                    for j in range(JB):
                        m = three(bank[3 + n % 4][:], w2_hi[:, j, w], w2_lo[:, j, w],
                                  hid_hi[:, c, j, :], hid_lo[:, c, j, :], j == 0, j == JB - 1)
                    m.then_inc(ff2_mm, 1)
                    if last and c == 1 and d == 0:
                        pe.wait_ge(ff1_relu, JB * NCH * NB)
                    if last and c > 0 and d == 2:
                        norm_sum(2 * NN + c - 1)
                    elif last and c > 0 and d == 3:
                        norm_spread(2 * NN + c - 1)

        mlp_block(0, first=True)
        with pe.Fori(1, NB - 1) as b:
            mlp_block(b)
        mlp_block(NB - 1, last=True)
        norm_sum(3 * NN - 1)
        norm_spread(3 * NN - 1)

    @block.scalar
    def _(act):
        def square(n, k):
            c = n % NN
            if n < NN:
                act.wait_ge(ld_x[c], 16)
            elif n < 2 * NN:
                act.wait_ge(out_evac, c * KD + k + 1)
            else:
                act.wait_ge(ff2_evac, (NB - 1) * NCH * KD + c * KD + k + 1)
            if shared(n):
                if k == 0 and n != 1:
                    after(act, norm_mm, 1 if n == 2 else n)
                dst = squares(n)[:, k, :]
            else:
                if n == NN and k == 0:
                    act.wait_ge(wo_lo_done, 16)
                elif k == 0:
                    act.wait_ge(norm_bc, n)
                elif k > 2:
                    act.wait_ge(sq_added, adds_v(n) + k - 2)
                dst = n_acc[:] if k == 0 else n_sq[k % 2][:]
            act.activation(dst, x[:, c, k, :], ACT.Square).then_inc(sq_done, 1)

        def root(n):
            act.wait_ge(norm_mm, n + 1)
            after(act, rstd_done, n)
            act.activation(sd[:], norm_bank(n)[:, 0:4], ACT.Sqrt, bias=eps[:], scale=1.0 / D
                           ).then_inc(sd_done, 1)

        def split_win_hi(j):
            act.wait_ge(ld_win, 16 * (j + 1))
            if j >= 2:
                act.wait_ge(in_mm, NCH * (j - 1))
            act.activation(win_hi[j % 2][:].rearrange("p k m -> p (k m)"), win_raw[:], ACT.Copy
                           ).then_inc(win_hi_done, 1)

        def split_wg_hi(f):
            act.wait_ge(ld_wg, 16 * (f + 1))
            after(act, gate_mm, 4 * NCH * f)
            act.activation(wg_hi[:].rearrange("p g m -> p (g m)"), wg_raw[:], ACT.Copy).then_inc(wg_hi_done, 1)

        act.wait_ge(ld_vec, 16)
        act.activation(c_sig[:], vec[:, V_C:V_C + 2 * KD], ACT.Sigmoid).then_inc(sig_c, 1)
        act.wait_ge(lam_abs, 1)
        act.activation(sp[:, 1, :], sp[:, 0, :], ACT.Exp, scale=-1.0).then_inc(lam_exp, 1)
        act.wait_ge(const_set, 4)
        for n in range(NN):
            for k in range(KD):
                square(n, k)
                if n > 0 and k == 3:
                    root(n - 1)
        act.wait_ge(norm_bc, 2)
        act.activation(rstd_sb[:], norm_bank(1)[:], ACT.Copy).then_inc(rstd_copied, 1)
        split_win_hi(0)

        def mod_copy(n):
            act.wait_ge(mod_mm, n + 1 if n < NQ else mod_count((n - NQ + 2) * KD - 1))
            after(act, mod_tr, n)
            act.activation(mod_row[:], bank[MB][:], ACT.Copy).then_inc(mod_rows, 1)


        def modulate_first(q):
            act.wait_ge(mod_cols, q + 1)
            act.wait_ge(amp_set, q + 1)
            for c, k in ((c, k) for c in range(NCH) for k in (2 * q, 2 * q + 1)):
                s = SEQ_OF[c]
                if c == 1:
                    act.wait_ge(xn_done_p, KD)
                else:
                    act.wait_ge(xn_done, KD if c == 0 else 2 * KD)
                act.activation(x[:, c, k, :], x[:, c, k, :], ACT.Identity, bias=mod[:, SHIFT1, k, s:s + 1],
                               scale=amp1[:, k, s:s + 1]).then_inc(h_done, 1)

        root(NN - 1)
        mod_copy(0)
        mod_copy(1)
        mod_copy(2)
        modulate_first(0)
        modulate_first(1)
        mod_copy(3)
        modulate_first(2)
        split_win_hi(1)
        modulate_first(3)
        act.wait_ge(hlo_done, NLOAD // 2)
        act.wait_ge(hlo_done_p, NLOAD // 2)
        split_wg_hi(0)

        def evac_in(j):
            for c in range(NCH):
                n = NCH * j + c
                act.wait_ge(in_mm, n + 1)
                src = bank[n % 4][:]
                cols = slice(c * CH, (c + 1) * CH)
                if j < 2 * FT and j % 2 == 0:
                    s = SEQ_OF[c]
                    after(act, conv_done, j // 2)
                    o = UPAD[s] + PADL + c * CH - OFFS[s]
                    act.activation(u_pad[:, o:o + CH], src, ACT.Copy).then_inc(in_evac, 1)
                elif j < 2 * FT:
                    act.activation(yr[:, j // 2, cols], src, ACT.Gelu_apprx_tanh).then_inc(in_evac, 1)
                else:
                    f = j - 2 * FT
                    if f == 0:
                        act.wait_ge(mod_mm, mod_count(3 * KD - 1))
                    if f == 1:
                        act.wait_ge(conv_done, FT)
                    if f > 1:
                        act.wait_ge(gate_mm, 2 * NCH * LRU_ALL)
                    act.activation(u_f[f][:, cols], src, ACT.Copy).then_inc(in_evac, 1)
                if c == 1 and 0 < j < NTILE - 1:
                    split_win_hi(j + 1)
                if gates_after(j, c):
                    g, gate = gates_after(j, c)
                    gate_sigmoids(g, gate)
                    if gate == 0 and g % 2 == 0:
                        lru_coefficients(g)
                    elif gate == 1:
                        if g % 2 == 1:
                            lru_coefficients(g)
                        if g % 2 == 0:
                            lru_sqrt(g)
                        elif g // 2 + 1 < FT:
                            split_wg_hi(g // 2 + 1)
                elif n >= 2 * NCH and gates_after(*divmod(n - 1, NCH)):
                    lru_sqrt(gates_after(*divmod(n - 1, NCH))[0])
                if (j, c) in ((4, 0), (8, 0)):
                    mod_copy(NQ + j // 4 - 1)

        def gate_sigmoids(g, gate):
            f, d = divmod(g, 2)
            dst, col = ((rr, V_BR), (ii, V_BI))[gate]
            after(act, (lru_m2, lru_scan)[gate], g)
            for c in range(NCH):
                act.wait_ge(gate_mm, (2 * g + gate) * NCH + c + 1)
                b = vec[:, col + d * FT + f:col + d * FT + f + 1]
                act.activation(dst[:, c * CH:(c + 1) * CH], bank[GB[c]][:], ACT.Sigmoid, bias=b
                               ).then_inc(gate_sig, 1)

        def lru_coefficients(g):
            f, d = divmod(g, 2)
            act.wait_ge(gate_sig, (2 * g + 1) * NCH)
            after(act, lru_scan, g)
            act.wait_ge(decay_set, 1)
            w = d * FT + f
            act.activation(aa[:], rr[:], ACT.Exp, scale=decay[:, 0, w:w + 1]).then_inc(lru_a, 1)
            act.wait_ge(lru_a, g + 1)
            act.activation(rr[:], rr[:], ACT.Tanh, scale=decay[:, 1, w:w + 1]).then_inc(lru_t, 1)
            after(act, lru_done, f)
            act.activation(qq[:], aa[:], ACT.Square).then_inc(lru_q, 1)

        def lru_sqrt(g):
            act.wait_ge(lru_m2, g + 1)
            act.activation(qq[:], qq[:], ACT.Sqrt).then_inc(lru_m, 1)

        def fold_split_hi(f):
            act.wait_ge(fold_done, f + 1)
            if f > 1:
                act.wait_ge(pq_mm, 3 * (f - 1))
            elif f == 1:
                act.wait_ge(in_mm, NCH * NTILE)
            else:
                act.wait_ge(lru_done, FT)
            act.activation(fold_hi[f % 2][:].rearrange("p t n -> p (t n)"),
                           fold[f][:].rearrange("p t n -> p (t n)"), ACT.Copy).then_inc(fold_hi_done, 1)

        for j in range(NTILE):
            evac_in(j)
            if j == NTILE - 2:
                fold_split_hi(0)
            if j == AB_AFTER:
                act.wait_ge(ab_mm, 1)
                act.activation(a_f32[:].rearrange("p f m -> p (f m)"), bank[GB[0]][:], ACT.Copy)
                act.activation(ab_hi[:, 0].rearrange("p f m -> p (f m)"), bank[GB[0]][:], ACT.Copy)
                act.activation(ab_hi[:, 1].rearrange("p f m -> p (f m)"), bank[GB[1]][:], ACT.Copy
                               ).then_inc(ab_act, 1)

        def split_wo_hi(i):
            act.wait_ge(ld_wo[i % 3], 16 * (i // 3 + 1))
            if i == 0:
                act.wait_ge(mixr_lo, FT * NCH)
                act.wait_ge(fold_done, 2)
            elif i == 4:
                act.wait_ge(pq_mm, 3 * FT)
                act.wait_ge(fold_lo_done, FT)
            elif i == 9:
                act.wait_ge(eo_mm, 2 * (FT - 1))
            elif i == 13:
                act.wait_ge(eo_mm, 2 * FT)
            act.activation(wo_hi[WO_ORDER[i]][:].rearrange("p k m -> p (k m)"), wo_raw[i % 3][:], ACT.Copy
                           ).then_inc(wo_hi_done, 1)

        def pq_split_hi(f):
            b = f % 2
            if f == 0:
                act.wait_ge(in_mm, NCH * NTILE)
            elif f == 1:
                act.wait_ge(mixr_lo, FT * NCH // 2)
            else:
                act.wait_ge(eo_mm, 2 * (f - 1))
            for i in range(3):
                act.wait_ge(pq_mm, 3 * f + i + 1)
                act.activation(pq_hi[b][:, i, :], bank[i][:], ACT.Copy,
                               scale=SEQS[0 if i < 2 else 1] ** -0.5).then_inc(pq_hi_done, 1)

        def edge_out():
            act.wait_ge(edge_mm, 1)
            src = bank[NBK][:, 0:4 * FT].rearrange("p (f e) -> p f e", e=4)
            for s in range(2):
                for sign in range(2):
                    m = act.activation(bias_e[:, :, s, sign], src[:, :, 2 * s], ACT.Copy,
                                       scale=SEQS[s] ** -0.5 * (1 - 2 * sign))
            m.then_inc(bias_done, 1)
            act.wait_ge(tab_lo_done, 8)
            for s in range(2):
                m = act.activation(yf[:, :, OFFS[s] + SEQS[s] // 2], src[:, :, 2 * s + 1], ACT.Copy,
                                   scale=SEQS[s] ** -0.5)
            m.then_inc(yf_edge, 1)

        def copy_e(f):
            act.wait_ge(bias_done, 1)
            for s in range(2):
                act.wait_ge(eo_mm, 2 * f + s + 1)
                after(act, eo_done, 3 * (f - 1) + 1 + 2 * s)
                src = bank[3][:] if s == 0 else bank[5][:, 0:256]
                h = SEQS[s] // 2
                for sign in range(2):
                    act.activation(e_sb[s][:, sign:h:2], src[:, sign::2], ACT.Identity,
                                   bias=bias_e[:, f, s, sign:sign + 1]).then_inc(e_done, 1)

        fold_split_hi(1)
        act.wait_ge(ld_tab, 16)
        act.wait_ge(in_mm, NCH * NTILE)
        def table_hi(rows):
            for i in rows:
                act.activation(tab_hi[:, i // 4, i % 4, :], tab_raw[:, i, :], ACT.Copy).then_inc(tab_hi_done, 1)

        table_hi(range(4))
        pq_split_hi(0)
        table_hi(range(4, 8))
        for f in range(FT):
            if f + 2 < FT:
                fold_split_hi(f + 2)
            if f + 1 < FT:
                pq_split_hi(f + 1)
            if f == 0:
                edge_out()
            if f == FT - 1:
                for i in range(9, 13):
                    split_wo_hi(i)
            copy_e(f)
            if f in (1, 2):
                for i in range(4 * (f - 1), 4 + 5 * (f - 1)):
                    split_wo_hi(i)

        act.wait_ge(eo_done, 3 * FT)
        for c in range(NCH):
            for f in range(FT):
                act.activation(hi_f[:, c, f, :], yf[:, f, c * CH:(c + 1) * CH], ACT.Copy).then_inc(mixf_hi, 1)
        for i in range(13, 16):
            split_wo_hi(i)

        def modulate(n):
            c = n % NN
            s = SEQ_OF[c]
            for k in range(KD):
                m = n * KD + k
                act.wait_ge(xn_done, xn_count(n) + k + 1)
                act.activation(hi(c, k), n_t[k % 2][:], ACT.Identity, bias=mod[:, SHIFT2, k, s:s + 1]
                               ).then_inc(hhi_done, 1)

        def split_w(b, which):
            dst, done = ((w1_hi, w1_hi_done), (w2_hi, w2_hi_done))[which]
            act.wait_ge(ld_w12, 16 * (2 * b + which + 1))
            if isinstance(b, int) and b == 0:
                act.wait_ge(out_mm, (NCH - 1) * KD + 4 if which == 0 else NCH * KD)
            elif which == 0:
                act.wait_ge(ff1_mm, JB * NCH * b)
            else:
                act.wait_ge(ff2_mm, NCH * KD * b)
            flat = dst[:].rearrange("p a m -> p (a m)")
            for i in range(4):
                act.activation(flat[:, i * CH:(i + 1) * CH], w12_raw[:, i * CH:(i + 1) * CH], ACT.Copy
                               ).then_inc(done, 1)

        for n in range(NN, 2 * NN):
            if n > NN:
                root(n - 1)
            square(n, 0)
            if n > NN:
                modulate(n - 1)
            for k in range(1, KD):
                if n == 2 * NN - 1 and k == 6:
                    split_w(0, 0)
                square(n, k)
        root(2 * NN - 1)

        def hidden(b, c):
            for j in range(JB):
                i = JB * c + j
                n = JB * NCH * b + i
                act.wait_ge(ff1_mm, n + 1)
                after(act, hid_lo_done, n - 1)
                act.activation(tmp[j][:], bank[i % 3][:], ACT.Relu).then_inc(ff1_relu, 1)
                act.wait_ge(ff1_relu, n + 1)
                act.activation(tmp[j][:], tmp[j][:], ACT.Square).then_inc(ff1_sq, 1)
                act.wait_ge(ff1_sq, n + 1)
                act.activation(hid_hi[:, c, j, :], tmp[j][:], ACT.Copy).then_inc(hid_hi_done, 1)

        def mlp_block(b, first=False, last=False):
            hidden(b, 0)
            if first:
                modulate(2 * NN - 1)
            split_w(b, 1)
            hidden(b, 1)
            hidden(b, 2)
            if not last:
                split_w(b + 1, 0)

        mlp_block(0, first=True)
        with act.Fori(1, NB - 1) as b:
            mlp_block(b)
        mlp_block(NB - 1, last=True)
        for n in range(2 * NN, 3 * NN):
            for k in range(KD):
                square(n, k)
            root(n)

    @block.vector
    def _(dve):
        own = [0]

        def chain(ins):
            own[0] += 1
            ins.then_inc(dve_own, 1)
            dve.wait_ge(dve_own, own[0])

        def add_square(n, k):
            i = adds_v(n) + add_order(n).index(k)
            if k == 0:
                dve.wait_ge(sq_added_p, adds_p(n + 1))
            if shared(n):
                acc, sq = squares(n)[:, pool_share(n), :], squares(n)[:, k, :]
            else:
                acc, sq = n_acc[:], n_sq[k % 2][:]
            after(dve, sq_added, i)
            if k > 0:
                dve.wait_ge(sq_done, n * KD + k + 1)
            dve.tensor_tensor(acc, acc, sq, ALU.add).then_inc(sq_added, 1)

        def rstd(n):
            dve.wait_ge(sd_done, n + 1)
            chain(dve.reciprocal(rc[:], sd[:]))
            after(dve, norm_bc, n)
            for b in range(4):
                m = dve.tensor_scalar(norm_diag(n)[:, b * P:(b + 1) * P], ident[:], rc[:, b:b + 1], None, ALU.mult)
            m.then_inc(rstd_done, 1)

        def amplitude(dst, g, scale):
            for s in range(2):
                m = dve.scalar_tensor_tensor(dst[:, :, s], mod[:, scale, :, s], 1.0, vec[:, g:g + KD], ALU.add,
                                             ALU.mult)
            m.then_inc(amp_set, 1)

        def mod_columns(r):
            dve.wait_ge(mod_tr, NQ + r)
            src = bank[NBK][:].rearrange("p (b i h s) -> p i h b s", b=4, i=2, h=2)
            bm = vec[:, V_BMOD + 2 * r * KD:V_BMOD + 2 * (r + 1) * KD].rearrange("p (i h b) -> p i h b", i=2, h=2)
            dst = mod[:, 2 * r:2 * r + 2, :, :].rearrange("p i (h b) s -> p i h b s", h=2)
            for s in range(2):
                for i in range(2):
                    m = dve.tensor_tensor(dst[:, i, :, :, s], src[:, i, :, :, s], bm[:, i], ALU.add)
            m.then_inc(mod_cols, 1)
            dve.wait_ge(mod_cols, NQ + r)

        dve.wait_ge(ld_vec, 16)
        dve.wait_ge(const_set, 4)
        dve.tensor_reduce(pick[:], ident[:].rearrange("p (g r) -> p r g", g=4)[:, 0:2, :], AX.X, ALU.add)
        lam = vec[:, V_LAM:V_LAM + 2 * FT]
        chain(dve.tensor_scalar(sp[:, 2, :], lam, -1.0, None, ALU.mult))
        chain(dve.tensor_tensor(sp[:, 0, :], lam, sp[:, 2, :], ALU.max))
        dve.sem_inc(lam_abs, 1)
        dve.wait_ge(sig_c, 1)
        for s in range(2):
            m = dve.tensor_tensor(c_silu[:, :, s], vec[:, V_C + s * KD:V_C + (s + 1) * KD],
                                  c_sig[:, s * KD:(s + 1) * KD], ALU.mult)
        m.then_inc(silu_c, 1)
        dve.wait_ge(lam_exp, 1)
        chain(dve.tensor_scalar(sp[:, 3, :], sp[:, 1, :], 2.0, None, ALU.add))
        chain(dve.reciprocal(sp[:, 4, :], sp[:, 3, :]))
        chain(dve.tensor_tensor(sp[:, 3, :], sp[:, 1, :], sp[:, 4, :], ALU.mult))
        chain(dve.tensor_tensor(sp[:, 4, :], sp[:, 3, :], sp[:, 3, :], ALU.mult))
        chain(dve.tensor_scalar(sp[:, 5, :], sp[:, 4, :], 1.0 / 19, None, ALU.mult))
        for odd in range(17, 2, -2):
            chain(dve.scalar_tensor_tensor(sp[:, 5, :], sp[:, 5, :], 1.0 / odd, sp[:, 4, :], ALU.add, ALU.mult))
        chain(dve.scalar_tensor_tensor(sp[:, 5, :], sp[:, 5, :], 1.0, sp[:, 3, :], ALU.add, ALU.mult))
        chain(dve.tensor_scalar(sp[:, 2, :], sp[:, 2, :], 0.0, None, ALU.max))
        chain(dve.scalar_tensor_tensor(sp[:, 5, :], sp[:, 5, :], 2.0, sp[:, 2, :], ALU.mult, ALU.add))
        dve.tensor_scalar(decay[:, 0, :], sp[:, 5, :], -LRU_C, None, ALU.mult)
        dve.tensor_scalar(decay[:, 1, :], sp[:, 5, :], LRU_C, None, ALU.mult).then_inc(decay_set, 1)
        def x_rstd(n):
            dve.wait_ge(norm_bc, n + 1)
            for k in range(KD):
                dve.tensor_tensor(x[:, n, k, :], x[:, n, k, :], norm_bank(n)[:], ALU.mult).then_inc(xn_done, 1)

        for n in range(NN):
            for k in add_order(n):
                add_square(n, k)
            if n < NN - 1:
                rstd(n)

        def mod_quarter_columns(q):
            dve.wait_ge(mod_tr, q + 1)
            tiles = slice(2 * q, 2 * q + 2)
            src = bank[NBK][:, 0:8].rearrange("p (i k s) -> p i k s", i=2, k=2)
            bm = vec[:, V_BMOD:V_BMOD + 2 * KD].rearrange("p (i k) -> p i k", i=2)
            for s in range(2):
                m = dve.tensor_tensor(mod[:, 0:2, tiles, s], src[:, :, :, s], bm[:, :, tiles], ALU.add)
            m.then_inc(mod_cols, 1)
            dve.wait_ge(mod_cols, q + 1)
            for s in range(2):
                m = dve.scalar_tensor_tensor(amp1[:, tiles, s], mod[:, SCALE1, tiles, s], 1.0,
                                             vec[:, V_GMIX + 2 * q:V_GMIX + 2 * q + 2], ALU.add, ALU.mult)
            m.then_inc(amp_set, 1)

        def first_split(q):
            for c in range(NCH):
                k = 2 * q
                m = (q * NCH + c) * 2
                for i in range(2):
                    dve.wait_ge(h_done, m + i + 1)
                    dve.tensor_copy(hi(c, k + i), x[:, c, k + i, :]).then_inc(hhi_done, 1)
                dve.wait_ge(hhi_done, m + 1)
                dve.tensor_tensor(lo(c, k), x[:, c, k, :], hi(c, k), ALU.subtract).then_inc(hlo_done, 1)

        x_rstd(0)
        rstd(2)
        mod_quarter_columns(0)
        x_rstd(2)
        mod_quarter_columns(1)
        mod_quarter_columns(2)
        first_split(0)
        first_split(1)
        first_split(2)
        mod_quarter_columns(3)
        first_split(3)

        def conv(f):
            dve.wait_ge(in_evac, NCH * (2 * f + 1))
            after(dve, lru_ix, 2 * f)
            after(dve, gate_mm, 4 * NCH * f)
            w = [vec[:, V_CONVW + t * FT + f:V_CONVW + t * FT + f + 1] for t in range(4)]
            b = vec[:, V_CONVB + f:V_CONVB + f + 1]
            for t in range(4):
                for s in range(2):
                    src = u_pad[:, UPAD[s] + t:UPAD[s] + t + SEQS[s]]
                    dst = uc[:, OFFS[s]:OFFS[s] + SEQS[s]]
                    if t == 0:
                        m = dve.tensor_scalar(dst, src, w[0], b, ALU.mult, ALU.add)
                    else:
                        m = dve.scalar_tensor_tensor(dst, src, w[t], dst, ALU.mult, ALU.add)
                chain(m)

        def conv_split():
            chain(dve.tensor_copy(uc_hi[:], uc[:]))
            dve.tensor_tensor(uc_lo[:], uc[:], uc_hi[:], ALU.subtract).then_inc(conv_done, 1)

        def lru_input(g):
            dve.wait_ge(gate_sig, 2 * NCH * (g + 1))
            dve.tensor_tensor(ii[:], ii[:], uc[:], ALU.mult).then_inc(lru_ix, 1)

        def lru_root(g):
            dve.wait_ge(lru_t, g + 1)
            dve.wait_ge(lru_q, g + 1)
            chain(dve.scalar_tensor_tensor(qq[:], qq[:], 1.0, rr[:], ALU.add, ALU.mult))
            dve.tensor_scalar(qq[:], qq[:], 0.0, None, ALU.max).then_inc(lru_m2, 1)

        def lru_group(g):
            f, d = divmod(g, 2)
            dve.wait_ge(lru_m, g + 1)
            dve.wait_ge(lru_ix, g + 1)
            chain(dve.tensor_tensor(ii[:], ii[:], qq[:], ALU.mult))
            dst = (hf, qq)[d]
            for s in range(2):
                o, e = OFFS[s], OFFS[s] + SEQS[s]
                cols = slice(o, e) if d == 0 else slice(e - 1, o - 1 if o else None, -1)
                m = dve.tensor_tensor_scan(dst[:, cols], aa[:, cols], ii[:, cols], 0.0, ALU.mult, ALU.add)
            m.then_inc(lru_scan, 1)
            if d == 1:
                dve.wait_ge(lru_scan, g + 1)
                chain(dve.tensor_tensor(hf[:], hf[:], qq[:], ALU.add))
                dve.wait_ge(in_evac, NCH * (2 * f + 2))
                dve.tensor_tensor(yr[:, f, :], yr[:, f, :], hf[:], ALU.mult).then_inc(lru_done, 1)
                dve.wait_ge(lru_done, f + 1)

        conv(0)
        conv_split()
        for g in range(LRU_ALL):
            if g % 2 == 0:
                lru_root(g)
            lru_input(g)
            following = g % 2 == 1 and g // 2 + 1 < FT
            if following:
                conv(g // 2 + 1)
            if g % 2 == 1:
                lru_root(g)
            if following:
                conv_split()
            if g == 3:
                mod_columns(1)
            lru_group(g)
        mod_columns(2)
        amplitude(amp2, V_GMLP, SCALE2)
        dve.wait_ge(ab_act, 1)
        for t in range(2):
            m = dve.tensor_tensor(ab_lo[:, t].rearrange("p f m -> p (f m)"), bank[GB[t]][:],
                                  ab_hi[:, t].rearrange("p f m -> p (f m)"), ALU.subtract)
        m.then_inc(ab_set, 1)

        def edges(f):
            dve.wait_ge(in_evac, NCH * (2 * FT + f + 1))
            for s in range(2):
                u = u_f[f][:, OFFS[s]:OFFS[s] + SEQS[s]]
                dve.tensor_copy(edge[:, f, 2 * s:2 * s + 1], u[:, SEQS[s] // 2:SEQS[s] // 2 + 1])
                m = dve.tensor_reduce(alt[:, s, :], u.rearrange("p (n t) -> p t n", t=2), AX.X, ALU.add)
            chain(m)
            for s in range(2):
                m = dve.tensor_tensor(edge[:, f, 2 * s + 1:2 * s + 2], alt[:, s, 0:1], alt[:, s, 1:2], ALU.subtract)
            m.then_inc(edge_done, 1)
            dve.wait_ge(edge_done, f + 1)

        def make_fold(f):
            if f == 0:
                dve.wait_ge(gate_mm, 2 * NCH * LRU_ALL)
                dve.wait_ge(ab_mm, 1)
            elif f == 2:
                dve.wait_ge(fold_lo_done, 1)
            elif f == 3:
                dve.wait_ge(fold_done, 1)
            for s in range(2):
                h, o, fo = SEQS[s] // 2, OFFS[s], HOFF[s]
                u = u_f[f]
                mirror = u[:, o + 2 * h - 1:o + h:-1]
                dve.tensor_tensor(fold[f][:, 0, fo + 1:fo + h], u[:, o + 1:o + h], mirror, ALU.add)
                dve.tensor_tensor(fold[f][:, 1, fo + 1:fo + h], u[:, o + 1:o + h], mirror, ALU.subtract)
                dve.tensor_copy(fold[f][:, 0, fo:fo + 1], u[:, o:o + 1])
                m = dve.memset(fold[f][:, 1, fo:fo + 1], 0.0)
            m.then_inc(fold_done, 1)

        def fold_split_lo(f):
            dve.wait_ge(fold_hi_done, f + 1)
            dve.tensor_tensor(fold_lo[f % 2][:].rearrange("p t n -> p (t n)"),
                              fold[f][:].rearrange("p t n -> p (t n)"),
                              fold_hi[f % 2][:].rearrange("p t n -> p (t n)"), ALU.subtract).then_inc(fold_lo_done, 1)

        def mix_split_hi(tiles):
            for f in tiles:
                for c in range(NCH):
                    dve.tensor_copy(hi_r[:, c, f, :], yr[:, f, c * CH:(c + 1) * CH]).then_inc(mixr_hi, 1)

        def pq_split_lo(f):
            b = f % 2
            for i in range(3):
                dve.wait_ge(pq_hi_done, 3 * f + i + 1)
                dve.scalar_tensor_tensor(pq_lo[b][:, i, :], bank[i][:], SEQS[0 if i < 2 else 1] ** -0.5,
                                         pq_hi[b][:, i, :], ALU.mult, ALU.subtract).then_inc(pq_lo_done, 1)

        def unfold(f):
            for s in range(2):
                h = SEQS[s] // 2
                o = OFFS[s]
                dve.wait_ge(e_done, 4 * f + 2 * s + 2)
                dve.wait_ge(eo_mm, 2 * f + s + 1)
                odd = bank[4][:] if s == 0 else bank[5][:, 256:512]
                m = dve.tensor_tensor(yf[:, f, o:o + h], e_sb[s][:, 0:h], odd[:, 0:h], ALU.subtract)
                if s == 0:
                    m = dve.tensor_tensor(yf[:, f, o + 2 * h - 1:o + h:-1], e_sb[s][:, 1:h], odd[:, 1:h], ALU.add)
                    m.then_inc(eo_done, 1)
                else:
                    m.then_inc(eo_done, 1)
                    dve.tensor_tensor(yf[:, f, o + 2 * h - 1:o + h:-1], e_sb[s][:, 1:h], odd[:, 1:h], ALU.add
                                      ).then_inc(eo_done, 1)

        edges(0)
        make_fold(0)
        edges(1)
        make_fold(1)
        fold_split_lo(0)
        edges(2)
        make_fold(2)
        dve.wait_ge(in_mm, NCH * NTILE)
        mix_split_hi(MIX_ORDER[:2])
        fold_split_lo(1)
        def table_lo(rows):
            for i in rows:
                dve.wait_ge(tab_hi_done, i + 1)
                dve.tensor_tensor(tab_lo[:, i // 4, i % 4, :], tab_raw[:, i, :], tab_hi[:, i // 4, i % 4, :],
                                  ALU.subtract).then_inc(tab_lo_done, 1)

        table_lo(range(3))
        pq_split_lo(0)
        table_lo(range(3, 8))
        mix_split_hi(MIX_ORDER[2:])
        edges(3)
        make_fold(3)
        for f in range(FT):
            if f + 2 < FT:
                fold_split_lo(f + 2)
            if f + 1 < FT:
                pq_split_lo(f + 1)
            unfold(f)
        for c in range(NCH):
            for f in range(FT):
                dve.wait_ge(mixf_hi, c * FT + f + 1)
                dve.tensor_tensor(lo_f[:, c, f, :], yf[:, f, c * CH:(c + 1) * CH], hi_f[:, c, f, :],
                                  ALU.subtract).then_inc(mixf_lo, 1)

        def norm_apply(n):
            c = n % NN
            s = SEQ_OF[c]
            dve.wait_ge(norm_bc, n + 1)
            for k in range(KD + 1):
                if k < KD:
                    if k >= 2:
                        dve.wait_ge(hlo_done, NLOAD // 2 + (n - NN) * KD + k - 1)
                    dve.scalar_tensor_tensor(n_t[k % 2][:], x[:, c, k, :], amp2[:, k, s:s + 1], norm_bank(n)[:],
                                             ALU.mult, ALU.mult).then_inc(xn_done, 1)
                if k > 0:
                    dve.wait_ge(hhi_done, n * KD + k)
                    dve.scalar_tensor_tensor(lo(c, k - 1), n_t[(k - 1) % 2][:], mod[:, SHIFT2, k - 1, s:s + 1],
                                             hi(c, k - 1), ALU.add, ALU.subtract).then_inc(hlo_done, 1)

        for c in range(NCH):
            s = SEQ_OF[c]
            dve.wait_ge(ld_x[c], 32)
            for d in range(KD):
                n = c * KD + d
                dve.wait_ge(out_mm, n + 1)
                b = d if c == 0 else (n - KD) % 6
                dve.scalar_tensor_tensor(x[:, c, d, :], bank[b][:], mod[:, GATE1, d, s:s + 1], x[:, c, d, :],
                                         ALU.mult, ALU.add).then_inc(out_evac, 1)
                if c > 0 and d == 0:
                    rstd(NN + c - 1)
                elif c > 0 and d == 1:
                    norm_apply(NN + c - 1)
                elif d > 1:
                    add_square(NN + c, d - 1)
            add_square(NN + c, KD - 1)
        rstd(2 * NN - 1)

        def hidden_lo(b, c):
            for j in range(JB):
                n = JB * NCH * b + JB * c + j
                dve.wait_ge(hid_hi_done, n + 1)
                dve.tensor_tensor(hid_lo[:, c, j, :], tmp[j][:], hid_hi[:, c, j, :], ALU.subtract
                                  ).then_inc(hid_lo_done, 1)

        def mlp_block(b, first=False, last=False):
            hidden_lo(b, 0)
            if first:
                norm_apply(2 * NN - 1)
            hidden_lo(b, 1)
            hidden_lo(b, 2)
            for c in range(NCH):
                s = SEQ_OF[c]
                for d in range(KD):
                    n = KD * c + d
                    dve.wait_ge(ff2_mm, NCH * KD * b + n + 1)
                    dve.scalar_tensor_tensor(x[:, c, d, :], bank[3 + n % 4][:], mod[:, GATE2, d, s:s + 1],
                                             x[:, c, d, :], ALU.mult, ALU.add).then_inc(ff2_evac, 1)
                    if last:
                        if c > 0 and d == 2:
                            rstd(2 * NN + c - 1)
                        if c > 0:
                            final(c - 1, FINAL_AFTER[c].get(d, ()))
                if last:
                    for k in add_order(2 * NN + c):
                        add_square(2 * NN + c, k)

        FINAL_AFTER = {1: {3: (0,), 4: (1, 2), 5: (3, 4), 6: (5, 6), 7: (7,)}, 2: {4: (0,), 5: (1, 2)}}

        def final(c, tiles):
            for k in tiles:
                dve.wait_ge(norm_bc, 2 * NN + c + 1)
                dve.scalar_tensor_tensor(x[:, c, k, :], x[:, c, k, :], vec[:, V_GFIN + k:V_GFIN + k + 1],
                                         norm_bank(2 * NN + c)[:], ALU.mult, ALU.mult).then_inc(y_done, 1)

        mlp_block(0, first=True)
        with dve.Fori(1, NB - 1) as b:
            mlp_block(b)
        mlp_block(NB - 1, last=True)
        final(NCH - 2, (3, 4, 5))
        rstd(3 * NN - 1)
        final(NCH - 2, (6, 7))
        final(NCH - 1, range(KD))

    @block.gpsimd
    def _(pool):
        pool.memset(c_silu[:], 0.0).then_inc(const_set, 1)
        pool.memset(ones[:], 1.0).then_inc(const_set, 1)
        pool.memset(eps[:], EPS).then_inc(const_set, 1)
        pool.memset(ident[:], 0.0).then_inc(pool_own, 1)
        pool.wait_ge(pool_own, 1)
        pool.affine_select(out=ident[:], in_=ident[:], compare_op=ALU.not_equal, fill=1.0, base=0,
                           pattern=[[-1, P]], channel_multiplier=1).then_inc(const_set, 1)
        for s in range(2):
            pool.memset(u_pad[:, UPAD[s]:UPAD[s] + PADL], 0.0)
            m = pool.memset(u_pad[:, UPAD[s] + PADL + SEQS[s]:UPAD[s] + PADL + SEQS[s] + PADR], 0.0)
        m.then_inc(const_set, 1)

        def split_win_lo(j):
            pool.wait_ge(win_hi_done, j + 1)
            pool.tensor_tensor(win_lo[j % 2][:].rearrange("p k m -> p (k m)"), win_raw[:],
                               win_hi[j % 2][:].rearrange("p k m -> p (k m)"), ALU.subtract
                               ).then_inc(win_lo_done, 1)

        def add_squares(n):
            for k in range(1, pool_share(n)):
                i = adds_p(n) + k - 1
                after(pool, sq_added_p, i)
                pool.wait_ge(sq_done, n * KD + k + 1)
                sq = squares(n)
                pool.tensor_tensor(sq[:, 0, :], sq[:, 0, :], sq[:, k, :], ALU.add).then_inc(sq_added_p, 1)

        for n in range(NN):
            add_squares(n)
        pool.wait_ge(rstd_copied, 1)
        for k in range(KD):
            pool.tensor_tensor(x[:, 1, k, :], x[:, 1, k, :], rstd_sb[:], ALU.mult).then_inc(xn_done_p, 1)
        split_win_lo(0)
        for q in range(NQ):
            if q == NQ - 1:
                split_win_lo(1)
            for c in range(NCH):
                k = 2 * q + 1
                pool.wait_ge(hhi_done, (q * NCH + c) * 2 + 2)
                pool.tensor_tensor(lo(c, k), x[:, c, k, :], hi(c, k), ALU.subtract).then_inc(hlo_done_p, 1)

        def split_wg_lo(f):
            pool.wait_ge(wg_hi_done, f + 1)
            pool.tensor_tensor(wg_lo[:].rearrange("p g m -> p (g m)"), wg_raw[:],
                               wg_hi[:].rearrange("p g m -> p (g m)"), ALU.subtract).then_inc(wg_lo_done, 1)

        split_wg_lo(0)
        for j in range(NTILE):
            if j + 1 < NTILE and j > 0:
                split_win_lo(j + 1)
            if j % 2 == 0 and 0 < j < 2 * FT:
                split_wg_lo(j // 2)

        for i, (f, c) in enumerate((f, c) for f in MIX_ORDER for c in range(NCH)):
            pool.wait_ge(mixr_hi, i + 1)
            pool.tensor_tensor(lo_r[:, c, f, :], yr[:, f, c * CH:(c + 1) * CH], hi_r[:, c, f, :],
                               ALU.subtract).then_inc(mixr_lo, 1)
        for i in range(16):
            pool.wait_ge(wo_hi_done, i + 1)
            pool.tensor_tensor(wo_lo[WO_ORDER[i]][:].rearrange("p k m -> p (k m)"), wo_raw[i % 3][:],
                               wo_hi[WO_ORDER[i]][:].rearrange("p k m -> p (k m)"), ALU.subtract
                               ).then_inc(wo_lo_done, 1)

        def split_w(b, which):
            dst, src, hi_done, done = ((w1_lo, w1_hi, w1_hi_done, w1_lo_done),
                                       (w2_lo, w2_hi, w2_hi_done, w2_lo_done))[which]
            dst = dst[:].rearrange("p a m -> p (a m)")
            src = src[:].rearrange("p a m -> p (a m)")
            for i in range(4):
                cols = slice(i * CH, (i + 1) * CH)
                pool.wait_ge(hi_done, 4 * b + i + 1)
                m = pool.tensor_tensor(dst[:, cols], w12_raw[:, cols], src[:, cols], ALU.subtract)
            m.then_inc(done, 1)

        split_w(0, 0)
        split_w(0, 1)
        with pool.Fori(1, NB) as b:
            split_w(b, 0)
            split_w(b, 1)
        for n in range(2 * NN, 3 * NN):
            add_squares(n)

    ctx.close()


def kernel(**inputs):
    import concourse.bacc as bacc
    from concourse.bass_utils import run_bass_kernel_spmd as run

    a = {k: np.asarray(v) for k, v in inputs.items()}

    def columns(v):
        return np.ascontiguousarray(np.asarray(v).reshape(-1, P).T)

    vec = np.concatenate([columns(v) for v in (
        a["c_prompt"], a["c_sample"], a["b_mod"], a["g_mix"], a["g_mlp"], a["g_final"], a["conv_w"],
        a["conv_b"], a["b_rgate"], a["b_igate"], a["lru_lambda"])], axis=1)

    def block_diagonal(w):
        lead = w.shape[:-3]
        out = np.zeros(lead + (w.shape[-3] // 2, P, P), w.dtype)
        out[..., :HEAD, :HEAD] = w[..., 0::2, :, :]
        out[..., HEAD:, HEAD:] = w[..., 1::2, :, :]
        return out

    xT = np.concatenate([a["x_prompt"][0].T, a["x_sample"][0].T], axis=1)
    w_in = a["w_in"][0].reshape(KD, P, NTILE, P).transpose(2, 1, 0, 3).reshape(NTILE, P, KD * P)
    w_mod1 = a["w_mod"][0][:, :2 * D].reshape(KD, P, 2, 4, D // 4).transpose(3, 1, 2, 0, 4).reshape(4, P, -1)
    gates = np.stack([block_diagonal(a["w_rgate"][0]), block_diagonal(a["w_igate"][0])], axis=1)
    w_gate = gates.transpose(2, 3, 0, 1, 4).reshape(FT, P, 4 * P)
    w_four = block_diagonal(a["w_fourier"][0]).transpose(1, 0, 2).reshape(P, FT * P)
    w_out = a["w_out"][0].reshape(KD, P, KD, P).transpose(2, 1, 0, 3).reshape(KD, P, KD * P)
    w_ff1 = a["w_ff1"][0].reshape(KD, P, NB, FB).transpose(2, 1, 0, 3).reshape(NB, P, KD * FB)
    w_ff2 = a["w_ff2"][0].reshape(NB, JB, P, D).transpose(0, 2, 1, 3).reshape(NB, P, JB * D)
    th = 2 * np.pi * (np.outer(np.arange(HEAD), np.arange(HEAD)) % HEAD) / HEAD
    dft_head = np.zeros((P, 2, P))
    for t, m in enumerate((np.cos(th), np.sin(th))):
        for h in range(2):
            dft_head[h * HEAD:(h + 1) * HEAD, t, h * HEAD:(h + 1) * HEAD] = m * HEAD ** -0.5
    ts = 2 * np.pi * (np.outer(np.arange(512), np.arange(CH)) % 1024) / 1024
    dft_seq = np.stack([np.cos(ts), np.sin(ts)]).reshape(2 * 4, P, CH).transpose(1, 0, 2)

    arrays, args = {}, {}
    nc = bacc.Bacc("TRN2", target_bir_lowering=False, num_devices=1, dynamic_dma_scratch_size=1024)
    for name, v in (("vec", vec), ("xT", xT), ("w_mod", a["w_mod"][0][:, 2 * D:]), ("w_mod1", w_mod1),
                    ("w_in", w_in), ("w_gate", w_gate),
                    ("w_four", w_four), ("w_out", w_out), ("w_ff1", w_ff1), ("w_ff2", w_ff2),
                    ("dft_head", dft_head.astype(np.float32)), ("dft_seq", dft_seq.astype(np.float32))):
        v = np.ascontiguousarray(v)
        arrays[f"in_{name}"] = v
        args[f"{name}_d"] = nc.dram_tensor(f"in_{name}", v.shape, mybir.dt.from_np(v.dtype),
                                           kind="ExternalInput").ap()
    args["yT_d"] = nc.dram_tensor("out_yT", (D, T), F32, kind="ExternalOutput").ap()
    build_encoder(nc, **args)
    r = run(nc, [arrays], core_ids=[0])
    yT = r.results[0]["out_yT"]
    return (np.ascontiguousarray(yT[:, :SEQS[0]].T)[None], np.ascontiguousarray(yT[:, SEQS[0]:].T)[None])
```
